# Optimizing a Trainium2 kernel written in Bass

```python
import math
import jax, jax.numpy as jnp
from jax import lax
import numpy as np

D_MODEL = 1024
BATCH = 1
SEQ = 256
DEPTH = 2

HEAD_DIM = 64
DIFF_HEADS = 4
DIFF_VDIM = 2 * HEAD_DIM
SB_HEADS = 8
DIFF_WIDTH = DIFF_HEADS * DIFF_VDIM
SB_WIDTH = SB_HEADS * HEAD_DIM
MIX_WIDTH = DIFF_WIDTH + SB_WIDTH
DIFF_QK = DIFF_HEADS * 2 * HEAD_DIM
SB_QK = SB_HEADS * HEAD_DIM
IN_WIDTH = 2 * DIFF_QK + DIFF_WIDTH + 2 * SB_QK + SB_WIDTH
Q_BLOCK = 128

PEER_HEADS = 8
N_KEYS = 128
N_EXPERTS = N_KEYS * N_KEYS
PEER_TOPK = 16
HALF_Q = 128
QUERY_DIM = 2 * HALF_Q
TOKEN_CHUNK = 128

DEEPNORM_ALPHA = (2.0 * DEPTH) ** 0.25
DEEPNORM_BETA = (8.0 * DEPTH) ** -0.25
LN_EPS = 1e-5
RMS_EPS = 1e-5


def layer_norm(h, g, b):
    hf = h.astype(jnp.float32)
    mu = jnp.mean(hf, axis=-1, keepdims=True)
    var = jnp.mean(jnp.square(hf - mu), axis=-1, keepdims=True)
    y = (hf - mu) * lax.rsqrt(var + LN_EPS) * g.astype(jnp.float32) + b.astype(jnp.float32)
    return y.astype(h.dtype)

def alibi_slopes():
    return jnp.asarray([2.0 ** (-8.0 * (i + 1) / DIFF_HEADS) for i in range(DIFF_HEADS)], jnp.float32)

def token_mixer(h, w_in, lq1, lk1, lq2, lk2, subln_g, w_o, layer):
    B, S, _ = h.shape
    proj = h @ w_in
    s1 = DIFF_QK
    s2 = s1 + DIFF_QK
    s3 = s2 + DIFF_WIDTH
    s4 = s3 + SB_QK
    s5 = s4 + SB_QK
    dq, dk, dv, sq, sk, sv = jnp.split(proj, [s1, s2, s3, s4, s5], axis=-1)
    dq = dq.reshape(B, S, DIFF_HEADS, 2, HEAD_DIM).transpose(0, 2, 3, 1, 4)
    dk = dk.reshape(B, S, DIFF_HEADS, 2, HEAD_DIM).transpose(0, 2, 3, 1, 4)
    dv = dv.reshape(B, S, DIFF_HEADS, DIFF_VDIM).transpose(0, 2, 1, 3)
    sq = sq.reshape(B, S, SB_HEADS, HEAD_DIM).transpose(0, 2, 1, 3)
    sk = sk.reshape(B, S, SB_HEADS, HEAD_DIM).transpose(0, 2, 1, 3)
    sv = sv.reshape(B, S, SB_HEADS, HEAD_DIM).transpose(0, 2, 1, 3)

    lambda_init = 0.8 - 0.6 * math.exp(-0.3 * layer)
    lam = (jnp.exp(jnp.sum(lq1.astype(jnp.float32) * lk1.astype(jnp.float32)))
           - jnp.exp(jnp.sum(lq2.astype(jnp.float32) * lk2.astype(jnp.float32)))
           + lambda_init)
    slopes = alibi_slopes()[None, :, None, None, None]
    scale = HEAD_DIM ** -0.5

    diff_out, sb_out = [], []
    for blk in range(S // Q_BLOCK):
        q0 = blk * Q_BLOCK
        kv_len = q0 + Q_BLOCK
        t_pos = q0 + jnp.arange(Q_BLOCK)
        s_pos = jnp.arange(kv_len)
        dist = (t_pos[:, None] - s_pos[None, :]).astype(jnp.float32)

        sc = jnp.einsum('bhmqd,bhmkd->bhmqk', dq[:, :, :, q0:kv_len], dk[:, :, :, :kv_len]).astype(jnp.float32) * scale
        sc = jnp.where(dist >= 0, sc - slopes * dist, -jnp.inf)
        p = jax.nn.softmax(sc, axis=-1)
        attn = p[:, :, 0] - lam * p[:, :, 1]
        diff_out.append(jnp.einsum('bhqk,bhkd->bhqd', attn.astype(dv.dtype), dv[:, :, :kv_len]))

        z = jnp.einsum('bgqd,bgkd->bgqk', sq[:, :, q0:kv_len], sk[:, :, :kv_len]).astype(jnp.float32) * scale
        strict = dist > 0
        log_fail = jnp.where(strict, jax.nn.log_sigmoid(-z), 0.0)
        log_later = lax.cumsum(log_fail, axis=3, reverse=True) - log_fail
        w = jnp.where(strict, jnp.exp(jax.nn.log_sigmoid(z) + log_later), 0.0)
        sb_out.append(jnp.einsum('bgqk,bgkd->bgqd', w.astype(sv.dtype), sv[:, :, :kv_len]))

    diff = jnp.concatenate(diff_out, axis=2).astype(jnp.float32)
    diff = diff * lax.rsqrt(jnp.mean(jnp.square(diff), axis=-1, keepdims=True) + RMS_EPS)
    diff = diff * subln_g.astype(jnp.float32) * (1.0 - lambda_init)
    diff = diff.astype(h.dtype).transpose(0, 2, 1, 3).reshape(B, S, DIFF_WIDTH)
    sb = jnp.concatenate(sb_out, axis=2).transpose(0, 2, 1, 3).reshape(B, S, SB_WIDTH)
    mixed = jnp.concatenate([diff, sb.astype(h.dtype)], axis=-1)
    return mixed @ w_o

def peer_ffn(h, w_query, sub_keys, expert_u, expert_v):
    B, S, D = h.shape
    T = B * S
    xt = h.reshape(T, D)
    q = (xt @ w_query).reshape(T, PEER_HEADS, 2, HALF_Q).astype(jnp.float32)
    scores = jnp.einsum('thpc,hpnc->thpn', q, sub_keys.astype(jnp.float32))
    top_s, top_i = lax.top_k(scores, PEER_TOPK)
    cand_s = top_s[:, :, 0, :, None] + top_s[:, :, 1, None, :]
    cand_i = top_i[:, :, 0, :, None] * N_KEYS + top_i[:, :, 1, None, :]
    cand_s = cand_s.reshape(T, PEER_HEADS, PEER_TOPK * PEER_TOPK)
    cand_i = cand_i.reshape(T, PEER_HEADS, PEER_TOPK * PEER_TOPK)
    best_s, best_pos = lax.top_k(cand_s, PEER_TOPK)
    idx = jnp.take_along_axis(cand_i, best_pos, axis=-1)
    gate = jax.nn.softmax(best_s, axis=-1)
    n_sel = PEER_HEADS * PEER_TOPK
    n_chunks = T // TOKEN_CHUNK

    def expert_chunk(args):
        xc, ic, gc = args
        u = expert_u[ic]
        act = jax.nn.gelu(jnp.einsum('cd,ced->ce', xc, u).astype(jnp.float32), approximate=False)
        v = expert_v[ic]
        return jnp.einsum('ce,ced->cd', (gc * act).astype(v.dtype), v)

    y = lax.map(expert_chunk, (xt.reshape(n_chunks, TOKEN_CHUNK, D),
                               idx.reshape(n_chunks, TOKEN_CHUNK, n_sel),
                               gate.reshape(n_chunks, TOKEN_CHUNK, n_sel)))
    return y.reshape(B, S, D).astype(h.dtype)

def first_inputs(seed: int = 0) -> dict:
    key = jax.random.key(seed)
    ks = jax.random.split(key, 16)
    f32 = jnp.float32
    beta = DEEPNORM_BETA
    col_scale = np.concatenate([np.ones(2 * DIFF_QK), np.full(DIFF_WIDTH, beta),
                                np.ones(2 * SB_QK), np.full(SB_WIDTH, beta)]).astype(np.float32)
    x = jax.random.normal(ks[0], (BATCH, SEQ, D_MODEL), f32)
    w_in = jax.random.normal(ks[1], (DEPTH, D_MODEL, IN_WIDTH), f32) * (D_MODEL ** -0.5) * jnp.asarray(col_scale)
    lam_q1 = 0.1 * jax.random.normal(ks[2], (DEPTH, HEAD_DIM), f32)
    lam_k1 = 0.1 * jax.random.normal(ks[3], (DEPTH, HEAD_DIM), f32)
    lam_q2 = 0.1 * jax.random.normal(ks[4], (DEPTH, HEAD_DIM), f32)
    lam_k2 = 0.1 * jax.random.normal(ks[5], (DEPTH, HEAD_DIM), f32)
    subln_g = 1.0 + 0.02 * jax.random.normal(ks[6], (DEPTH, DIFF_VDIM), f32)
    w_o = jax.random.normal(ks[7], (DEPTH, MIX_WIDTH, D_MODEL), f32) * (MIX_WIDTH ** -0.5) * beta
    ln1_g = 1.0 + 0.02 * jax.random.normal(ks[8], (DEPTH, D_MODEL), f32)
    ln1_b = 0.02 * jax.random.normal(ks[9], (DEPTH, D_MODEL), f32)
    w_query = jax.random.normal(ks[10], (DEPTH, D_MODEL, PEER_HEADS * QUERY_DIM), f32) * (D_MODEL ** -0.5)
    sub_keys = jax.random.normal(ks[11], (DEPTH, PEER_HEADS, 2, N_KEYS, HALF_Q), f32) * (HALF_Q ** -0.5)
    expert_u = jax.random.normal(ks[12], (DEPTH, N_EXPERTS, D_MODEL), f32) * (D_MODEL ** -0.5) * beta
    expert_v = jax.random.normal(ks[13], (DEPTH, N_EXPERTS, D_MODEL), f32) * beta
    ln2_g = 1.0 + 0.02 * jax.random.normal(ks[14], (DEPTH, D_MODEL), f32)
    ln2_b = 0.02 * jax.random.normal(ks[15], (DEPTH, D_MODEL), f32)
    return {"x": x, "w_in": w_in, "lam_q1": lam_q1, "lam_k1": lam_k1, "lam_q2": lam_q2,
            "lam_k2": lam_k2, "subln_g": subln_g, "w_o": w_o, "ln1_g": ln1_g, "ln1_b": ln1_b,
            "w_query": w_query, "sub_keys": sub_keys, "expert_u": expert_u, "expert_v": expert_v,
            "ln2_g": ln2_g, "ln2_b": ln2_b}

def first_block(x, w_in, lam_q1, lam_k1, lam_q2, lam_k2, subln_g, w_o, ln1_g, ln1_b,
              w_query, sub_keys, expert_u, expert_v, ln2_g, ln2_b):
    h = x
    for l in range(DEPTH):
        mix = token_mixer(h, w_in[l], lam_q1[l], lam_k1[l], lam_q2[l], lam_k2[l], subln_g[l], w_o[l], l)
        h = layer_norm(DEEPNORM_ALPHA * h + mix, ln1_g[l], ln1_b[l])
        ffn = peer_ffn(h, w_query[l], sub_keys[l], expert_u[l], expert_v[l])
        h = layer_norm(DEEPNORM_ALPHA * h + ffn, ln2_g[l], ln2_b[l])
    return h


DH = 64
QBLK = 128
NSA_HEADS = 8
NSA_GROUPS = 2
NSA_R = NSA_HEADS // NSA_GROUPS
L_CMP = 32
D_CMP = 16
CMP_HIDDEN = 128
L_SLC = 64
N_SEL = 8
WINDOW = 512
MLA_HEADS = 4
MLA_NOPE = 64
MLA_ROPE = 32
MLA_V = 64
MLA_Q_LORA = 384
MLA_KV_LORA = 128
ROPE_THETA = 10000.0
FOX_HEADS = 4
XA_HEADS = 4
MEM_LEN = 256
D_FF = 4 * D_MODEL
T5_BUCKETS = 32
T5_MAX_DIST = 128
NSA_W = NSA_HEADS * DH
NSA_KV = NSA_GROUPS * DH
MLA_W = MLA_HEADS * MLA_V
FOX_W = FOX_HEADS * DH
XA_W = XA_HEADS * DH
IN_SIZES = (NSA_W, NSA_KV, NSA_KV, NSA_KV, NSA_KV, NSA_KV, NSA_KV, 3 * NSA_HEADS,
            MLA_Q_LORA, MLA_KV_LORA, MLA_ROPE,
            FOX_W, FOX_W, FOX_W, FOX_HEADS)
N_IN = sum(IN_SIZES)
DN_ALPHA = (2 * DEPTH) ** 0.25
DN_BETA = (8 * DEPTH) ** -0.25
RMS_EPS_2 = 1e-6
NEG = -1e30
FORCE = 1e4


def layer_norm_2(x, g, b):
    x32 = x.astype(jnp.float32)
    mu = jnp.mean(x32, axis=-1, keepdims=True)
    var = jnp.mean(jnp.square(x32 - mu), axis=-1, keepdims=True)
    return ((x32 - mu) * lax.rsqrt(var + LN_EPS) * g + b).astype(x.dtype)

def rms_norm(x, g):
    x32 = x.astype(jnp.float32)
    return (x32 * lax.rsqrt(jnp.mean(jnp.square(x32), axis=-1, keepdims=True) + RMS_EPS_2) * g).astype(x.dtype)

def rope(x, pos):
    half = x.shape[-1] // 2
    inv = ROPE_THETA ** (-jnp.arange(half, dtype=jnp.float32) / half)
    ang = pos.astype(jnp.float32)[:, None] * inv[None, :]
    cos = jnp.cos(ang)[None, :, None, :].astype(x.dtype)
    sin = jnp.sin(ang)[None, :, None, :].astype(x.dtype)
    x1, x2 = x[..., :half], x[..., half:]
    return jnp.concatenate([x1 * cos - x2 * sin, x1 * sin + x2 * cos], axis=-1)

def t5_bucket(dist):
    n = jnp.maximum(dist, 0)
    max_exact = T5_BUCKETS // 2
    nf = jnp.maximum(n, 1).astype(jnp.float32)
    large = max_exact + (jnp.log(nf / max_exact) / math.log(T5_MAX_DIST / max_exact)
                         * (T5_BUCKETS - max_exact)).astype(jnp.int32)
    large = jnp.minimum(large, T5_BUCKETS - 1)
    return jnp.where(n < max_exact, n, large)

def causal_block_attention(q, k, v, cum_log_f=None):
    B, S, H, dk = q.shape
    dv = v.shape[-1]
    nqb = S // QBLK
    scale = dk ** -0.5
    qb = q.reshape(B, nqb, QBLK, H, dk).transpose(1, 0, 2, 3, 4)
    key_pos = jnp.arange(S)
    decay_k = None if cum_log_f is None else cum_log_f.transpose(0, 2, 1)

    def one_block(args):
        i, q_i = args
        q_pos = i * QBLK + jnp.arange(QBLK)
        s = jnp.einsum('bqhd,bkhd->bhqk', q_i, k).astype(jnp.float32) * scale
        if decay_k is not None:
            decay_q = lax.dynamic_slice_in_dim(decay_k, i * QBLK, QBLK, axis=2)
            s = s + decay_q[..., None] - decay_k[:, :, None, :]
        s = jnp.where(key_pos[None, :] <= q_pos[:, None], s, NEG)
        p = jax.nn.softmax(s, axis=-1).astype(v.dtype)
        return jnp.einsum('bhqk,bkhd->bqhd', p, v)

    out = lax.map(one_block, (jnp.arange(nqb), qb))
    return out.transpose(1, 0, 2, 3, 4).reshape(B, S, H * dv)

def nsa_attention(q, k_cmp, v_cmp, k_slc, v_slc, k_win, v_win, gate_logits,
                  cmp_pe, cmp_w1, cmp_w2, t5_table):
    B, S, _ = q.shape
    G, R = NSA_GROUPS, NSA_R
    nqb = S // QBLK
    n_cmp = (S - L_CMP) // D_CMP + 1
    n_slc = S // L_SLC
    n_sel = min(N_SEL, n_slc)
    scale = DH ** -0.5
    k_cmp, v_cmp, k_slc, v_slc, k_win, v_win = [a.reshape(B, S, G, DH) for a in
                                                  (k_cmp, v_cmp, k_slc, v_slc, k_win, v_win)]

    tok_idx = jnp.arange(n_cmp)[:, None] * D_CMP + jnp.arange(L_CMP)[None, :]

    def compress(kv, pe, w1, w2):
        blocks = kv[:, tok_idx] + pe[None, None, :, None, :]
        flat = blocks.transpose(0, 1, 3, 2, 4).reshape(B, n_cmp, G, L_CMP * DH)
        return jax.nn.gelu(flat @ w1) @ w2

    kc = compress(k_cmp, cmp_pe[0], cmp_w1[0], cmp_w2[0])
    vc = compress(v_cmp, cmp_pe[1], cmp_w1[1], cmp_w2[1])
    cmp_end = jnp.arange(n_cmp) * D_CMP + (L_CMP - 1)

    c_lo = jnp.arange(n_cmp)[:, None] * D_CMP
    s_lo = jnp.arange(n_slc)[None, :] * L_SLC
    overlap = (jnp.maximum(jnp.minimum(c_lo + L_CMP, s_lo + L_SLC) - jnp.maximum(c_lo, s_lo), 0)
               .astype(jnp.float32) / D_CMP)

    ks_blk = k_slc.reshape(B, n_slc, L_SLC, G, DH).transpose(0, 3, 1, 2, 4)
    vs_blk = v_slc.reshape(B, n_slc, L_SLC, G, DH).transpose(0, 3, 1, 2, 4)
    kw_pad = jnp.pad(k_win, ((0, 0), (WINDOW, 0), (0, 0), (0, 0)))
    vw_pad = jnp.pad(v_win, ((0, 0), (WINDOW, 0), (0, 0), (0, 0)))

    qb = q.reshape(B, nqb, QBLK, G, R, DH).transpose(1, 0, 3, 4, 2, 5)
    gb = jax.nn.sigmoid(gate_logits).reshape(B, nqb, QBLK, G, R, 3).transpose(1, 0, 3, 4, 2, 5)
    bias_tab = t5_table.reshape(T5_BUCKETS, G, R).transpose(1, 2, 0)
    b_idx = jnp.arange(B)[:, None, None, None]
    g_idx = jnp.arange(G)[None, :, None, None]
    g5 = jnp.arange(G)[None, :, None, None, None]
    r5 = jnp.arange(R)[None, None, :, None, None]
    blk_ids = jnp.arange(n_slc)

    def one_block(args):
        i, q_i, g_i = args
        t = i * QBLK + jnp.arange(QBLK)
        dist_c = t[:, None] - cmp_end[None, :]
        valid_c = dist_c >= 0
        s_c = (jnp.einsum('bgrqd,bcgd->bgrqc', q_i, kc).astype(jnp.float32) * scale
               + bias_tab[:, :, t5_bucket(dist_c)])
        p_c = jax.nn.softmax(jnp.where(valid_c, s_c, NEG), axis=-1) * valid_c
        o_c = jnp.einsum('bgrqc,bcgd->bgrqd', p_c.astype(vc.dtype), vc)
        imp = jnp.einsum('bgrqc,cn->bgqn', p_c, overlap)
        cur = t // L_SLC
        forced = ((blk_ids[None, :] == 0) | (blk_ids[None, :] == cur[:, None])
                  | (blk_ids[None, :] == cur[:, None] - 1))
        causal_blk = blk_ids[None, :] * L_SLC <= t[:, None]
        imp = jnp.where(causal_blk, imp + FORCE * forced, NEG)
        _, sel = lax.top_k(imp, n_sel)
        k_sel = ks_blk[b_idx, g_idx, sel].reshape(B, G, QBLK, n_sel * L_SLC, DH)
        v_sel = vs_blk[b_idx, g_idx, sel].reshape(B, G, QBLK, n_sel * L_SLC, DH)
        pos_sel = (sel[..., None] * L_SLC + jnp.arange(L_SLC)).reshape(B, G, QBLK, n_sel * L_SLC)
        dist_s = t[:, None] - pos_sel
        s_s = (jnp.einsum('bgrqd,bgqkd->bgrqk', q_i, k_sel).astype(jnp.float32) * scale
               + bias_tab[g5, r5, t5_bucket(dist_s)[:, :, None]])
        p_s = jax.nn.softmax(jnp.where((dist_s >= 0)[:, :, None], s_s, NEG), axis=-1)
        o_s = jnp.einsum('bgrqk,bgqkd->bgrqd', p_s.astype(v_sel.dtype), v_sel)
        pos_w = i * QBLK - WINDOW + jnp.arange(WINDOW + QBLK)
        dist_w = t[:, None] - pos_w[None, :]
        valid_w = (dist_w >= 0) & (dist_w < WINDOW) & (pos_w[None, :] >= 0)
        k_w = lax.dynamic_slice_in_dim(kw_pad, i * QBLK, WINDOW + QBLK, axis=1)
        v_w = lax.dynamic_slice_in_dim(vw_pad, i * QBLK, WINDOW + QBLK, axis=1)
        s_w = (jnp.einsum('bgrqd,bkgd->bgrqk', q_i, k_w).astype(jnp.float32) * scale
               + bias_tab[:, :, t5_bucket(dist_w)])
        p_w = jax.nn.softmax(jnp.where(valid_w, s_w, NEG), axis=-1)
        o_w = jnp.einsum('bgrqk,bkgd->bgrqd', p_w.astype(v_w.dtype), v_w)
        return g_i[..., 0:1] * o_c + g_i[..., 1:2] * o_s + g_i[..., 2:3] * o_w

    out = lax.map(one_block, (jnp.arange(nqb), qb, gb))
    return out.transpose(1, 0, 4, 2, 3, 5).reshape(B, S, NSA_W)

def mla_attention(c_q, c_kv, k_rope, q_norm, w_uq, kv_norm, w_ukv):
    B, S, _ = c_q.shape
    pos = jnp.arange(S)
    q = (rms_norm(c_q, q_norm) @ w_uq).reshape(B, S, MLA_HEADS, MLA_NOPE + MLA_ROPE)
    q = jnp.concatenate([q[..., :MLA_NOPE], rope(q[..., MLA_NOPE:], pos)], axis=-1)
    kv = (rms_norm(c_kv, kv_norm) @ w_ukv).reshape(B, S, MLA_HEADS, MLA_NOPE + MLA_V)
    k_r = jnp.broadcast_to(rope(k_rope[:, :, None, :], pos), (B, S, MLA_HEADS, MLA_ROPE))
    k = jnp.concatenate([kv[..., :MLA_NOPE], k_r], axis=-1)
    return causal_block_attention(q, k, kv[..., MLA_NOPE:])

def fox_attention(q, k, v, f_logit, b_f):
    B, S, _ = q.shape
    shp = (B, S, FOX_HEADS, DH)
    cum = jnp.cumsum(jax.nn.log_sigmoid((f_logit + b_f).astype(jnp.float32)), axis=1)
    return causal_block_attention(q.reshape(shp), k.reshape(shp), v.reshape(shp), cum_log_f=cum)

def hybrid_mixer(h, w_in, cmp_pe, cmp_w1, cmp_w2, t5_table, q_norm, w_uq, kv_norm, w_ukv,
                 b_f, w_gate, w_br_nsa, w_br_mla, w_br_fox, w_out):
    B, S, _ = h.shape
    split_points = np.cumsum(IN_SIZES)[:-1].tolist()
    (nq, nkc, nvc, nks, nvs, nkw, nvw, ngate,
     cq, ckv, kr, fq, fk, fv, ff) = jnp.split(h @ w_in, split_points, axis=-1)
    o_nsa = nsa_attention(nq, nkc, nvc, nks, nvs, nkw, nvw, ngate, cmp_pe, cmp_w1, cmp_w2, t5_table)
    o_mla = mla_attention(cq, ckv, kr, q_norm, w_uq, kv_norm, w_ukv)
    o_fox = fox_attention(fq, fk, fv, ff, b_f)
    gates = jax.nn.sigmoid(h @ w_gate).reshape(B, S, 3, D_MODEL)
    merged = (gates[:, :, 0] * (o_nsa @ w_br_nsa) + gates[:, :, 1] * (o_mla @ w_br_mla)
              + gates[:, :, 2] * (o_fox @ w_br_fox))
    return merged @ w_out

def memory_cross_attention(x, mem, w_q, w_kv, w_o):
    B, S, _ = x.shape
    M = mem.shape[1]
    q = (x @ w_q).reshape(B, S, XA_HEADS, DH)
    kv = (mem @ w_kv).reshape(B, M, 2, XA_HEADS, DH)
    k, v = kv[:, :, 0], kv[:, :, 1]
    s = jnp.einsum('bqhd,bmhd->bhqm', q, k).astype(jnp.float32) * (DH ** -0.5)
    p = jax.nn.softmax(s, axis=-1).astype(v.dtype)
    o = jnp.einsum('bhqm,bmhd->bqhd', p, v).reshape(B, S, XA_W)
    return o @ w_o

def second_inputs(seed: int = 0) -> dict:
    key = jax.random.key(seed)
    ks = jax.random.split(key, 32)
    L = DEPTH

    def dense(k, shape, fan_in, scale=1.0):
        return jax.random.normal(k, shape, jnp.float32) * (scale * fan_in ** -0.5)

    def normal(k, shape, scale=1.0):
        return jax.random.normal(k, shape, jnp.float32) * scale

    return {
        'x': normal(ks[0], (BATCH, SEQ, D_MODEL)),
        'mem': normal(ks[1], (BATCH, MEM_LEN, D_MODEL)),
        'w_in': dense(ks[2], (L, D_MODEL, N_IN), D_MODEL),
        'cmp_pe': normal(ks[3], (L, 2, L_CMP, DH), 0.1),
        'cmp_w1': dense(ks[4], (L, 2, L_CMP * DH, CMP_HIDDEN), L_CMP * DH),
        'cmp_w2': dense(ks[5], (L, 2, CMP_HIDDEN, DH), CMP_HIDDEN),
        't5_table': normal(ks[6], (T5_BUCKETS, NSA_HEADS), 0.5),
        'mla_q_norm': 1.0 + normal(ks[7], (L, MLA_Q_LORA), 0.02),
        'mla_w_uq': dense(ks[8], (L, MLA_Q_LORA, MLA_HEADS * (MLA_NOPE + MLA_ROPE)), MLA_Q_LORA),
        'mla_kv_norm': 1.0 + normal(ks[9], (L, MLA_KV_LORA), 0.02),
        'mla_w_ukv': dense(ks[10], (L, MLA_KV_LORA, MLA_HEADS * (MLA_NOPE + MLA_V)), MLA_KV_LORA),
        'fox_b_f': jax.random.uniform(ks[11], (L, FOX_HEADS), jnp.float32, 1.0, 6.0),
        'w_gate': dense(ks[12], (L, D_MODEL, 3 * D_MODEL), D_MODEL),
        'w_br_nsa': dense(ks[13], (L, NSA_W, D_MODEL), NSA_W),
        'w_br_mla': dense(ks[14], (L, MLA_W, D_MODEL), MLA_W),
        'w_br_fox': dense(ks[15], (L, FOX_W, D_MODEL), FOX_W),
        'w_mix_out': dense(ks[16], (L, D_MODEL, D_MODEL), D_MODEL, DN_BETA),
        'xa_w_q': dense(ks[17], (L, D_MODEL, XA_W), D_MODEL),
        'xa_w_kv': dense(ks[18], (L, D_MODEL, 2 * XA_W), D_MODEL),
        'xa_w_o': dense(ks[19], (L, XA_W, D_MODEL), XA_W, DN_BETA),
        'mlp_w_up': dense(ks[20], (L, D_MODEL, D_FF), D_MODEL),
        'mlp_w_down': dense(ks[21], (L, D_FF, D_MODEL), D_FF, DN_BETA),
        'ln_g': 1.0 + normal(ks[22], (L, 3, D_MODEL), 0.02),
        'ln_b': normal(ks[23], (L, 3, D_MODEL), 0.02),
    }

def second_block(x, mem, w_in, cmp_pe, cmp_w1, cmp_w2, t5_table, mla_q_norm, mla_w_uq, mla_kv_norm,
              mla_w_ukv, fox_b_f, w_gate, w_br_nsa, w_br_mla, w_br_fox, w_mix_out, xa_w_q, xa_w_kv,
              xa_w_o, mlp_w_up, mlp_w_down, ln_g, ln_b):
    for l in range(DEPTH):
        y = hybrid_mixer(x, w_in[l], cmp_pe[l], cmp_w1[l], cmp_w2[l], t5_table, mla_q_norm[l],
                         mla_w_uq[l], mla_kv_norm[l], mla_w_ukv[l], fox_b_f[l], w_gate[l],
                         w_br_nsa[l], w_br_mla[l], w_br_fox[l], w_mix_out[l])
        x = layer_norm_2(DN_ALPHA * x + y, ln_g[l, 0], ln_b[l, 0])
        y = memory_cross_attention(x, mem, xa_w_q[l], xa_w_kv[l], xa_w_o[l])
        x = layer_norm_2(DN_ALPHA * x + y, ln_g[l, 1], ln_b[l, 1])
        y = jnp.square(jax.nn.relu(x @ mlp_w_up[l])) @ mlp_w_down[l]
        x = layer_norm_2(DN_ALPHA * x + y, ln_g[l, 2], ln_b[l, 2])
    return x


def setup_inputs(seed=0):
    out = dict(first_inputs(seed))
    for name, value in second_inputs(seed + 1).items():
        if name != "x":
            out[name + "_2"] = value
    return out


def reference(
    x, w_in, lam_q1, lam_k1, lam_q2, lam_k2, subln_g, w_o, ln1_g, ln1_b, w_query, sub_keys,
    expert_u, expert_v, ln2_g, ln2_b, mem_2, w_in_2, cmp_pe_2, cmp_w1_2, cmp_w2_2, t5_table_2,
    mla_q_norm_2, mla_w_uq_2, mla_kv_norm_2, mla_w_ukv_2, fox_b_f_2, w_gate_2, w_br_nsa_2,
    w_br_mla_2, w_br_fox_2, w_mix_out_2, xa_w_q_2, xa_w_kv_2, xa_w_o_2, mlp_w_up_2,
    mlp_w_down_2, ln_g_2, ln_b_2,
):
    x = first_block(
        x, w_in, lam_q1, lam_k1, lam_q2, lam_k2, subln_g, w_o, ln1_g, ln1_b, w_query, sub_keys,
        expert_u, expert_v, ln2_g, ln2_b,
    )
    return second_block(
        x, mem_2, w_in_2, cmp_pe_2, cmp_w1_2, cmp_w2_2, t5_table_2, mla_q_norm_2, mla_w_uq_2,
        mla_kv_norm_2, mla_w_ukv_2, fox_b_f_2, w_gate_2, w_br_nsa_2, w_br_mla_2, w_br_fox_2,
        w_mix_out_2, xa_w_q_2, xa_w_kv_2, xa_w_o_2, mlp_w_up_2, mlp_w_down_2, ln_g_2, ln_b_2,
    )


_drawn_inputs = setup_inputs


def setup_inputs(seed=0):
    import zlib

    import numpy as np

    out = dict(_drawn_inputs(seed))
    spreads = {}
    factors = {'lam_q2': 3.022,
     'subln_g': 4.596,
     'cmp_pe_2': 7.113,
     'mla_q_norm_2': 8.0,
     'mla_kv_norm_2': 8.0}
    for name, (base, spread) in spreads.items():
        noise = np.random.default_rng([zlib.crc32(name.encode()), seed]).standard_normal(out[name].shape)
        drawn = base * np.exp(spread * noise) if base else spread * noise
        out[name] = __import__('jax').numpy.asarray(drawn.astype(out[name].dtype))
    for name, factor in factors.items():
        out[name] = (out[name] * factor).astype(out[name].dtype)
    return out
```

```python
import math
from contextlib import ExitStack

import numpy as np
import concourse.bass as bass
from concourse import mybir

F32 = mybir.dt.float32
U32 = mybir.dt.uint32
ALU = mybir.AluOpType
ACT = mybir.ActivationFunctionType
AX = mybir.AxisListType

P = 128
SEQ, D = 256, 1024
TT = SEQ // P
KC = D // P
LAYERS = 2
SLOTS = 4
TILE = 2048
NEG = -1e30
ALPHA = (2.0 * LAYERS) ** 0.25
HD = 64

A_SMALL = 0
A_PROJ = 1
A_WO = A_PROJ + 12
A_LN1 = A_WO + 4
A_WQ = A_LN1 + 1
A_KEYS = A_WQ + 8
A_EXP = A_KEYS + 1
N_EXPERTS = 16384
PAIRS = N_EXPERTS // 256
A_LN2 = A_EXP + 2 * PAIRS
A_TILES = A_LN2 + 1
A_TILES += -A_TILES % SLOTS

B_SMALL = 0
B_PROJ = 1
B_CMP = B_PROJ + 12
B_GATE = B_CMP + 2
B_MIX = B_GATE + 16
B_LN1 = B_MIX + 4
B_XQ = B_LN1 + 1
B_MEM = B_XQ + 1
B_XK = B_MEM + 1
B_XV = B_XK + 1
B_XO = B_XV + 1
B_LN2 = B_XO + 1
B_MLP = B_LN2 + 1
MLP_PAIRS = 16
B_LN3 = B_MLP + 2 * MLP_PAIRS
B_TILES = B_LN3 + 1
B_TILES += -B_TILES % SLOTS
ALL_TILES = LAYERS * (A_TILES + B_TILES)

CONST = {}
_at = 0
for _name, _n in [("ident", P), ("flip", P), ("tri", P), ("ones", P), ("iota", P), ("alibi", 4 * 256), ("causal", 256),
                  ("strict", 384), ("negstrict", 384), ("cum", 256), ("rope", 64), ("cmpok", 30), ("bucket", 384),
                  ("eps", 3)]:
    CONST[_name] = slice(_at, _at + _n)
    _at += _n
CONST_COLS = _at
N_CMP = 15

A_LAM, A_SUBG, A_LINI, A_LOUT = 0, 256, 257, 258
B_UQ, B_UKV, B_W2, B_PE, B_QN, B_KVN, B_BF = 0, 1152, 1664, 1792, 1856, 1859, 1860

UNITS_A = 8
NSA_U, MLA_U, FOX_U, XA_U = 16, 4, 4, 4
UNITS_B = NSA_U + MLA_U + FOX_U + XA_U


def rings(base, turn):
    return 16 * (base + turn + 1)


class Steps:

    def __init__(self, eng, sem, start, per_layer, layer):
        self.eng, self.sem, self.n = eng, sem, 0
        self.start, self.per_layer, self.layer = start, per_layer, layer

    def after(self, ins):
        self.n += 1
        ins.then_inc(self.sem, 1)
        self.eng.wait_ge(self.sem, self.layer * self.per_layer + (self.start + self.n))

    def close(self):
        assert self.n == self.per_layer, f"{self.n} steps"


DVE_A, DVE_B = 84, 115


def program(nc, stream, x_in, consts, table, scratch, out):
    ctx = ExitStack()
    with ctx:
        def sb(name, shape, dt=F32):
            return ctx.enter_context(nc.sbuf_tensor(name, shape, dt))

        def sem(name):
            return ctx.enter_context(nc.semaphore(name))

        ring = sb("ring", [P, SLOTS, TILE])
        x = sb("x", [P, TT, D])
        xT = sb("xT", [P, KC, SEQ])
        cs = sb("cs", [P, CONST_COLS])
        tab = sb("tab", [32, 8])
        arena = sb("arena", [P, SEQ * P])
        selT = sb("selT", [P, 3, SEQ])
        work = sb("work", [P, 4, 512])
        mv = sb("mv", [P, TT, 2])
        st = sb("st", [P, TT, 2, 6])
        std = sb("std", [P, TT])
        rstd = sb("rstd", [P, TT])
        spare = sb("spare", [P, 1])
        ps = [ctx.enter_context(nc.psum_tensor(f"ps{i}", [P, 512], F32)) for i in range(8)]

        ident, tri, ones, iota = (cs[:, CONST[n]] for n in ("ident", "tri", "ones", "iota"))
        gates = arena[:, :].rearrange("p (t i) -> p t i", i=P)

        at = [0]

        def room(n, start=None):
            if start is not None:
                at[0] = start
            at[0] += n
            assert at[0] <= SEQ * P
            return arena[:, at[0] - n:at[0]]

        def slot(k):
            return ring[:, k % SLOTS, :]

        def chunks(k):
            return slot(k).rearrange("p (c n) -> p c n", c=KC)

        slot_full = [sem(f"slot_full{s}") for s in range(SLOTS)]
        tile_done = sem("tile_done")
        small_read = sem("small_read")
        loaded = sem("loaded")
        ln_var, ln_std, ln_x = sem("ln_var"), sem("ln_std"), sem("ln_x")
        xt_mm, xt_ready = sem("xt_mm"), sem("xt_ready")
        dve_step = sem("dve_step")
        stored = sem("stored")

        PA, PB = A_TILES // SLOTS, B_TILES // SLOTS

        def arrived(eng, block, l, k, i=0):
            base = l * PA if block == 1 else l * PB + LAYERS * PA
            eng.wait_ge(slot_full[k % SLOTS], (base + i + (k // SLOTS + 1)) * 16)

        def finished(eng, block, l, k, i=0):
            base = l * A_TILES if block == 1 else l * B_TILES + LAYERS * A_TILES
            eng.wait_ge(tile_done, base + 4 * i + (k + 1))

        def up_features(w, src, bank):
            for fb in range(2):
                for c in range(KC):
                    last = nc.tensor.matmul(ps[bank][:, fb * SEQ:(fb + 1) * SEQ], w[:, c, fb * P:(fb + 1) * P],
                                            src[:, c, :], start=(c == 0), stop=(c == KC - 1))
            return last

        def up_tokens(w, src, bank, n=256):
            for tt in range(TT):
                for c in range(KC):
                    last = nc.tensor.matmul(ps[bank][:, tt * 256:tt * 256 + n], src[:, c, tt * P:(tt + 1) * P],
                                            w[:, c, 0:n], start=(c == 0), stop=(c == KC - 1))
            return last

        def down(w, lhs, first, last_tile):
            for j in range(2):
                for tt in range(TT):
                    for half in range(2):
                        last = nc.tensor.matmul(ps[2 * tt + half][:, :], lhs(j, tt),
                                                w[:, j * D + half * 512:j * D + half * 512 + 512],
                                                start=(first and j == 0), stop=(last_tile and j == 1))
            return last

        def pe_turn_x(pe, n=None, tiles=1):
            for tt in range(TT):
                if n is not None:
                    pe.wait_ge(ln_x, n * TT + (tt + 1))
                if n is not None and tt == TT - 1:
                    pe.sem_inc(tile_done, tiles)
                for g in range(2):
                    for j in range(4):
                        c = 4 * g + j
                        last = nc.tensor.transpose(ps[4 + 2 * tt + g][:, j * P:(j + 1) * P],
                                                   x[:, tt, c * P:(c + 1) * P], ident)
                    last.then_inc(xt_mm, 1)

        def act_turn_x(act, m):
            for tt in range(TT):
                for g in range(2):
                    act.wait_ge(xt_mm, m * 4 + (2 * tt + g + 1))
                    nc.scalar.activation(xT[:, 4 * g:4 * g + 4, tt * P:(tt + 1) * P],
                                         ps[4 + 2 * tt + g][:, :].rearrange("p (j n) -> p j n", j=4),
                                         ACT.Copy).then_inc(xt_ready, 1)

        def act_norm(act, n):
            act.wait_ge(ln_var, n + 1)
            nc.scalar.activation(std[:, :], mv[:, :, 1], ACT.Sqrt,
                                 bias=cs[:, CONST["eps"]][:, 0:1]).then_inc(ln_std, 1)
            act_turn_x(act, n + 1)

        def carry_wait():
            nc.vector.memset(spare[:, :], 0.0)

        def dve_norm(dve, step, n, block, l, k):
            finished(dve, block, l, k - 1)
            for tt in range(TT):
                for half in range(2):
                    h = x[:, tt, half * 512:(half + 1) * 512]
                    last = nc.vector.scalar_tensor_tensor(h, h, ALPHA, ps[2 * tt + half][:, :], ALU.mult, ALU.add)
            step.after(last)
            for tt in range(TT):
                for half in range(2):
                    last = nc.vector.bn_stats(st[:, tt, half, :], x[:, tt, half * 512:(half + 1) * 512])
            step.after(last)
            carry_wait()
            for tt in range(TT):
                last = nc.vector.bn_aggr(mv[:, tt, :], st[:, tt, :, :])
            last.then_inc(ln_var, 1)
            dve.wait_ge(ln_std, n + 1)
            step.after(nc.vector.reciprocal(rstd[:, :], std[:, :]))
            for tt in range(TT):
                last = nc.vector.tensor_scalar(x[:, tt, :], x[:, tt, :], mv[:, tt, 0:1], rstd[:, tt:tt + 1],
                                               ALU.subtract, ALU.mult)
            step.after(last)
            arrived(dve, block, l, k)
            for tt in range(TT):
                last = nc.vector.tensor_tensor(x[:, tt, :], x[:, tt, :], slot(k)[:, 0:D], ALU.mult)
            step.after(last)
            for tt in range(TT):
                last = nc.vector.tensor_tensor(x[:, tt, :], x[:, tt, :], slot(k)[:, D:2 * D], ALU.add)
                last.then_inc(ln_x, 1)

        sc_first = sem("sc_first")
        sc_mm, sm_max, sm_exp, sm_p = sem("sc_mm"), sem("sm_max"), sem("sm_exp"), sem("sm_p")
        pt_mm, pt_ev, pv_mm = sem("pt_mm"), sem("pt_ev"), sem("pv_mm")

        def pe_units(pe, base, units, scores, values):
            def score(u):
                if u >= 2:
                    pe.wait_ge(sm_max, base + (u - 1))
                for m in range(2):
                    klen = units[u]["keys"]
                    last = scores(units[u], m, ps[4 + u % 2][:, m * 256:m * 256 + klen])
                    if m == 0:
                        last.then_inc(sc_first, 1)
                        pe.wait_ge(sc_first, base + (u + 1))
                last.then_inc(sc_mm, 1)

            def turn(u):
                pe.wait_ge(sm_p, base + (u + 1))
                if u >= 2:
                    pe.wait_ge(pt_ev, base + (u - 1))
                for m in range(units[u]["turned"]):
                    for kt in range(units[u]["keys"] // P):
                        last = nc.tensor.transpose(ps[6 + u % 2][:, (2 * m + kt) * P:(2 * m + kt + 1) * P],
                                                   E[:, u % 2, m, kt * P:(kt + 1) * P], ident)
                last.then_inc(pt_mm, 1)

            score(0)
            score(1)
            for u in range(len(units)):
                turn(u)
                if u + 2 < len(units):
                    score(u + 2)
                pe.wait_ge(pt_ev, base + (u + 1))
                for m in range(2):
                    last = values(units[u], m, PT[:, u % 2, m, :, :])
                last.then_inc(pv_mm, 1)

        def act_units(act, base, units):
            def exps(u):
                act.wait_ge(sm_max, base + (u + 1))
                if u >= 2:
                    act.wait_ge(pt_mm, base + (u - 1))
                klen = units[u]["keys"]
                for m in range(2):
                    last = nc.scalar.activation(E[:, u % 2, m, 0:klen], S[:, u % 2, m, 0:klen], ACT.Exp,
                                                bias=negmax[:, u % 2, m:m + 1], accum_out=total[:, u % 2, m:m + 1])
                last.then_inc(sm_exp, 1)

            exps(0)
            for u in range(len(units)):
                if u + 1 < len(units):
                    exps(u + 1)
                act.wait_ge(pt_mm, base + (u + 1))
                if u >= 2:
                    act.wait_ge(pv_mm, base + (u - 1))
                n, maps = units[u]["keys"] // P, units[u]["turned"]
                nc.scalar.activation(PT[:, u % 2, 0:maps, 0:n, :],
                                     ps[6 + u % 2][:, :].rearrange("p (m k q) -> p m k q", m=2, k=2)[:, 0:maps, 0:n, :],
                                     ACT.Copy).then_inc(pt_ev, 1)

        def dve_units(dve, step, base, units, scale_probs):
            def bias(u):
                w = units[u]
                klen = w["keys"]
                dve.wait_ge(sc_mm, base + (u + 1))
                if u >= 2:
                    dve.wait_ge(sm_exp, base + (u - 1))
                raw = ps[4 + u % 2][:, :].rearrange("p (m k) -> p m k", m=2)[:, :, 0:klen]
                s = S[:, u % 2, :, 0:klen]
                if w["table"] is None:
                    last = nc.vector.tensor_copy(s, raw)
                elif w["minus"] is None:
                    for m in range(2):
                        last = nc.vector.scalar_tensor_tensor(s[:, m, :], raw[:, m, :], w["scale"], w["table"][m],
                                                              ALU.mult, ALU.add)
                else:
                    for m in range(2):
                        last = nc.vector.scalar_tensor_tensor(s[:, m, :], raw[:, m, :], w["minus"][m], w["table"][m],
                                                              ALU.subtract, ALU.add)
                step.after(last)
                nc.vector.tensor_reduce(negmax[:, u % 2, :], s, AX.X, ALU.max, negate=True).then_inc(sm_max, 1)

            bias(0)
            for u in range(len(units)):
                if u + 1 < len(units):
                    bias(u + 1)
                dve.wait_ge(sm_exp, base + (u + 1))
                step.after(nc.vector.reciprocal(rsum[:, u % 2, :], total[:, u % 2, :]))
                scale_probs(units[u], u, step).then_inc(sm_p, 1)

        def plain_scale(unit, u, step):
            klen = unit["keys"]
            if unit["gate"] is not None:
                step.after(nc.vector.tensor_tensor(rsum[:, u % 2, :], rsum[:, u % 2, :], unit["gate"], ALU.mult))
            for m in range(2):
                e = E[:, u % 2, m, 0:klen]
                last = nc.vector.tensor_scalar(e, e, rsum[:, u % 2, m:m + 1], None, ALU.mult)
            return last

        negmax, total, rsum = sb("negmax", [P, 2, 2]), sb("total", [P, 2, 2]), sb("rsum", [P, 2, 2])

        qk = room(16 * SEQ, 0).rearrange("p (b n) -> p b n", b=16)
        vt = room(TT * 1024).rearrange("p (t n) -> p t n", t=TT)
        S = room(1024).rearrange("p (u m k) -> p u m k", u=2, m=2)
        E = room(1024).rearrange("p (u m k) -> p u m k", u=2, m=2)
        PT = room(1024).rearrange("p (u m k q) -> p u m k q", u=2, m=2, k=2)
        shared_top = at[0]
        mixT = room(8 * SEQ).rearrange("p (b n) -> p b n", b=8)
        O = room(TT * 512).rearrange("p (t n) -> p t n", t=TT)
        Osq = room(TT * 512).rearrange("p (t n) -> p t n", t=TT)
        sb_e, sb_l, sb_sp, sb_z, sb_f, sb_w = (room(768).rearrange("p (u n) -> p u n", u=2) for _ in range(6))
        smA = room(512)
        lam2, lamp, ms, rs = room(128), room(2), room(8), room(8)
        neglam = room(1)
        elam = room(2)
        q2 = room(16 * SEQ, 0).rearrange("p (b n) -> p b n", b=16)
        sc = room(TT * 16 * P).rearrange("p (t h n) -> p t h n", t=TT, h=16)
        sc2 = room(16 * P).rearrange("p (h n) -> p h n", h=16)
        top = room(TT * 256).rearrange("p (t h n) -> p t h n", t=TT, h=16)
        topi = room(TT * 256).bitcast(U32).rearrange("p (t h n) -> p t h n", t=TT, h=16)
        topf = room(TT * 256).rearrange("p (t h n) -> p t h n", t=TT, h=16)
        cand = room(8 * 256).rearrange("p (h n) -> p h n", h=8)
        cand2 = room(8 * 256).rearrange("p (h n) -> p h n", h=8)
        best = room(P).rearrange("p (h n) -> p h n", h=8)
        pos = room(P).bitcast(U32).rearrange("p (h n) -> p h n", h=8)
        half_u = room(2 * P).bitcast(U32).rearrange("p (s h n) -> p s h n", s=2, h=8)
        half_f = room(2 * P).rearrange("p (s h n) -> p s h n", s=2, h=8)
        hot = room(8 * 256).rearrange("p (h n a) -> p h n a", h=8, a=16)
        chosen = room(TT * 3 * P).rearrange("p (t s k) -> p t s k", t=TT, s=3)
        gexp = room(TT * P).rearrange("p (t h n) -> p t h n", t=TT, h=8)
        gmax, gsum = room(8), room(8)

        proj_ev = sem("proj_ev")
        lam_sum, lam_exp = sem("lam_sum"), sem("lam_exp")
        o_copied, ms_ready, ms_root, o_scaled, ot_mm, mix_ready = (
            sem(n) for n in ("o_copied", "ms_ready", "ms_root", "o_scaled", "ot_mm", "mix_ready"))
        z_mm, z_log, z_fail, z_sum, z_exp_in, z_w, z_pv, z_out = (
            sem(n) for n in ("z_mm", "z_log", "z_fail", "z_sum", "z_exp_in", "z_w", "z_pv", "z_out"))
        z_abs, z_exp = sem("z_abs"), sem("z_exp")
        wq_ev, key_mm, key_ev = sem("wq_ev"), sem("key_mm"), sem("key_ev")
        g_diff, g_exp, chosen_ready, sel_mm, sel_ev = (
            sem(n) for n in ("g_diff", "g_exp", "chosen_ready", "sel_mm", "sel_ev"))
        hot_ready, hot_mm, gate_ev = sem("hot_ready"), sem("hot_mm"), sem("gate_ev")
        u_act, u_w = sem("u_act"), sem("u_w")

        alibi = cs[:, CONST["alibi"]].rearrange("p (h k) -> p h k", h=4)
        diff_units = []
        for qt in range(TT):
            for h in range(4):
                off = 0 if qt else P
                t = alibi[:, h, off:256]
                diff_units.append(dict(keys=P * (qt + 1), qt=qt, h=h, table=[t, t], scale=1.0, minus=None, gate=None,
                                       turned=1))

        def diff_scores(w, m, out):
            part = slice(64 * m, 64 * m + 64)
            return nc.tensor.matmul(out, qk[part, w["h"], w["qt"] * P:(w["qt"] + 1) * P],
                                    qk[part, 4 + w["h"], 0:w["keys"]], start=True, stop=True)

        def diff_values(w, m, pt):
            if m:
                return diff_values.last
            n = w["keys"] // P
            for kt in range(n):
                diff_values.last = nc.tensor.matmul(ps[w["qt"]][:, w["h"] * P:(w["h"] + 1) * P], pt[:, kt, :],
                                                    vt[:, kt, w["h"] * P:(w["h"] + 1) * P],
                                                    start=(kt == 0), stop=(kt == n - 1))
            return diff_values.last

        def diff_scale(unit, u, step):
            klen = unit["keys"]
            e = E[:, u % 2, :, 0:klen]
            nc.vector.tensor_scalar(e[:, 0, :], e[:, 0, :], rsum[:, u % 2, 0:1], None, ALU.mult)
            step.after(nc.vector.tensor_tensor(rsum[:, u % 2, 1:2], rsum[:, u % 2, 1:2], neglam, ALU.mult))
            return nc.vector.scalar_tensor_tensor(e[:, 0, :], e[:, 1, :], rsum[:, u % 2, 1:2], e[:, 0, :],
                                                  ALU.mult, ALU.add)


        act_sb = [work[:, 0, :], work[:, 1, :]]
        w_sb = [work[:, 2, :], work[:, 3, :]]

        def pe_pairs(pe, block, l, k, pairs, done):
            def up(p, i, tile, guard=True):
                arrived(pe, block, l, tile, i)
                if guard:
                    pe.wait_ge(u_act, done + 2 * i + (p - 1))
                up_features(chunks(tile), xT, 4 + p % 2).then_inc(tile_done, 1)

            def add(p, i, tile, first=False, last=False):
                arrived(pe, block, l, tile, i)
                pe.wait_ge(u_w, done + 2 * i + (p + 1))
                down(slot(tile), lambda j, tt: w_sb[p % 2][:, j * SEQ + tt * P:j * SEQ + (tt + 1) * P],
                     first, last).then_inc(tile_done, 1)

            up(0, 0, k, False)
            up(1, 0, k + 1, False)
            add(0, 0, k + 2, first=True)
            up(2, 0, k + 3)
            add(1, 0, k + 4)
            with pe.Fori(1, (pairs - 2) // 2) as i:
                up(1, i, k + 1)
                add(0, i, k + 2)
                up(2, i, k + 3)
                add(1, i, k + 4)
            n = (pairs - 2) // 2
            up(1, n, k + 1)
            add(0, n, k + 2)
            add(1, n, k + 3, last=True)

        def act_pairs(act, block, l, k, pairs, done, func):
            def one(p, i, tile, guard=True):
                finished(act, block, l, tile, i)
                if guard:
                    act.wait_ge(u_w, done + 2 * i + (p - 1))
                nc.scalar.activation(act_sb[p % 2], ps[4 + p % 2][:, :], func).then_inc(u_act, 1)

            one(0, 0, k, False)
            one(1, 0, k + 1, False)
            with act.Fori(0, (pairs - 2) // 2) as i:
                one(2, i, k + 3)
                one(3, i, k + 5)

        def dve_pairs(dve, block, l, k, pairs, done, weigh):
            def one(p, i, tile, guard=True):
                dve.wait_ge(u_act, done + 2 * i + (p + 1))
                if guard:
                    finished(dve, block, l, tile, i)
                weigh(p, i).then_inc(u_w, 1)

            one(0, 0, None, False)
            one(1, 0, None, False)
            with dve.Fori(0, (pairs - 2) // 2) as i:
                one(2, i, k + 2)
                one(3, i, k + 4)

        hot_a = work[:, 0:2, :].rearrange("p s (t i) -> p s t i", t=4)
        hot_b = work[:, 2:4, :].rearrange("p s (t i) -> p s t i", t=4)
        TURNS = SEQ // 8

        def pe_block1(pe, l):
            pe.wait_ge(small_read, l + 1)
            pe.sem_inc(tile_done, 1)
            pe.wait_ge(xt_ready, l * 8 + 4)
            for j in range(12):
                k = A_PROJ + j
                arrived(pe, 1, l, k)
                if j >= 4:
                    pe.wait_ge(proj_ev, l * 12 + (j - 3))
                (up_features if j < 8 else up_tokens)(chunks(k), xT, 4 + j % 4).then_inc(tile_done, 1)
            pe.wait_ge(proj_ev, l * 12 + 12)
            pe_units(pe, l * UNITS_A, diff_units, diff_scores, diff_values)
            pe.wait_ge(pt_ev, l * UNITS_A + UNITS_A)

            def sb_scores(h):
                part = slice(64 * (h % 2), 64 * (h % 2) + 64)
                q, kk = 8 + h // 2, 12 + h // 2
                if h >= 2:
                    pe.wait_ge(z_fail, l * 8 + (h - 1))
                nc.tensor.matmul(ps[4 + h % 2][:, 0:SEQ], qk[part, kk, 0:P], qk[part, q, :], start=True, stop=True)
                nc.tensor.matmul(ps[4 + h % 2][:, SEQ:SEQ + P], qk[part, kk, P:SEQ], qk[part, q, P:SEQ],
                                 start=True, stop=True).then_inc(z_mm, 1)

            sb_scores(0)
            for h in range(8):
                if h + 1 < 8:
                    sb_scores(h + 1)
                pe.wait_ge(z_fail, l * 8 + (h + 1))
                if h:
                    pe.wait_ge(z_exp_in, l * 8 + h)
                f = sb_f[:, h % 2, :]
                nc.tensor.matmul(ps[6][:, 0:SEQ], tri, f[:, 0:SEQ], start=True, stop=False)
                nc.tensor.matmul(ps[6][:, P:SEQ], ones, f[:, SEQ:SEQ + P], start=False, stop=True)
                nc.tensor.matmul(ps[6][:, SEQ:SEQ + P], tri, f[:, SEQ:SEQ + P], start=True,
                                 stop=True).then_inc(z_sum, 1)
                pe.wait_ge(z_w, l * 8 + (h + 1))
                bank = 7 if h // 2 % 2 == 0 else 2
                part = slice(64 * (h % 2), 64 * (h % 2) + 64)
                if h % 2 == 0 and h >= 4:
                    pe.wait_ge(z_out, l * 4 + (h // 2 - 1))
                v = slice(512 + 64 * h, 512 + 64 * h + 64)
                w = sb_w[:, h % 2, :]
                nc.tensor.matmul(ps[bank][part, 0:SEQ], vt[:, 0, v], w[:, 0:SEQ], start=True, stop=False)
                nc.tensor.matmul(ps[bank][part, P:SEQ], vt[:, 1, v], w[:, SEQ:SEQ + P], start=False,
                                 stop=True).then_inc(z_pv, 1)
            for tt in range(TT):
                pe.wait_ge(o_scaled, l * TT + (tt + 1))
                for h in range(4):
                    last = nc.tensor.transpose(ps[4 + tt][:, h * P:(h + 1) * P], O[:, tt, h * P:(h + 1) * P], ident)
                last.then_inc(ot_mm, 1)
            pe.wait_ge(mix_ready, l * TT + TT)
            pe.wait_ge(z_out, l * 4 + 4)
            for j in range(4):
                arrived(pe, 1, l, A_WO + j)
                down(slot(A_WO + j), lambda i, tt: mixT[:, 2 * j + i, tt * P:(tt + 1) * P], j == 0,
                     j == 3).then_inc(tile_done, 1)
            pe_turn_x(pe, l * 2)
            pe.wait_ge(xt_ready, l * 8 + 8)
            for j in range(8):
                k = A_WQ + j
                arrived(pe, 1, l, k)
                if j >= 4:
                    pe.wait_ge(wq_ev, l * 8 + (j - 3))
                up_features(chunks(k), xT, 4 + j % 4).then_inc(tile_done, 1)
            pe.wait_ge(wq_ev, l * 8 + 8)
            arrived(pe, 1, l, A_KEYS)
            for n in range(8):
                tt, g = n // 4, n % 4
                if n >= 4:
                    pe.wait_ge(key_ev, l * 8 + (n - 3))
                for j in range(4):
                    hp = 4 * g + j
                    last = nc.tensor.matmul(ps[4 + g][:, j * P:(j + 1) * P], q2[:, hp, tt * P:(tt + 1) * P],
                                            slot(A_KEYS)[:, hp * P:(hp + 1) * P], start=True, stop=True)
                last.then_inc(key_mm if n < 7 else tile_done, 1)
            for tt in range(TT):
                pe.wait_ge(chosen_ready, l * TT + (tt + 1))
                for s in range(3):
                    last = nc.tensor.transpose(ps[tt][:, s * P:(s + 1) * P], chosen[:, tt, s, :], ident)
                last.then_inc(sel_mm, 1)
            pe.wait_ge(key_ev, l * 8 + 8)

            def gate_rows(i, b, guard):
                pe.wait_ge(hot_ready, l * (2 * TURNS) + 2 * i + (b + 1))
                if guard:
                    pe.wait_ge(gate_ev, l * (2 * TURNS) + 2 * i + (b - 1))
                for t in range(4):
                    last = nc.tensor.matmul(ps[6 + b][:, t * P:(t + 1) * P], hot_b[:, b, t, :], hot_a[:, b, t, :],
                                            start=True, stop=True)
                last.then_inc(hot_mm, 1)

            gate_rows(0, 0, False)
            gate_rows(0, 1, False)
            with pe.Fori(1, TURNS) as i:
                gate_rows(i, 0, True)
                gate_rows(i, 1, True)
            pe.wait_ge(gate_ev, l * (2 * TURNS) + 2 * TURNS)
            pe_pairs(pe, 1, l, A_EXP, PAIRS, l * PAIRS)
            pe_turn_x(pe, l * 2 + 1)

        def act_block1(act, l):
            act.wait_ge(lam_sum, l + 1)
            nc.scalar.activation(elam, lamp, ACT.Exp).then_inc(lam_exp, 1)
            for j in range(12):
                k = A_PROJ + j
                finished(act, 1, l, k)
                src = ps[4 + j % 4][:, :].rearrange("p (a n) -> p a n", a=2)
                if j < 8:
                    scale = HD ** -0.5 if j in (0, 1, 4, 5) else 1.0
                    nc.scalar.activation(qk[:, 2 * j:2 * j + 2, :], src, ACT.Copy, scale=scale).then_inc(proj_ev, 1)
                else:
                    c = (j - 8) * 256
                    nc.scalar.activation(vt[:, :, c:c + 256], src, ACT.Copy).then_inc(proj_ev, 1)
            act_units(act, l * UNITS_A, diff_units)
            act.wait_ge(pv_mm, l * UNITS_A + UNITS_A)
            for tt in range(TT):
                nc.scalar.activation(O[:, tt, :], ps[tt][:, :], ACT.Copy).then_inc(o_copied, 1)
            for h in range(8):
                u = h % 2
                act.wait_ge(z_mm, l * 8 + (h + 1))
                if h >= 2:
                    act.wait_ge(z_fail, l * 8 + (h - 1))
                nc.scalar.activation(sb_e[:, u, :], ps[4 + u][:, 0:384], ACT.Abs).then_inc(z_abs, 1)
                act.wait_ge(z_abs, l * 16 + (2 * h + 1))
                nc.scalar.activation(sb_e[:, u, :], sb_e[:, u, :], ACT.Exp, scale=-1.0).then_inc(z_abs, 1)
                act.wait_ge(z_abs, l * 16 + (2 * h + 2))
                nc.scalar.activation(sb_l[:, u, :], sb_e[:, u, :], ACT.Ln, bias=1.0).then_inc(z_log, 1)
                act.wait_ge(z_exp_in, l * 8 + (h + 1))
                if h >= 2:
                    act.wait_ge(z_pv, l * 8 + (h - 1))
                nc.scalar.activation(sb_w[:, u, :], sb_z[:, u, :], ACT.Exp).then_inc(z_w, 1)
                if h % 2:
                    act.wait_ge(z_pv, l * 8 + (h + 1))
                    bank = 7 if h // 2 % 2 == 0 else 2
                    nc.scalar.activation(mixT[:, 4 + h // 2, :], ps[bank][:, 0:SEQ], ACT.Copy).then_inc(z_out, 1)
            act.wait_ge(ms_ready, l + 1)
            nc.scalar.activation(rs, ms, ACT.Sqrt, scale=1.0 / P, bias=cs[:, CONST["eps"]][:, 0:1]).then_inc(ms_root, 1)
            for tt in range(TT):
                act.wait_ge(ot_mm, l * TT + (tt + 1))
                nc.scalar.activation(mixT[:, 0:4, tt * P:(tt + 1) * P],
                                     ps[4 + tt][:, :].rearrange("p (h q) -> p h q", h=4), ACT.Copy,
                                     scale=smA[:, A_SUBG - 256:A_SUBG - 255]).then_inc(mix_ready, 1)
            act_norm(act, l * 2)
            for j in range(8):
                finished(act, 1, l, A_WQ + j)
                nc.scalar.activation(q2[:, 2 * j:2 * j + 2, :], ps[4 + j % 4][:, :].rearrange("p (a n) -> p a n", a=2),
                                     ACT.Copy).then_inc(wq_ev, 1)
            for n in range(8):
                tt, g = n // 4, n % 4
                if n < 7:
                    act.wait_ge(key_mm, l * 7 + (n + 1))
                else:
                    finished(act, 1, l, A_KEYS)
                nc.scalar.activation(sc[:, tt, 4 * g:4 * g + 4, :],
                                     ps[4 + g][:, :].rearrange("p (h n) -> p h n", h=4), ACT.Copy).then_inc(key_ev, 1)
            for tt in range(TT):
                act.wait_ge(g_diff, l * TT + (tt + 1))
                nc.scalar.activation(gexp[:, tt, :, :], gexp[:, tt, :, :], ACT.Exp).then_inc(g_exp, 1)
            for tt in range(TT):
                act.wait_ge(sel_mm, l * TT + (tt + 1))
                nc.scalar.activation(selT[:, :, tt * P:(tt + 1) * P],
                                     ps[tt][:, 0:3 * P].rearrange("p (s t) -> p s t", s=3), ACT.Copy).then_inc(sel_ev, 1)
            with act.Fori(0, TURNS) as i:
                for b in range(2):
                    act.wait_ge(hot_mm, l * (2 * TURNS) + 2 * i + (b + 1))
                    nc.scalar.activation(arena[:, bass.ds(i * 1024 + b * 512, 512)], ps[6 + b][:, :],
                                         ACT.Copy).then_inc(gate_ev, 1)
            act_pairs(act, 1, l, A_EXP, PAIRS, l * PAIRS, ACT.Gelu)
            act_norm(act, l * 2 + 1)

        def dve_block1(dve, l):
            step = Steps(dve, dve_step, 0, DVE_A, l)
            arrived(dve, 1, l, A_SMALL)
            small = slot(A_SMALL)
            lq = small[:, 0:256].rearrange("p (a b n) -> p a b n", a=2, b=2)
            nc.vector.tensor_copy(smA[:, 0:4], small[:, A_SUBG:A_SUBG + 4])
            step.after(nc.vector.tensor_tensor(lam2.rearrange("p (a n) -> p a n", a=2), lq[:, :, 0, :], lq[:, :, 1, :],
                                               ALU.mult))
            dve.sem_inc(small_read, 1)
            nc.vector.tensor_reduce(lamp, lam2.rearrange("p (a n) -> p a n", a=2), AX.X, ALU.add).then_inc(lam_sum, 1)
            step.after(nc.vector.tensor_scalar(smA[:, 0:1], smA[:, 0:1], smA[:, 2:3], None, ALU.mult))
            dve.wait_ge(lam_exp, l + 1)
            step.after(nc.vector.tensor_tensor(neglam, elam[:, 1:2], elam[:, 0:1], ALU.subtract))
            step.after(nc.vector.tensor_tensor(neglam, neglam, smA[:, 1:2], ALU.subtract))
            dve_units(dve, step, l * UNITS_A, diff_units, diff_scale)
            dve.wait_ge(o_copied, l * TT + TT)
            step.after(nc.vector.tensor_tensor(Osq, O, O, ALU.mult))
            nc.vector.tensor_reduce(ms, Osq.rearrange("p t (h n) -> p (t h) n", h=4), AX.X, ALU.add).then_inc(ms_ready, 1)
            strict, negstrict = cs[:, CONST["strict"]], cs[:, CONST["negstrict"]]
            for h in range(8):
                u = h % 2
                z = ps[4 + u][:, 0:384]
                dve.wait_ge(z_log, l * 8 + (h + 1))
                if h >= 2:
                    dve.wait_ge(z_w, l * 8 + (h - 1))
                nc.vector.tensor_tensor(sb_z[:, u, :], z, strict, ALU.add)
                step.after(nc.vector.scalar_tensor_tensor(sb_sp[:, u, :], z, 0.0, sb_l[:, u, :], ALU.max, ALU.add))
                nc.vector.tensor_tensor(sb_f[:, u, :], sb_sp[:, u, :], negstrict, ALU.mult).then_inc(z_fail, 1)
                dve.wait_ge(z_sum, l * 8 + (h + 1))
                nc.vector.tensor_tensor(sb_z[:, u, :], ps[6][:, 0:384], sb_z[:, u, :], ALU.add).then_inc(z_exp_in, 1)
            dve.wait_ge(ms_root, l + 1)
            step.after(nc.vector.reciprocal(rs, rs))
            for tt in range(TT):
                o = O[:, tt, :].rearrange("p (h n) -> p h n", h=4)
                r = rs[:, 4 * tt:4 * tt + 4].unsqueeze(2).to_broadcast([P, 4, P])
                nc.vector.tensor_tensor(o, o, r, ALU.mult).then_inc(o_scaled, 1)
            dve_norm(dve, step, l * 2, 1, l, A_LN1)
            for tt in range(TT):
                dve.wait_ge(key_ev, l * 8 + 4 * (tt + 1))
                carry_wait()
                for h in range(16):
                    last = nc.vector.max(top[:, tt, h, 0:8], sc[:, tt, h, :])
                step.after(last)
                carry_wait()
                for h in range(16):
                    nc.vector.max_index(topi[:, tt, h, 0:8], top[:, tt, h, 0:8], sc[:, tt, h, :])
                    last = nc.vector.match_replace(sc2[:, h, :], top[:, tt, h, 0:8], sc[:, tt, h, :], NEG * 1e8)
                step.after(last)
                carry_wait()
                for h in range(16):
                    last = nc.vector.max(top[:, tt, h, 8:16], sc2[:, h, :])
                step.after(last)
                carry_wait()
                for h in range(16):
                    last = nc.vector.max_index(topi[:, tt, h, 8:16], top[:, tt, h, 8:16], sc2[:, h, :])
                step.after(last)
                t2 = top[:, tt, :, :].rearrange("p (h s) n -> p h s n", s=2)
                nc.vector.tensor_copy(topf[:, tt, :, :], topi[:, tt, :, :])
                for h in range(8):
                    last = nc.vector.tensor_tensor(cand[:, h, :].rearrange("p (a b) -> p a b", a=16),
                                                   t2[:, h, 0, :].unsqueeze(2).to_broadcast([P, 16, 16]),
                                                   t2[:, h, 1, :].unsqueeze(1).to_broadcast([P, 16, 16]), ALU.add)
                step.after(last)
                carry_wait()
                for h in range(8):
                    last = nc.vector.max(best[:, h, 0:8], cand[:, h, :])
                step.after(last)
                carry_wait()
                for h in range(8):
                    nc.vector.max_index(pos[:, h, 0:8], best[:, h, 0:8], cand[:, h, :])
                    last = nc.vector.match_replace(cand2[:, h, :], best[:, h, 0:8], cand[:, h, :], NEG * 1e8)
                step.after(last)
                carry_wait()
                for h in range(8):
                    last = nc.vector.max(best[:, h, 8:16], cand2[:, h, :])
                step.after(last)
                carry_wait()
                for h in range(8):
                    last = nc.vector.max_index(pos[:, h, 8:16], best[:, h, 8:16], cand2[:, h, :])
                nc.vector.tensor_tensor(gexp[:, tt, :, :], best, best[:, :, 0:1].to_broadcast([P, 8, 16]),
                                        ALU.subtract).then_inc(g_diff, 1)
                dve.wait_ge(g_diff, l * TT + (tt + 1))
                nc.vector.tensor_scalar(half_u[:, 0, :, :], pos, 4, None, ALU.logical_shift_right)
                step.after(nc.vector.tensor_scalar(half_u[:, 1, :, :], pos, 15, None, ALU.bitwise_and))
                step.after(nc.vector.tensor_copy(half_f, half_u))
                f2 = topf[:, tt, :, :].rearrange("p (h s) n -> p h s n", s=2)
                for s in range(2):
                    for h in range(8):
                        last = nc.vector.tensor_tensor(hot[:, h, :, :],
                                                       half_f[:, s, h, :].unsqueeze(2).to_broadcast([P, 16, 16]),
                                                       iota[:, 0:16].unsqueeze(1).to_broadcast([P, 16, 16]), ALU.is_equal)
                    step.after(last)
                    for h in range(8):
                        last = nc.vector.tensor_tensor(hot[:, h, :, :], hot[:, h, :, :],
                                                       f2[:, h, s, :].unsqueeze(1).to_broadcast([P, 16, 16]), ALU.mult)
                    step.after(last)
                    step.after(nc.vector.tensor_reduce(chosen[:, tt, s, :].rearrange("p (h n) -> p h n", h=8), hot,
                                                       AX.X, ALU.add))
                dve.wait_ge(g_exp, l * TT + (tt + 1))
                step.after(nc.vector.tensor_reduce(gsum, gexp[:, tt, :, :], AX.X, ALU.add))
                step.after(nc.vector.reciprocal(gsum, gsum))
                nc.vector.tensor_tensor(chosen[:, tt, 2, :].rearrange("p (h n) -> p h n", h=8), gexp[:, tt, :, :],
                                        gsum.unsqueeze(2).to_broadcast([P, 8, 16]), ALU.mult).then_inc(chosen_ready, 1)

            dve.wait_ge(sel_ev, l * TT + TT)

            def one_hot(i, b, guard):
                if guard:
                    dve.wait_ge(hot_mm, l * (2 * TURNS) + 2 * i + (b - 1))
                for t in range(4):
                    tok = bass.ds(i * 8 + (4 * b + t), 1)
                    nc.vector.tensor_scalar(hot_b[:, b, t, :], iota, selT[:, 1, tok], None, ALU.is_equal)
                    last = nc.vector.tensor_scalar(hot_a[:, b, t, :], iota, selT[:, 0, tok], selT[:, 2, tok],
                                                   ALU.is_equal, ALU.mult)
                last.then_inc(hot_ready, 1)

            one_hot(0, 0, False)
            one_hot(0, 1, False)
            with dve.Fori(1, TURNS) as i:
                one_hot(i, 0, True)
                one_hot(i, 1, True)
            dve.wait_ge(gate_ev, l * (2 * TURNS) + 2 * TURNS)

            def weigh(p, i):
                g = gates[:, :, bass.ds(i * 4 + 2 * p, 2)].rearrange("p t b -> p b t")
                return nc.vector.tensor_tensor(w_sb[p % 2].rearrange("p (b t) -> p b t", b=2),
                                               act_sb[p % 2].rearrange("p (b t) -> p b t", b=2), g, ALU.mult)

            dve_pairs(dve, 1, l, A_EXP, PAIRS, l * PAIRS, weigh)
            dve_norm(dve, step, l * 2 + 1, 1, l, A_LN2)
            step.close()

        at[0] = 0
        nq = room(4 * SEQ).rearrange("p (b n) -> p b n", b=4)
        kvc = room(2 * SEQ).rearrange("p (b n) -> p b n", b=2)
        ks = room(2 * SEQ).rearrange("p (b n) -> p b n", b=2)
        kw = room(2 * SEQ).rearrange("p (b n) -> p b n", b=2)
        fq = room(2 * SEQ).rearrange("p (b n) -> p b n", b=2)
        fk = room(2 * SEQ).rearrange("p (b n) -> p b n", b=2)
        vsw = room(TT * 256).rearrange("p (t n) -> p t n", t=TT)
        fv = room(TT * 256).rearrange("p (t n) -> p t n", t=TT)
        cqkv = room(TT * 512).rearrange("p (t n) -> p t n", t=TT)
        misc = room(TT * 64).rearrange("p (t n) -> p t n", t=TT)
        assert at[0] <= shared_top - 3 * 1024
        at[0] = shared_top
        T = room(8 * 256).rearrange("p (h k) -> p h k", h=8)
        smB = room(TILE)
        cT = room(4 * SEQ).rearrange("p (b n) -> p b n", b=4)
        mq = room(TT * 384).rearrange("p (t h n) -> p t h n", t=TT, h=4)
        mk = room(TT * 384).rearrange("p (t h n) -> p t h n", t=TT, h=4)
        mv2 = room(TT * 256).rearrange("p (t h n) -> p t h n", t=TT, h=4)
        mqT = room(4 * SEQ).rearrange("p (h n) -> p h n", h=4)
        mkT = room(4 * SEQ).rearrange("p (h n) -> p h n", h=4)
        lfb = room(TT * 512).rearrange("p (t h n) -> p t h n", t=TT, h=4)
        xb = room(32 * 32).rearrange("p (l g n) -> p l g n", l=32, g=2)
        hid = room(64).rearrange("p (s n) -> p s n", s=2)
        kcT = room(32)
        vc = room(2 * HD)
        cS = room(TT * 8 * 16).rearrange("p (t h n) -> p t h n", t=TT, h=8)
        oT = room(8 * SEQ).rearrange("p (b n) -> p b n", b=8)
        merged = room(8 * SEQ).rearrange("p (b n) -> p b n", b=8)
        late = room(3 * 1024)
        PcT = late[:, 0:TT * 1024].rearrange("p (t h q) -> p t h q", t=TT, h=8)
        sig = late[:, 0:3 * 512].rearrange("p (b n) -> p b n", b=3)
        prod = late[:, 3 * 512:6 * 512].rearrange("p (b n) -> p b n", b=3)
        xq = room(2 * SEQ).rearrange("p (b n) -> p b n", b=2)
        xk = room(2 * SEQ).rearrange("p (b n) -> p b n", b=2)
        xv = room(TT * 256).rearrange("p (t n) -> p t n", t=TT)
        xo = room(2 * SEQ).rearrange("p (b n) -> p b n", b=2)
        sq = merged[:, 0:4, :].rearrange("p (t b) n -> p t (b n)", t=TT)
        rt = room(6 * 64).rearrange("p (s h n) -> p s h n", s=6, h=4)
        rk = room(TT * 32).rearrange("p (t n) -> p t n", t=TT)
        gsig = room(TT * 24).rearrange("p (t h b) -> p t h b", t=TT, b=3)
        rms = room(4).rearrange("p (t s) -> p t s", t=TT)
        rmr = room(4).rearrange("p (t s) -> p t s", t=TT)
        fy, fa, fe, fl, flf = (room(8) for _ in range(5))
        negcum = room(8).rearrange("p (t h) -> p t h", t=TT)
        cmax, csum = (room(16).rearrange("p (t h) -> p t h", t=TT) for _ in range(2))
        bd = room(384)

        b_ev, b_rms, b_root, b_scaled, c_mm, c_ev = (
            sem(n) for n in ("b_ev", "b_rms", "b_root", "b_scaled", "c_mm", "c_ev"))
        q_mm, kv_mm, kv_ev, mla_ready, mt_mm, mt_ev = (
            sem(n) for n in ("q_mm", "kv_mm", "kv_ev", "mla_ready", "mt_mm", "mt_ev"))
        xb_ready, hid_act, kc_mm, kc_ev = sem("xb_ready"), sem("hid_act"), sem("kc_mm"), sem("kc_ev")
        f_y, f_log, f_ready, f_mm, f_cum = (sem(n) for n in ("f_y", "f_log", "f_ready", "f_mm", "f_cum"))
        g_sig, cs_mm, cs_max, cs_exp, cs_p, ct_mm, ct_ev = (
            sem(n) for n in ("g_sig", "cs_mm", "cs_max", "cs_exp", "cs_p", "ct_mm", "ct_ev"))
        ob_ev, sig_mm, sig_ready, br_mm, br_used = (sem(n) for n in ("ob_ev", "sig_mm", "sig_ready", "br_mm", "br_used"))
        x_ev, xo_ev = sem("x_ev"), sem("xo_ev")
        t_mm, t_ev, t_out, t_in, t_flip, t_ready = (
            sem(n) for n in ("t_mm", "t_ev", "t_out", "t_in", "t_flip", "t_ready"))

        causal = cs[:, CONST["causal"]]
        cum = cs[:, CONST["cum"]]
        rope = cs[:, CONST["rope"]].rearrange("p (t s n) -> p t s n", t=TT, s=2)
        cmpok = cs[:, CONST["cmpok"]].rearrange("p (t n) -> p t n", t=TT)
        CN = [7, 15]
        smg = smB[:, B_QN:B_QN + 4]
        w_uq = smB[:, B_UQ:B_UKV].rearrange("p (c n) -> p c n", c=3)
        w_ukv = smB[:, B_UKV:B_W2]
        w_2 = smB[:, B_W2:B_PE].rearrange("p (s n) -> p s n", s=2)

        def unit(kind, pair, qt, **more):
            n = P * (qt + 1)
            off = 0 if qt else P
            u = dict(kind=kind, pair=pair, qt=qt, keys=n, scale=1.0, minus=None, gate=None,
                     table=[causal[:, off:256]] * 2, turned=2)
            u.update(more)
            return u

        mix_units = []
        for pair in range(4):
            for qt in range(TT):
                for kind in (1, 2):
                    off = 0 if qt else P
                    mix_units.append(unit(kind, pair, qt, gate=gsig[:, qt, 2 * pair:2 * pair + 2, kind],
                                          table=[T[:, 2 * pair + m, off:256] for m in range(2)]))
        for pair in range(2):
            for qt in range(TT):
                mix_units.append(unit("mla", pair, qt, scale=96 ** -0.5))
        for pair in range(2):
            for qt in range(TT):
                mix_units.append(unit("fox", pair, qt, minus=[negcum[:, qt, 2 * pair + m:2 * pair + m + 1]
                                                              for m in range(2)]))
        mem_units = [unit("mem", pair, qt, keys=SEQ, table=None) for pair in range(2) for qt in range(TT)]

        def b_scores(w, m, out):
            kind, pair, qt = w["kind"], w["pair"], w["qt"]
            q = slice(qt * P, (qt + 1) * P)
            part = slice(64 * m, 64 * m + 64)
            if kind in (1, 2):
                k = ks if kind == 1 else kw
                return nc.tensor.matmul(out, nq[part, pair, q], k[part, pair // 2, 0:w["keys"]], start=True, stop=True)
            if kind == "mla":
                h = 2 * pair + m
                return nc.tensor.matmul(out, mqT[0:96, h, q], mkT[0:96, h, 0:w["keys"]], start=True, stop=True)
            if kind == "mem":
                return nc.tensor.matmul(out, xq[part, pair, q], xk[part, pair, :], start=True, stop=True)
            h = 2 * pair + m
            nc.tensor.matmul(out, fq[part, pair, q], fk[part, pair, 0:w["keys"]], start=True, stop=False)
            last = nc.tensor.matmul(out, lfb[:, 0, h, :], cum[:, 0:w["keys"]], start=False, stop=(qt == 0))
            if qt:
                last = nc.tensor.matmul(out[:, P:SEQ], lfb[:, 1, h, :], cum[:, 0:P], start=False, stop=True)
            return last

        def b_values(w, m, pt):
            kind, pair, qt = w["kind"], w["pair"], w["qt"]
            part = slice(64 * m, 64 * m + 64)
            col = qt * P
            h = 2 * pair + m
            if kind in (1, 2):
                bank, v = pair, (lambda kt: vsw[:, kt, (kind - 1) * P + (pair // 2) * HD:][:, 0:HD])
            elif kind == "mla":
                bank, col, v = pair, col + SEQ, (lambda kt: mv2[:, kt, h, :])
            elif kind == "fox":
                bank, col, v = 2 + pair, col + SEQ, (lambda kt: fv[:, kt, h * HD:(h + 1) * HD])
            else:
                bank, v = pair, (lambda kt: xv[:, kt, h * HD:(h + 1) * HD])
            out = ps[bank][part, col:col + P]
            n = w["keys"] // P
            for kt in range(n):
                last = nc.tensor.matmul(out, v(kt), pt[:, kt, :], start=(kt == 0 and kind != 2),
                                        stop=(kt == n - 1 and kind != 1), skip_group_check=(kind in (1, 2)))
            if kind == 2:
                g = pair // 2
                last = nc.tensor.matmul(out, vc[0:CN[qt], g * HD:(g + 1) * HD], PcT[0:CN[qt], qt, h, :],
                                        start=False, stop=True, skip_group_check=True)
            return last

        def pe_block2(pe, l):
            turns = 4 + 8 * LAYERS + 12 * l
            pe.wait_ge(small_read, LAYERS + l + 1)
            pe.sem_inc(tile_done, 1)
            pe.wait_ge(xt_ready, turns)
            for j in range(12):
                k = B_PROJ + j
                arrived(pe, 2, l, k)
                if j >= 4:
                    pe.wait_ge(b_ev, l * 12 + (j - 3))
                up = up_features(chunks(k), xT, 4 + j % 4) if j < 7 else \
                    up_tokens(chunks(k), xT, 4 + j % 4, 64 if j == 11 else 256)
                up.then_inc(tile_done, 1)
            pe.wait_ge(b_ev, l * 12 + 12)
            pe.wait_ge(xb_ready, l + 1)
            for j in range(2):
                arrived(pe, 2, l, B_CMP + j)
                w = slot(B_CMP + j).rearrange("p (l n) -> p l n", l=16)
                for s in range(2):
                    part = slice(64 * s, 64 * s + 64)
                    for i in range(16):
                        last = nc.tensor.matmul(ps[4 + s][:, 0:2 * N_CMP], w[part, i, :],
                                                xb[part, 16 * j + i, :, 0:N_CMP],
                                                start=(i == 0 and j == 0), stop=(i == 15 and j == 1))
                last.then_inc(tile_done, 1)
            pe.wait_ge(b_scaled, l + 1)
            for tt in range(TT):
                for c in range(4):
                    last = nc.tensor.transpose(ps[tt][:, c * P:(c + 1) * P], cqkv[:, tt, c * P:(c + 1) * P], ident)
                last.then_inc(c_mm, 1)
            pe.wait_ge(hid_act, l * 2 + 2)
            for half in range(2):
                nc.tensor.matmul(ps[6][64 * half:64 * half + 64, 0:2 * N_CMP], w_2[:, 0, :], hid[:, 0, 0:2 * N_CMP],
                                 start=True, stop=True)
            for g in range(2):
                last = nc.tensor.matmul(ps[7][0:N_CMP, g * HD:(g + 1) * HD], hid[:, 1, g * N_CMP:(g + 1) * N_CMP],
                                        w_2[:, 1, :], start=True, stop=True)
            last.then_inc(kc_mm, 1)
            pe.wait_ge(f_ready, l + 1)
            lf = flf.rearrange("p (t h) -> p t h", t=TT)
            nc.tensor.matmul(ps[3][:, 0:4], cum[:, 0:P], lf[:, 0, :], start=True, stop=True)
            nc.tensor.matmul(ps[3][:, 4:8], cum[:, P:SEQ], lf[:, 0, :], start=True, stop=False)
            nc.tensor.matmul(ps[3][:, 4:8], cum[:, 0:P], lf[:, 1, :], start=False, stop=True).then_inc(f_mm, 1)
            pe.wait_ge(f_cum, l + 1)
            for tt in range(TT):
                pe.wait_ge(c_ev, l * 2 + (tt + 1))
                t = slice(tt * P, (tt + 1) * P)
                for c in range(3):
                    last = nc.tensor.matmul(ps[2 + tt][:, 0:384], cT[:, c, t], w_uq[:, c, :], start=(c == 0),
                                            stop=(c == 2))
                last.then_inc(q_mm, 1)
                nc.tensor.matmul(ps[4 + tt][:, :], cT[:, 3, t], w_ukv, start=True, stop=True).then_inc(kv_mm, 1)
            pe.wait_ge(kc_ev, l * 2 + 2)
            for tt in range(TT):
                for h in range(8):
                    part = slice(64 * (h % 2), 64 * (h % 2) + 64)
                    g = h // 4
                    col = 64 * tt + h // 2 * 16
                    last = nc.tensor.matmul(ps[6 + h % 2][:, col:col + N_CMP], nq[part, h // 2, tt * P:(tt + 1) * P],
                                            kcT[part, g * N_CMP:(g + 1) * N_CMP], start=True, stop=True)
                last.then_inc(cs_mm, 1)
            for tt in range(TT):
                pe.wait_ge(mla_ready, l * 2 + (tt + 1))
                for j, src in enumerate((mq, mk)):
                    for h in range(4):
                        last = nc.tensor.transpose(ps[2 * j + tt][0:96, h * P:(h + 1) * P], src[:, tt, h, :], ident)
                    last.then_inc(mt_mm, 1)
            for tt in range(TT):
                pe.wait_ge(cs_p, l * 2 + (tt + 1))
                for g in range(2):
                    for h in range(4):
                        last = nc.tensor.transpose(ps[4 + 2 * tt + g][0:CN[tt], h * P:(h + 1) * P],
                                                   cS[:, tt, 4 * g + h, 0:CN[tt]], ident)
                    last.then_inc(ct_mm, 1)
            pe.wait_ge(mt_ev, l * 4 + 4)
            pe.wait_ge(ct_ev, l * 4 + 4)
            pe_units(pe, done_b + l * UNITS_B, mix_units, b_scores, b_values)
            pe.wait_ge(ob_ev, l * 4 + 4)
            for i in range(4):
                for b in range(3):
                    k = B_GATE + 4 * i + b
                    arrived(pe, 2, l, k)
                    if i:
                        pe.wait_ge(sig_ready, l * 12 + (3 * (i - 1) + b + 1))
                    up_features(chunks(k), xT, 4 + b).then_inc(tile_done, 1)
                k = B_GATE + 4 * i + 3
                arrived(pe, 2, l, k)
                if i:
                    pe.wait_ge(br_used, l * 4 + i)
                w = chunks(k)
                for b, cc in enumerate(((0, 2, 4, 6), (1, 3), (5, 7))):
                    for fb in range(2):
                        for n, c in enumerate(cc):
                            last = nc.tensor.matmul(ps[b][:, fb * SEQ:(fb + 1) * SEQ], w[:, c, fb * P:(fb + 1) * P],
                                                    oT[:, c, :], start=(n == 0), stop=(n == len(cc) - 1))
                last.then_inc(tile_done, 1)
            pe.wait_ge(br_used, l * 4 + 4)
            for j in range(4):
                arrived(pe, 2, l, B_MIX + j)
                down(slot(B_MIX + j), lambda i, tt: merged[:, 2 * j + i, tt * P:(tt + 1) * P], j == 0,
                     j == 3).then_inc(tile_done, 1)
            norm = 2 * LAYERS + 3 * l
            pe_turn_x(pe, norm)
            pe.wait_ge(xt_ready, turns + 4)
            arrived(pe, 2, l, B_XQ)
            up_features(chunks(B_XQ), xT, 4).then_inc(tile_done, 1)
            arrived(pe, 2, l, B_MEM)
            arrived(pe, 2, l, B_XK)
            up_features(chunks(B_XK), chunks(B_MEM), 5)
            arrived(pe, 2, l, B_XV)
            up_tokens(chunks(B_XV), chunks(B_MEM), 6).then_inc(tile_done, 3)
            pe.wait_ge(x_ev, l * 3 + 3)
            pe_units(pe, done_b + l * UNITS_B + len(mix_units), mem_units, b_scores, b_values)
            pe.wait_ge(xo_ev, l * 2 + 2)
            arrived(pe, 2, l, B_XO)
            down(slot(B_XO), lambda i, tt: xo[:, i, tt * P:(tt + 1) * P], True, True).then_inc(tile_done, 1)
            pe_turn_x(pe, norm + 1)
            pe.wait_ge(xt_ready, turns + 8)
            pe_pairs(pe, 2, l, B_MLP, MLP_PAIRS, LAYERS * PAIRS + l * MLP_PAIRS)
            for k in range(B_LN3 + 1, B_TILES):
                arrived(pe, 2, l, k)
            pe_turn_x(pe, norm + 2, B_TILES - B_LN3)

        done_b = LAYERS * UNITS_A

        def act_block2(act, l):
            dests = [nq[:, 0:2, :], nq[:, 2:4, :], kvc, ks, kw, fq, fk, vsw, fv, cqkv[:, :, 0:256], cqkv[:, :, 256:512],
                     misc]
            for j in range(12):
                finished(act, 2, l, B_PROJ + j)
                n = 64 if j == 11 else 256
                src = ps[4 + j % 4][:, :].rearrange("p (a n) -> p a n", a=2)[:, :, 0:n]
                nc.scalar.activation(dests[j], src, ACT.Copy, scale=HD ** -0.5 if j in (0, 1, 5) else 1.0)\
                    .then_inc(b_ev, 1)
            act.wait_ge(b_ev, l * 12 + 12)
            nc.scalar.activation(gsig.rearrange("p t h b -> p t (h b)"), misc[:, :, 32:56], ACT.Sigmoid)\
                .then_inc(g_sig, 1)
            act.wait_ge(b_rms, l + 1)
            nc.scalar.activation(rmr[:, :, 0], rms[:, :, 0], ACT.Sqrt, scale=1.0 / 384, bias=cs[:, CONST["eps"]][:, 1:2])
            nc.scalar.activation(rmr[:, :, 1], rms[:, :, 1], ACT.Sqrt, scale=1.0 / P, bias=cs[:, CONST["eps"]][:, 1:2])\
                .then_inc(b_root, 1)
            act.wait_ge(f_y, l + 1)
            nc.scalar.activation(fa, fy, ACT.Abs).then_inc(f_log, 1)
            act.wait_ge(f_log, l * 3 + 1)
            nc.scalar.activation(fe, fa, ACT.Exp, scale=-1.0).then_inc(f_log, 1)
            act.wait_ge(f_log, l * 3 + 2)
            nc.scalar.activation(fl, fe, ACT.Ln, bias=1.0).then_inc(f_log, 1)
            finished(act, 2, l, B_CMP + 1)
            for s in range(2):
                nc.scalar.activation(hid[:, s, 0:2 * N_CMP], ps[4 + s][:, 0:2 * N_CMP], ACT.Gelu_apprx_tanh)\
                    .then_inc(hid_act, 1)
            act.wait_ge(kc_mm, l + 1)
            nc.scalar.activation(kcT[:, 0:2 * N_CMP], ps[6][:, 0:2 * N_CMP], ACT.Copy).then_inc(kc_ev, 1)
            nc.scalar.activation(vc[0:N_CMP, :], ps[7][0:N_CMP, 0:P], ACT.Copy).then_inc(kc_ev, 1)
            for tt in range(TT):
                act.wait_ge(kv_mm, l * 2 + (tt + 1))
                kv = ps[4 + tt][:, :].rearrange("p (h n) -> p h n", h=4)
                nc.scalar.activation(mk[:, tt, :, 0:HD], kv[:, :, 0:HD], ACT.Copy)
                nc.scalar.activation(mv2[:, tt, :, :], kv[:, :, HD:2 * HD], ACT.Copy).then_inc(kv_ev, 1)
            for tt in range(TT):
                act.wait_ge(cs_max, l * 2 + (tt + 1))
                s = cS[:, tt, :, 0:CN[tt]]
                nc.scalar.activation(s, s, ACT.Exp).then_inc(cs_exp, 1)
            for tt in range(TT):
                for j, dst in enumerate((mqT, mkT)):
                    act.wait_ge(mt_mm, l * 4 + (2 * tt + j + 1))
                    nc.scalar.activation(dst[0:96, :, tt * P:(tt + 1) * P],
                                         ps[2 * j + tt][0:96, :].rearrange("p (h q) -> p h q", h=4), ACT.Copy)\
                        .then_inc(mt_ev, 1)
            for tt in range(TT):
                for g in range(2):
                    act.wait_ge(ct_mm, l * 4 + (2 * tt + g + 1))
                    nc.scalar.activation(PcT[0:CN[tt], tt, 4 * g:4 * g + 4, :],
                                         ps[4 + 2 * tt + g][0:CN[tt], :].rearrange("p (h q) -> p h q", h=4),
                                         ACT.Copy).then_inc(ct_ev, 1)
            act_units(act, done_b + l * UNITS_B, mix_units)
            act.wait_ge(pv_mm, done_b + l * UNITS_B + len(mix_units))
            for b in range(4):
                nc.scalar.activation(oT[:, 2 * b:2 * b + 2, :], ps[b][:, :].rearrange("p (a n) -> p a n", a=2),
                                     ACT.Copy).then_inc(ob_ev, 1)
            for i in range(4):
                for b in range(3):
                    finished(act, 2, l, B_GATE + 4 * i + b)
                    if i:
                        act.wait_ge(br_used, l * 4 + i)
                    nc.scalar.activation(sig[:, b, :], ps[4 + b][:, :], ACT.Sigmoid).then_inc(sig_ready, 1)
            norm = 2 * LAYERS + 3 * l
            act_norm(act, norm)
            finished(act, 2, l, B_XQ)
            nc.scalar.activation(xq, ps[4][:, :].rearrange("p (a n) -> p a n", a=2), ACT.Copy,
                                 scale=HD ** -0.5).then_inc(x_ev, 1)
            finished(act, 2, l, B_XV)
            nc.scalar.activation(xk, ps[5][:, :].rearrange("p (a n) -> p a n", a=2), ACT.Copy).then_inc(x_ev, 1)
            nc.scalar.activation(xv, ps[6][:, :].rearrange("p (a n) -> p a n", a=2), ACT.Copy).then_inc(x_ev, 1)
            act_units(act, done_b + l * UNITS_B + len(mix_units), mem_units)
            act.wait_ge(pv_mm, done_b + (l + 1) * UNITS_B)
            for b in range(2):
                nc.scalar.activation(xo[:, b, :], ps[b][:, 0:SEQ], ACT.Copy).then_inc(xo_ev, 1)
            act_norm(act, norm + 1)
            act_pairs(act, 2, l, B_MLP, MLP_PAIRS, LAYERS * PAIRS + l * MLP_PAIRS, ACT.Relu)
            act_norm(act, norm + 2)

        def dve_block2(dve, l):
            step = Steps(dve, dve_step, LAYERS * DVE_A, DVE_B, l)
            arrived(dve, 2, l, B_SMALL)
            step.after(nc.vector.tensor_copy(smB, slot(B_SMALL)))
            dve.sem_inc(small_read, 1)
            dve.wait_ge(b_ev, l * 12 + 3)
            for g in range(2):
                for part in range(2):
                    src = kvc[:, g, 16 * part:16 * part + 16 * N_CMP].rearrange("p (n l) -> p l n", l=16)
                    pe_ = smB[:, B_PE + 16 * part:B_PE + 16 * part + 16].unsqueeze(2).to_broadcast([P, 16, N_CMP])
                    last = nc.vector.tensor_tensor(xb[:, 16 * part:16 * part + 16, g, 0:N_CMP], src, pe_, ALU.add)
            last.then_inc(xb_ready, 1)
            dve.wait_ge(b_ev, l * 12 + 12)
            step.after(nc.vector.tensor_tensor(sq, cqkv, cqkv, ALU.mult))
            nc.vector.tensor_reduce(rms[:, :, 0], sq[:, :, 0:384], AX.X, ALU.add)
            nc.vector.tensor_reduce(rms[:, :, 1], sq[:, :, 384:512], AX.X, ALU.add).then_inc(b_rms, 1)
            nc.vector.tensor_tensor(fy.rearrange("p (t h) -> p t h", t=TT), misc[:, :, 56:60],
                                    smB[:, B_BF:B_BF + 4].unsqueeze(1).to_broadcast([P, TT, 4]), ALU.add)\
                .then_inc(f_y, 1)
            dve.wait_ge(b_root, l + 1)
            step.after(nc.vector.reciprocal(rmr, rmr))
            for tt in range(TT):
                nc.vector.tensor_scalar(cqkv[:, tt, 0:384], cqkv[:, tt, 0:384], rmr[:, tt, 0:1], None, ALU.mult)
                last = nc.vector.tensor_scalar(cqkv[:, tt, 384:512], cqkv[:, tt, 384:512], rmr[:, tt, 1:2], None,
                                               ALU.mult)
            last.then_inc(b_scaled, 1)
            dve.wait_ge(f_log, l * 3 + 3)
            step.after(nc.vector.scalar_tensor_tensor(flf, fy, 0.0, fl, ALU.min, ALU.subtract))
            for tt in range(TT):
                last = nc.vector.tensor_copy(lfb[:, tt, :, :],
                                             flf[:, 4 * tt:4 * tt + 4].unsqueeze(2).to_broadcast([P, 4, P]))
            last.then_inc(f_ready, 1)
            for tt in range(TT):
                dve.wait_ge(c_mm, l * 2 + (tt + 1))
                nc.vector.tensor_tensor(cT[:, :, tt * P:(tt + 1) * P], ps[tt][:, :].rearrange("p (c q) -> p c q", c=4),
                                        smg.unsqueeze(2).to_broadcast([P, 4, P]), ALU.mult).then_inc(c_ev, 1)
            dve.wait_ge(f_mm, l + 1)
            nc.vector.tensor_copy(negcum.rearrange("p t h -> p (t h)"), ps[3][:, 0:8]).then_inc(f_cum, 1)
            for tt in range(TT):
                q = mq[:, tt, :, :]
                dve.wait_ge(q_mm, l * 2 + (tt + 1))
                raw = ps[2 + tt][:, 0:384].rearrange("p (h n) -> p h n", h=4)
                nc.vector.tensor_copy(q[:, :, 0:HD], raw[:, :, 0:HD])
                cos = rope[:, tt, 0, :].unsqueeze(1).to_broadcast([P, 4, 16])
                sin = rope[:, tt, 1, :].unsqueeze(1).to_broadcast([P, 4, 16])
                x1, x2 = raw[:, :, HD:HD + 16], raw[:, :, HD + 16:HD + 32]
                nc.vector.tensor_tensor(rt[:, 0, :, :], x1, cos, ALU.mult)
                nc.vector.tensor_tensor(rt[:, 1, :, :], x2, sin, ALU.mult)
                nc.vector.tensor_tensor(rt[:, 2, :, :], x1, sin, ALU.mult)
                nc.vector.tensor_tensor(rt[:, 3, :, :], x2, cos, ALU.mult)
                y1, y2 = misc[:, tt, 0:16], misc[:, tt, 16:32]
                c1, s1 = rope[:, tt, 0, :], rope[:, tt, 1, :]
                nc.vector.tensor_tensor(rt[:, 4, 0, :], y1, c1, ALU.mult)
                nc.vector.tensor_tensor(rt[:, 4, 1, :], y2, s1, ALU.mult)
                nc.vector.tensor_tensor(rt[:, 4, 2, :], y1, s1, ALU.mult)
                step.after(nc.vector.tensor_tensor(rt[:, 4, 3, :], y2, c1, ALU.mult))
                nc.vector.tensor_tensor(q[:, :, HD:HD + 16], rt[:, 0, :, :], rt[:, 1, :, :], ALU.subtract)
                nc.vector.tensor_tensor(q[:, :, HD + 16:HD + 32], rt[:, 2, :, :], rt[:, 3, :, :], ALU.add)
                nc.vector.tensor_tensor(rk[:, tt, 0:16], rt[:, 4, 0, :], rt[:, 4, 1, :], ALU.subtract)
                step.after(nc.vector.tensor_tensor(rk[:, tt, 16:32], rt[:, 4, 2, :], rt[:, 4, 3, :], ALU.add))
                dve.wait_ge(kv_ev, l * 2 + (tt + 1))
                nc.vector.tensor_copy(mk[:, tt, :, HD:96], rk[:, tt, :].unsqueeze(1).to_broadcast([P, 4, 32]))\
                    .then_inc(mla_ready, 1)
            for tt in range(TT):
                n = CN[tt]
                first = 31 if tt else 159
                s = cS[:, tt, :, 0:n]
                dve.wait_ge(cs_mm, l * 2 + 2)
                for odd in range(2):
                    raw = ps[6 + odd][:, 64 * tt:64 * tt + 64].rearrange("p (h n) -> p h n", h=4)
                    last = nc.vector.tensor_tensor(s[:, odd:8:2, :], raw[:, :, 0:n],
                                                   T[:, odd:8:2, first:first + 16 * (n - 1) + 1:16], ALU.add)
                step.after(last)
                step.after(nc.vector.tensor_reduce(cmax[:, tt, :], s, AX.X, ALU.max))
                nc.vector.tensor_tensor(s, s, cmax[:, tt, :].unsqueeze(2).to_broadcast([P, 8, n]), ALU.subtract)\
                    .then_inc(cs_max, 1)
            dve.wait_ge(g_sig, l + 1)
            for tt in range(TT):
                n = CN[tt]
                s = cS[:, tt, :, 0:n]
                dve.wait_ge(cs_exp, l * 2 + (tt + 1))
                step.after(nc.vector.tensor_reduce(csum[:, tt, :], s, AX.X, ALU.add))
                step.after(nc.vector.reciprocal(csum[:, tt, :], csum[:, tt, :]))
                step.after(nc.vector.tensor_tensor(csum[:, tt, :], csum[:, tt, :], gsig[:, tt, :, 0], ALU.mult))
                step.after(nc.vector.tensor_tensor(s, s, csum[:, tt, :].unsqueeze(2).to_broadcast([P, 8, n]), ALU.mult))
                nc.vector.tensor_tensor(s, s, cmpok[:, tt, 0:n].unsqueeze(1).to_broadcast([P, 8, n]), ALU.mult)\
                    .then_inc(cs_p, 1)
            dve_units(dve, step, done_b + l * UNITS_B, mix_units, plain_scale)
            for i in range(4):
                finished(dve, 2, l, B_GATE + 4 * i + 3)
                dve.wait_ge(sig_ready, l * 12 + 3 * (i + 1))
                for b in range(3):
                    last = nc.vector.tensor_tensor(prod[:, b, :], ps[b][:, :], sig[:, b, :], ALU.mult)
                step.after(last)
                step.after(nc.vector.tensor_tensor(prod[:, 0, :], prod[:, 0, :], prod[:, 1, :], ALU.add))
                nc.vector.tensor_tensor(merged[:, 2 * i:2 * i + 2, :].rearrange("p a n -> p (a n)"), prod[:, 0, :],
                                        prod[:, 2, :], ALU.add).then_inc(br_used, 1)
            norm = 2 * LAYERS + 3 * l
            dve_norm(dve, step, norm, 2, l, B_LN1)
            dve_units(dve, step, done_b + l * UNITS_B + len(mix_units), mem_units, plain_scale)
            dve_norm(dve, step, norm + 1, 2, l, B_LN2)

            def weigh(p, i):
                return nc.vector.tensor_tensor(w_sb[p % 2], act_sb[p % 2], act_sb[p % 2], ALU.mult)

            dve_pairs(dve, 2, l, B_MLP, MLP_PAIRS, LAYERS * PAIRS + l * MLP_PAIRS, weigh)
            dve_norm(dve, step, norm + 2, 2, l, B_LN3)
            step.close()

        all_norms = 2 * LAYERS + 3 * LAYERS
        block = ctx.enter_context(nc.Block())

        @block.sync
        def _(sp):
            sp.dma_start(x[:, :, :], x_in.rearrange("(t p) n -> p t n", p=P)).then_inc(loaded, 16)
            sp.dma_start(cs[:, :], consts[:, :]).then_inc(loaded, 16)
            sp.dma_start(tab[:, :], table[:, :]).then_inc(loaded, 16)
            for s in range(SLOTS):
                sp.dma_start(slot(s), stream[s, :, :]).then_inc(slot_full[s], 16)
            with sp.Fori(1, ALL_TILES // SLOTS) as g:
                for s in range(SLOTS):
                    sp.wait_ge(tile_done, 4 * g + (s - 3))
                    sp.dma_start(slot(s), stream[bass.ds(4 * g + s, 1), :, :].rearrange("o p n -> p (o n)"))\
                        .then_inc(slot_full[s], 16)
            sp.wait_ge(ln_x, all_norms * TT)
            sp.dma_start(out.rearrange("(t p) n -> p t n", p=P), x[:, :, :]).then_inc(stored, 16)
            sp.wait_ge(stored, 16)

        @block.gpsimd
        def _(pool):
            pool.wait_ge(t_ev, 1)
            pool.dma_start(scratch[:, :], bd[0:8, :]).then_inc(t_out, 16)
            pool.wait_ge(t_out, 16)
            band = bass.AP(tensor=scratch.tensor, offset=0, ap=[[1, P], [384, 8], [1, 256]])
            pool.dma_start(merged, band).then_inc(t_in, 16)

        @block.scalar
        def _(act):
            act_turn_x(act, 0)
            with act.Fori(0, LAYERS) as l:
                act_block1(act, l)
            act.wait_ge(t_mm, 1)
            nc.scalar.activation(bd[0:8, :], ps[0][0:8, 0:384], ACT.Copy).then_inc(t_ev, 1)
            with act.Fori(0, LAYERS) as l:
                act_block2(act, l)

        @block.vector
        def _(dve):
            dve.wait_ge(loaded, 48)
            with dve.Fori(0, LAYERS) as l:
                dve_block1(dve, l)
            dve.wait_ge(t_flip, 1)
            for b in range(4):
                last = nc.vector.tensor_tensor(T[:, 2 * b:2 * b + 2, :], ps[b][:, :].rearrange("p (h k) -> p h k", h=2),
                                               causal.unsqueeze(1).to_broadcast([P, 2, 256]), ALU.add)
            last.then_inc(t_ready, 1)
            dve.wait_ge(t_ready, 1)
            with dve.Fori(0, LAYERS) as l:
                dve_block2(dve, l)

        @block.tensor
        def _(pe):
            pe.wait_ge(loaded, 48)
            pe_turn_x(pe)
            with pe.Fori(0, LAYERS) as l:
                pe_block1(pe, l)
            nc.tensor.matmul(ps[0][0:8, 0:384], tab[:, :], cs[0:32, CONST["bucket"]], start=True,
                             stop=True).then_inc(t_mm, 1)
            pe.wait_ge(t_in, 16)
            for b in range(4):
                last = nc.tensor.matmul(ps[b][:, :], cs[:, CONST["flip"]],
                                        merged[:, 2 * b:2 * b + 2, :].rearrange("p a n -> p (a n)"), start=True,
                                        stop=True)
            last.then_inc(t_flip, 1)
            with pe.Fori(0, LAYERS) as l:
                pe_block2(pe, l)


def constants():
    c = np.zeros((P, CONST_COLS), np.float32)
    p = np.arange(P)[:, None]
    j = np.arange(256)[None, :]
    c[:, CONST["ident"]] = np.eye(P)
    c[:, CONST["flip"]] = np.eye(P)[::-1]
    c[:, CONST["tri"]] = p >= j[:, :P]
    c[:, CONST["ones"]] = 1.0
    c[:, CONST["iota"]] = j[:, :P]
    dist = P + p - j
    causal = np.where(dist >= 0, 0.0, NEG)
    c[:, CONST["causal"]] = causal
    for h in range(4):
        slope = np.float32(2.0 ** (-8.0 * (h + 1) / 4))
        c[:, CONST["alibi"].start + 256 * h:CONST["alibi"].start + 256 * (h + 1)] = \
            np.where(dist >= 0, -slope * dist.astype(np.float32), NEG)
    strict = p < j
    strict = np.concatenate([strict, strict[:, :P]], 1)
    c[:, CONST["strict"]] = np.where(strict, 0.0, NEG)
    c[:, CONST["negstrict"]] = -1.0 * strict
    c[:, CONST["cum"]] = -1.0 * (p <= j)
    inv = (10000.0 ** (-np.arange(16, dtype=np.float32) / 16)).astype(np.float32)
    rope = np.zeros((P, TT, 2, 16), np.float32)
    ok = np.zeros((P, TT, N_CMP), np.float32)
    for tt in range(TT):
        ang = (tt * P + p).astype(np.float32) * inv[None, :]
        rope[:, tt, 0], rope[:, tt, 1] = np.cos(ang), np.sin(ang)
        ok[:, tt] = tt * P + p >= 16 * np.arange(N_CMP)[None, :] + 31
    c[:, CONST["rope"]] = rope.reshape(P, -1)
    c[:, CONST["cmpok"]] = ok.reshape(P, -1)
    n = np.maximum(255 - np.arange(384), 0)
    f = np.float32
    large = 16 + (np.log(np.maximum(n, 1).astype(f) / f(16)) / f(math.log(8.0)) * f(16)).astype(np.int32)
    bucket = np.where(n < 16, n, np.minimum(large, 31))
    c[:32, CONST["bucket"]] = np.arange(32)[:, None] == bucket[None, :]
    c[:, CONST["eps"]] = [[1e-5, 1e-6, 0.0]]
    return c


def up_tiles(w):
    n = w.shape[1] // 256
    return w.reshape(KC, P, n, 256).transpose(2, 1, 0, 3).reshape(n, P, TILE)


def down_tiles(w):
    n = w.shape[0] // 256
    return w.reshape(n, 2, P, D).transpose(0, 2, 1, 3).reshape(n, P, TILE)


def paired(out, up, dn):
    n = len(up)
    out[0] = up[0]
    out[1:2 * n - 1:2] = up[1:]
    out[2:2 * n - 1:2] = dn[:-1]
    out[2 * n - 1] = dn[-1]


def norm_tile(g, b):
    return np.broadcast_to(np.concatenate([g, b])[None, :], (P, TILE))


def lay_out(v):
    s = np.zeros((ALL_TILES, P, TILE), np.float32)
    for l in range(LAYERS):
        t = s[l * A_TILES:(l + 1) * A_TILES]
        small = t[A_SMALL]
        small[:, 0:256] = np.concatenate([v[n][l] for n in ("lam_q1", "lam_k1", "lam_q2", "lam_k2")])[None, :]
        small[:, A_SUBG] = v["subln_g"][l]
        init = 0.8 - 0.6 * math.exp(-0.3 * l)
        small[:, A_LINI], small[:, A_LOUT] = init, 1.0 - init
        w = v["w_in"][l]
        dq, dk, dv, sq, sk, sv = (w[:, 512 * i:512 * (i + 1)] for i in range(6))
        t[A_PROJ:A_WO] = up_tiles(np.concatenate([dq, dk, sq, sk, dv, sv], 1))
        t[A_WO:A_LN1] = down_tiles(v["w_o"][l])
        t[A_LN1] = norm_tile(v["ln1_g"][l], v["ln1_b"][l])
        t[A_WQ:A_KEYS] = up_tiles(v["w_query"][l])
        t[A_KEYS] = v["sub_keys"][l].reshape(16, P, P).transpose(2, 0, 1).reshape(P, TILE)
        u = v["expert_u"][l].reshape(PAIRS, 256, KC, P).transpose(0, 3, 2, 1).reshape(PAIRS, P, TILE)
        paired(t[A_EXP:A_LN2], u, down_tiles(v["expert_v"][l]))
        t[A_LN2] = norm_tile(v["ln2_g"][l], v["ln2_b"][l])

        t = s[LAYERS * A_TILES + l * B_TILES:][:B_TILES]
        small = t[B_SMALL]
        small[:, B_UQ:B_UKV] = v["mla_w_uq_2"][l].reshape(3, P, 384).transpose(1, 0, 2).reshape(P, 1152)
        small[:, B_UKV:B_W2] = v["mla_w_ukv_2"][l]
        small[:, B_W2:B_PE] = v["cmp_w2_2"][l].transpose(1, 0, 2).reshape(P, 128)
        small[:, B_PE:B_PE + 32] = v["cmp_pe_2"][l].transpose(0, 2, 1).reshape(P, 32)
        small[:, B_QN:B_KVN] = v["mla_q_norm_2"][l].reshape(3, P).T
        small[:, B_KVN] = v["mla_kv_norm_2"][l]
        small[:, B_BF:B_BF + 4] = v["fox_b_f_2"][l][None, :]
        w = v["w_in_2"][l]
        sizes = (512, 128, 128, 128, 128, 128, 128, 24, 384, 128, 32, 256, 256, 256, 4)
        at = np.cumsum((0,) + sizes)
        nq, kc, vc, ks, vs, kw, vw, ng, cq, ckv, kr, fq, fk, fv, ff = (w[:, a:a + n] for a, n in zip(at, sizes))
        g0, g1 = slice(0, 64), slice(64, 128)
        t[B_PROJ:B_CMP] = up_tiles(np.concatenate(
            [nq, kc[:, g0], vc[:, g0], kc[:, g1], vc[:, g1], ks[:, g0], ks[:, g0], ks[:, g1], ks[:, g1],
             kw[:, g0], kw[:, g0], kw[:, g1], kw[:, g1], fq, fk, vs, vw, fv, cq, ckv, kr, ng, ff,
             np.zeros((D, 196), np.float32)], 1))
        w1 = v["cmp_w1_2"][l].reshape(2, 2, 16, HD, P)
        t[B_CMP:B_GATE] = w1.transpose(1, 0, 3, 2, 4).reshape(2, P, TILE)
        gate = up_tiles(v["w_gate_2"][l]).reshape(3, 4, P, TILE)
        a, b, c = v["w_br_nsa_2"][l], v["w_br_mla_2"][l], v["w_br_fox_2"][l]
        rows = [x[P * i:P * (i + 1)] for x, i in ((a, 0), (b, 0), (a, 1), (b, 1), (a, 2), (c, 0), (a, 3), (c, 1))]
        branch = up_tiles(np.concatenate(rows, 0))
        for i in range(4):
            t[B_GATE + 4 * i:B_GATE + 4 * i + 3] = gate[:, i]
            t[B_GATE + 4 * i + 3] = branch[i]
        t[B_MIX:B_LN1] = down_tiles(v["w_mix_out_2"][l])
        for n, k in enumerate((B_LN1, B_LN2, B_LN3)):
            t[k] = norm_tile(v["ln_g_2"][l, n], v["ln_b_2"][l, n])
        t[B_XQ] = up_tiles(v["xa_w_q_2"][l])[0]
        t[B_MEM] = up_tiles(np.ascontiguousarray(v["mem_2"][0].T))[0]
        t[B_XK:B_XO] = up_tiles(v["xa_w_kv_2"][l])
        t[B_XO] = down_tiles(v["xa_w_o_2"][l])[0]
        paired(t[B_MLP:B_LN3], up_tiles(v["mlp_w_up_2"][l]), down_tiles(v["mlp_w_down_2"][l]))
    return s


def kernel(**inputs):
    import concourse.bacc as bacc
    from concourse.bass_utils import run_bass_kernel_spmd

    v = {n: np.asarray(a) for n, a in inputs.items()}
    arrays = {
        "stream": lay_out(v),
        "x_in": np.ascontiguousarray(v["x"][0]),
        "consts": constants(),
        "table": np.ascontiguousarray(v["t5_table_2"]),
    }
    nc = bacc.Bacc("TRN2", target_bir_lowering=False, num_devices=1)
    aps = [nc.dram_tensor(n, a.shape, F32, kind="ExternalInput").ap() for n, a in arrays.items()]
    scratch = nc.dram_tensor("scratch", (8, 384), F32, kind="Internal").ap()
    out = nc.dram_tensor("out", (SEQ, D), F32, kind="ExternalOutput").ap()
    program(nc, *aps, scratch, out)
    r = run_bass_kernel_spmd(nc, [arrays], core_ids=[0])
    return np.asarray(r.results[0]["out"]).reshape(1, SEQ, D)
```

```python
import itertools
import math
from contextlib import ExitStack

import numpy as np
import concourse.bass as bass
from concourse import mybir

F32 = mybir.dt.float32
F32R = mybir.dt.float32r
U32 = mybir.dt.uint32
ALU = mybir.AluOpType
ACT = mybir.ActivationFunctionType
AX = mybir.AxisListType

P = 128
SEQ, D = 256, 1024
TT = SEQ // P
KC = D // P
LAYERS = 2
SLOTS = 4
TILE = 2048
NEG = -1e30
ALPHA = (2.0 * LAYERS) ** 0.25
HD = 64

A_SMALL = 0
A_PROJ = 1
A_WO = A_PROJ + 12
A_LN1 = A_WO + 4
A_KEYS = A_LN1 + 1
A_WQ = A_KEYS + 1
A_EXP = A_WQ + 8
N_EXPERTS = 16384
PAIRS = N_EXPERTS // 256
A_LN2 = A_EXP + 2 * PAIRS
A_TILES = A_LN2 + 1
A_TILES += -A_TILES % SLOTS

B_SMALL = 0
B_PROJ = 1
B_CMP = B_PROJ + 12
B_GATE = B_CMP + 2
B_MIX = B_GATE + 16
B_LN1 = B_MIX + 4
B_XQ = B_LN1 + 1
B_MEM = B_XQ + 1
B_XK = B_MEM + 1
B_XV = B_XK + 1
B_XO = B_XV + 1
B_LN2 = B_XO + 1
B_MLP = B_LN2 + 1
MLP_PAIRS = 16
B_LN3 = B_MLP + 2 * MLP_PAIRS
B_TILES = B_LN3 + 1
B_TILES += -B_TILES % SLOTS
ALL_TILES = LAYERS * (A_TILES + B_TILES)

CONST = {}
_at = 0
for _name, _n in [("ident", P), ("flip", P), ("tri", P), ("ones", P), ("iota", P), ("alibi", 4 * 256), ("causal", 256),
                  ("strict", 384), ("negstrict", 384), ("cum", 256), ("rope", 64), ("cmpok", 30), ("bucket", 384),
                  ("eps", 3)]:
    CONST[_name] = slice(_at, _at + _n)
    _at += _n
CONST_COLS = _at
N_CMP = 15

A_LAM, A_SUBG, A_LINI, A_LOUT = 0, 256, 257, 258
B_UQ, B_UKV, B_W2, B_PE, B_QN, B_KVN, B_BF = 0, 1152, 1664, 1792, 1856, 1859, 1860

UNITS_A = 8
NSA_U, MLA_U, FOX_U, XA_U = 16, 4, 4, 4
UNITS_B = NSA_U + MLA_U + FOX_U + XA_U


def rings(base, turn):
    return 16 * (base + turn + 1)


class Steps:

    def __init__(self, eng, sem, start, per_layer, layer):
        self.eng, self.sem, self.n = eng, sem, 0
        self.start, self.per_layer, self.layer = start, per_layer, layer

    def after(self, ins):
        self.n += 1
        ins.then_inc(self.sem, 1)
        self.eng.wait_ge(self.sem, self.layer * self.per_layer + (self.start + self.n))

    def close(self):
        assert self.n == self.per_layer, f"{self.n} steps"


DVE_A, DVE_B = 124, 115


def program(nc, stream, x_in, consts, table, scratch, out):
    ctx = ExitStack()
    with ctx:
        def sb(name, shape, dt=F32):
            return ctx.enter_context(nc.sbuf_tensor(name, shape, dt))

        def sem(name):
            return ctx.enter_context(nc.semaphore(name))

        ring = sb("ring", [P, SLOTS, TILE])
        x = sb("x", [P, TT, D])
        xT = sb("xT", [P, KC, SEQ])
        cs = sb("cs", [P, CONST_COLS])
        tab = sb("tab", [32, 8])
        arena_at = nc.sbuf_base
        arena = sb("arena", [P, SEQ * P])
        selT = sb("selT", [P, 3, SEQ])
        work = sb("work", [P, 4, 512])
        mv = sb("mv", [P, TT, 2])
        st = sb("st", [P, TT, 2, 6])
        std = sb("std", [P, TT])
        rstd = sb("rstd", [P, TT])
        spare = sb("spare", [P, 16])
        cells = itertools.count()
        ps = [ctx.enter_context(nc.psum_tensor(f"ps{i}", [P, 512], F32)) for i in range(8)]

        ident, tri, ones, iota = (cs[:, CONST[n]] for n in ("ident", "tri", "ones", "iota"))
        gates = arena[:, 0:SEQ * P // 2].rearrange("p (t i) -> p t i", i=P // 2)

        over = [arena_at + 4 * (SEQ * P // 2)]

        def part(name, *shape):
            t = nc.alloc_sbuf_tensor_at(name, [P, *shape], F32R, offset=over[0])
            over[0] += 4 * math.prod(shape)
            return t

        tile_h, tile_l = part("tile_h", 2, TILE), part("tile_l", 2, TILE)
        x_h, x_l = part("x_h", KC, SEQ), part("x_l", KC, SEQ)
        w_h, w_l = part("w_h", 2, 512), part("w_l", 2, 512)
        assert over[0] <= arena_at + 4 * (SEQ * P - 2048)

        at = [0]

        def room(n, start=None):
            if start is not None:
                at[0] = start
            at[0] += n
            assert at[0] <= SEQ * P
            return arena[:, at[0] - n:at[0]]

        def slot(k):
            return ring[:, k % SLOTS, :]

        def chunks(k):
            return slot(k).rearrange("p (c n) -> p c n", c=KC)

        slot_full = [sem(f"slot_full{s}") for s in range(SLOTS)]
        tile_done = sem("tile_done")
        small_read = sem("small_read")
        loaded = sem("loaded")
        ln_var, ln_std, ln_x = sem("ln_var"), sem("ln_std"), sem("ln_x")
        xt_mm, xt_ready = sem("xt_mm"), sem("xt_ready")
        dve_step = sem("dve_step")
        stored = sem("stored")

        PA, PB = A_TILES // SLOTS, B_TILES // SLOTS

        def arrived(eng, block, l, k, i=0):
            base = l * PA if block == 1 else l * PB + LAYERS * PA
            eng.wait_ge(slot_full[k % SLOTS], (base + i + (k // SLOTS + 1)) * 16)

        def finished(eng, block, l, k, i=0):
            base = l * A_TILES if block == 1 else l * B_TILES + LAYERS * A_TILES
            eng.wait_ge(tile_done, base + 4 * i + (k + 1))

        def up_features(w, src, bank):
            for fb in range(2):
                for c in range(KC):
                    last = nc.tensor.matmul(ps[bank][:, fb * SEQ:(fb + 1) * SEQ], w[:, c, fb * P:(fb + 1) * P],
                                            src[:, c, :], start=(c == 0), stop=(c == KC - 1))
            return last

        def up_tokens(w, src, bank, n=256):
            for tt in range(TT):
                for c in range(KC):
                    last = nc.tensor.matmul(ps[bank][:, tt * 256:tt * 256 + n], src[:, c, tt * P:(tt + 1) * P],
                                            w[:, c, 0:n], start=(c == 0), stop=(c == KC - 1))
            return last

        def down(w, lhs, first, last_tile):
            for j in range(2):
                for tt in range(TT):
                    for half in range(2):
                        last = nc.tensor.matmul(ps[2 * tt + half][:, :], lhs(j, tt),
                                                w[:, j * D + half * 512:j * D + half * 512 + 512],
                                                start=(first and j == 0), stop=(last_tile and j == 1))
            return last

        def pe_turn_x(pe, n=None, tiles=1):
            for tt in range(TT):
                if n is not None:
                    pe.wait_ge(ln_x, n * TT + (tt + 1))
                if n is not None and tt == TT - 1:
                    pe.sem_inc(tile_done, tiles)
                for g in range(2):
                    for j in range(4):
                        c = 4 * g + j
                        last = nc.tensor.transpose(ps[4 + 2 * tt + g][:, j * P:(j + 1) * P],
                                                   x[:, tt, c * P:(c + 1) * P], ident)
                    last.then_inc(xt_mm, 1)

        def act_turn_x(act, m):
            for tt in range(TT):
                for g in range(2):
                    act.wait_ge(xt_mm, m * 4 + (2 * tt + g + 1))
                    nc.scalar.activation(xT[:, 4 * g:4 * g + 4, tt * P:(tt + 1) * P],
                                         ps[4 + 2 * tt + g][:, :].rearrange("p (j n) -> p j n", j=4),
                                         ACT.Copy).then_inc(xt_ready, 1)

        def act_norm(act, n):
            act.wait_ge(ln_var, n + 1)
            nc.scalar.activation(std[:, :], mv[:, :, 1], ACT.Sqrt,
                                 bias=cs[:, CONST["eps"]][:, 0:1]).then_inc(ln_std, 1)
            act_turn_x(act, n + 1)

        def carry_wait():
            cell = next(cells) % 16
            nc.vector.memset(spare[:, cell:cell + 1], 0.0)

        def dve_norm(dve, step, n, block, l, k):
            finished(dve, block, l, k - 1)
            for tt in range(TT):
                for half in range(2):
                    h = x[:, tt, half * 512:(half + 1) * 512]
                    last = nc.vector.scalar_tensor_tensor(h, h, ALPHA, ps[2 * tt + half][:, :], ALU.mult, ALU.add)
            step.after(last)
            for tt in range(TT):
                for half in range(2):
                    last = nc.vector.bn_stats(st[:, tt, half, :], x[:, tt, half * 512:(half + 1) * 512])
            step.after(last)
            carry_wait()
            for tt in range(TT):
                last = nc.vector.bn_aggr(mv[:, tt, :], st[:, tt, :, :])
            last.then_inc(ln_var, 1)
            dve.wait_ge(ln_std, n + 1)
            step.after(nc.vector.reciprocal(rstd[:, :], std[:, :]))
            for tt in range(TT):
                last = nc.vector.tensor_scalar(x[:, tt, :], x[:, tt, :], mv[:, tt, 0:1], rstd[:, tt:tt + 1],
                                               ALU.subtract, ALU.mult)
            step.after(last)
            arrived(dve, block, l, k)
            for tt in range(TT):
                last = nc.vector.tensor_tensor(x[:, tt, :], x[:, tt, :], slot(k)[:, 0:D], ALU.mult)
            step.after(last)
            for tt in range(TT):
                last = nc.vector.tensor_tensor(x[:, tt, :], x[:, tt, :], slot(k)[:, D:2 * D], ALU.add)
                last.then_inc(ln_x, 1)

        sc_first = sem("sc_first")
        sc_mm, sm_max, sm_exp, sm_p = sem("sc_mm"), sem("sm_max"), sem("sm_exp"), sem("sm_p")
        pt_mm, pt_ev, pv_mm = sem("pt_mm"), sem("pt_ev"), sem("pv_mm")

        def pe_units(pe, base, units, scores, values):
            def score(u):
                if u >= 2:
                    pe.wait_ge(sm_max, base + (u - 1))
                for m in range(2):
                    klen = units[u]["keys"]
                    last = scores(units[u], m, ps[4 + u % 2][:, m * 256:m * 256 + klen])
                    if m == 0:
                        last.then_inc(sc_first, 1)
                        pe.wait_ge(sc_first, base + (u + 1))
                last.then_inc(sc_mm, 1)

            def turn(u):
                pe.wait_ge(sm_p, base + (u + 1))
                if u >= 2:
                    pe.wait_ge(pt_ev, base + (u - 1))
                for m in range(units[u]["turned"]):
                    for kt in range(units[u]["keys"] // P):
                        last = nc.tensor.transpose(ps[6 + u % 2][:, (2 * m + kt) * P:(2 * m + kt + 1) * P],
                                                   E[:, u % 2, m, kt * P:(kt + 1) * P], ident)
                last.then_inc(pt_mm, 1)

            score(0)
            score(1)
            for u in range(len(units)):
                turn(u)
                if u + 2 < len(units):
                    score(u + 2)
                pe.wait_ge(pt_ev, base + (u + 1))
                for m in range(2):
                    last = values(units[u], m, PT[:, u % 2, m, :, :])
                last.then_inc(pv_mm, 1)

        def act_units(act, base, units):
            def exps(u):
                act.wait_ge(sm_max, base + (u + 1))
                if u >= 2:
                    act.wait_ge(pt_mm, base + (u - 1))
                klen = units[u]["keys"]
                for m in range(2):
                    last = nc.scalar.activation(E[:, u % 2, m, 0:klen], S[:, u % 2, m, 0:klen], ACT.Exp,
                                                bias=negmax[:, u % 2, m:m + 1], accum_out=total[:, u % 2, m:m + 1])
                last.then_inc(sm_exp, 1)

            exps(0)
            for u in range(len(units)):
                if u + 1 < len(units):
                    exps(u + 1)
                act.wait_ge(pt_mm, base + (u + 1))
                if u >= 2:
                    act.wait_ge(pv_mm, base + (u - 1))
                n, maps = units[u]["keys"] // P, units[u]["turned"]
                nc.scalar.activation(PT[:, u % 2, 0:maps, 0:n, :],
                                     ps[6 + u % 2][:, :].rearrange("p (m k q) -> p m k q", m=2, k=2)[:, 0:maps, 0:n, :],
                                     ACT.Copy).then_inc(pt_ev, 1)

        def dve_units(dve, step, base, units, scale_probs):
            def bias(u):
                w = units[u]
                klen = w["keys"]
                dve.wait_ge(sc_mm, base + (u + 1))
                if u >= 2:
                    dve.wait_ge(sm_exp, base + (u - 1))
                raw = ps[4 + u % 2][:, :].rearrange("p (m k) -> p m k", m=2)[:, :, 0:klen]
                s = S[:, u % 2, :, 0:klen]
                if w["table"] is None:
                    last = nc.vector.tensor_copy(s, raw)
                elif w["minus"] is None:
                    for m in range(2):
                        last = nc.vector.scalar_tensor_tensor(s[:, m, :], raw[:, m, :], w["scale"], w["table"][m],
                                                              ALU.mult, ALU.add)
                else:
                    for m in range(2):
                        last = nc.vector.scalar_tensor_tensor(s[:, m, :], raw[:, m, :], w["minus"][m], w["table"][m],
                                                              ALU.subtract, ALU.add)
                step.after(last)
                nc.vector.tensor_reduce(negmax[:, u % 2, :], s, AX.X, ALU.max, negate=True).then_inc(sm_max, 1)

            bias(0)
            for u in range(len(units)):
                if u + 1 < len(units):
                    bias(u + 1)
                dve.wait_ge(sm_exp, base + (u + 1))
                step.after(nc.vector.reciprocal(rsum[:, u % 2, :], total[:, u % 2, :]))
                scale_probs(units[u], u, step).then_inc(sm_p, 1)

        def plain_scale(unit, u, step):
            klen = unit["keys"]
            if unit["gate"] is not None:
                step.after(nc.vector.tensor_tensor(rsum[:, u % 2, :], rsum[:, u % 2, :], unit["gate"], ALU.mult))
            for m in range(2):
                e = E[:, u % 2, m, 0:klen]
                last = nc.vector.tensor_scalar(e, e, rsum[:, u % 2, m:m + 1], None, ALU.mult)
            return last

        negmax, total, rsum = sb("negmax", [P, 2, 2]), sb("total", [P, 2, 2]), sb("rsum", [P, 2, 2])

        qk = room(16 * SEQ, 0).rearrange("p (b n) -> p b n", b=16)
        vt = room(TT * 1024).rearrange("p (t n) -> p t n", t=TT)
        S = room(1024).rearrange("p (u m k) -> p u m k", u=2, m=2)
        E = room(1024).rearrange("p (u m k) -> p u m k", u=2, m=2)
        PT = room(1024).rearrange("p (u m k q) -> p u m k q", u=2, m=2, k=2)
        shared_top = at[0]
        mixT = room(8 * SEQ).rearrange("p (b n) -> p b n", b=8)
        O = room(TT * 512).rearrange("p (t n) -> p t n", t=TT)
        Osq = room(TT * 512).rearrange("p (t n) -> p t n", t=TT)
        sb_e, sb_l, sb_sp, sb_z, sb_f, sb_w = (room(768).rearrange("p (u n) -> p u n", u=2) for _ in range(6))
        smA = room(512)
        lam2, lamp, ms, rs = room(128), room(2), room(8), room(8)
        neglam = room(1)
        elam = room(2)
        q2 = room(16 * SEQ, 0).rearrange("p (b n) -> p b n", b=16)
        sc = room(TT * 16 * P).rearrange("p (t h n) -> p t h n", t=TT, h=16)
        sc2 = room(4 * P).rearrange("p (h n) -> p h n", h=4)
        top = room(TT * 256).rearrange("p (t h n) -> p t h n", t=TT, h=16)
        topi = room(TT * 256).bitcast(U32).rearrange("p (t h n) -> p t h n", t=TT, h=16)
        topf = room(TT * 256).rearrange("p (t h n) -> p t h n", t=TT, h=16)
        cand = room(TT * 256).rearrange("p (t n) -> p t n", t=TT)
        cand2 = room(TT * 256).rearrange("p (t n) -> p t n", t=TT)
        best = room(TT * P).rearrange("p (t h n) -> p t h n", t=TT, h=8)
        pos = room(TT * P).bitcast(U32).rearrange("p (t h n) -> p t h n", t=TT, h=8)
        half_u = room(2 * P).bitcast(U32).rearrange("p (s h n) -> p s h n", s=2, h=8)
        half_f = room(2 * P).rearrange("p (s h n) -> p s h n", s=2, h=8)
        hot = room(8 * 256).rearrange("p (h n a) -> p h n a", h=8, a=16)
        chosen = room(TT * 3 * P).rearrange("p (t s k) -> p t s k", t=TT, s=3)
        gexp = room(TT * P).rearrange("p (t h n) -> p t h n", t=TT, h=8)
        gsum = room(8)
        keys = room(TILE, 28672 - TILE)

        proj_ev = sem("proj_ev")
        lam_sum, lam_exp = sem("lam_sum"), sem("lam_exp")
        o_copied, ms_ready, ms_root, o_scaled, ot_mm, mix_ready = (
            sem(n) for n in ("o_copied", "ms_ready", "ms_root", "o_scaled", "ot_mm", "mix_ready"))
        z_mm, z_log, z_fail, z_sum, z_exp_in, z_w, z_pv, z_out = (
            sem(n) for n in ("z_mm", "z_log", "z_fail", "z_sum", "z_exp_in", "z_w", "z_pv", "z_out"))
        z_abs, z_exp = sem("z_abs"), sem("z_exp")
        keys_ready, wq_ev, key_mm, key_ev = sem("keys_ready"), sem("wq_ev"), sem("key_mm"), sem("key_ev")
        g_diff, g_exp, chosen_ready, sel_mm, sel_ev = (
            sem(n) for n in ("g_diff", "g_exp", "chosen_ready", "sel_mm", "sel_ev"))
        hot_ready, hot_mm, gate_ev = sem("hot_ready"), sem("hot_mm"), sem("gate_ev")
        u_act, u_prod, u_w = sem("u_act"), sem("u_prod"), sem("u_w")
        hi_ready, lo_ready, xh_ready, xl_ready = sem("hi_ready"), sem("lo_ready"), sem("xh_ready"), sem("xl_ready")
        hot_rows = sem("hot_rows")
        hotb_ready, apart_ready, square_ready = sem("hotb_ready"), sem("apart_ready"), sem("square_ready")

        alibi = cs[:, CONST["alibi"]].rearrange("p (h k) -> p h k", h=4)
        diff_units = []
        for qt in range(TT):
            for h in range(4):
                off = 0 if qt else P
                t = alibi[:, h, off:256]
                diff_units.append(dict(keys=P * (qt + 1), qt=qt, h=h, table=[t, t], scale=1.0, minus=None, gate=None,
                                       turned=1))

        def diff_scores(w, m, out):
            part = slice(64 * m, 64 * m + 64)
            return nc.tensor.matmul(out, qk[part, w["h"], w["qt"] * P:(w["qt"] + 1) * P],
                                    qk[part, 4 + w["h"], 0:w["keys"]], start=True, stop=True)

        def diff_values(w, m, pt):
            if m:
                return diff_values.last
            n = w["keys"] // P
            for kt in range(n):
                diff_values.last = nc.tensor.matmul(ps[w["qt"]][:, w["h"] * P:(w["h"] + 1) * P], pt[:, kt, :],
                                                    vt[:, kt, w["h"] * P:(w["h"] + 1) * P],
                                                    start=(kt == 0), stop=(kt == n - 1))
            return diff_values.last

        def diff_scale(unit, u, step):
            klen = unit["keys"]
            e = E[:, u % 2, :, 0:klen]
            nc.vector.tensor_scalar(e[:, 0, :], e[:, 0, :], rsum[:, u % 2, 0:1], None, ALU.mult)
            step.after(nc.vector.tensor_tensor(rsum[:, u % 2, 1:2], rsum[:, u % 2, 1:2], neglam, ALU.mult))
            return nc.vector.scalar_tensor_tensor(e[:, 0, :], e[:, 1, :], rsum[:, u % 2, 1:2], e[:, 0, :],
                                                  ALU.mult, ALU.add)


        act_sb = [work[:, 0, :], work[:, 1, :]]

        def pair_chunks(t, m):
            return t[:, m % 2, :].rearrange("p (c n) -> p c n", c=KC)

        def pe_pairs(pe, block, l, k, pairs, done, turn, first, last):
            def split(m, i):
                pe.wait_ge(lo_ready, 4 * done + 8 * i + (2 * m + 2))

            def up(p, m, i, guard=True):
                split(m, i)
                if guard:
                    pe.wait_ge(u_act, done + 2 * i + (p - 1))
                uh, ul = pair_chunks(tile_h, m), pair_chunks(tile_l, m)
                for fb in range(2):
                    out = ps[4 + p % 2][:, fb * SEQ:(fb + 1) * SEQ]
                    f = slice(fb * P, (fb + 1) * P)
                    for c in range(KC):
                        nc.tensor.matmul(out, uh[:, c, f], x_h[:, c, :], start=(c == 0), stop=False)
                        nc.tensor.matmul(out, uh[:, c, f], x_l[:, c, :], start=False, stop=False)
                        ins = nc.tensor.matmul(out, ul[:, c, f], x_h[:, c, :], start=False, stop=(c == KC - 1))
                ins.then_inc(tile_done, 1)

            def add(p, m, i, opens=False, closes=False):
                split(m, i)
                pe.wait_ge(u_w, done + 2 * i + (p + 1))
                for j in range(2):
                    for tt in range(TT):
                        t = slice(j * SEQ + tt * P, j * SEQ + (tt + 1) * P)
                        wh, wl = w_h[:, p % 2, t], w_l[:, p % 2, t]
                        for half in range(2):
                            out = ps[2 * tt + half][:, :]
                            n = slice(j * D + half * 512, j * D + half * 512 + 512)
                            vh, vl = tile_h[:, m % 2, n], tile_l[:, m % 2, n]
                            nc.tensor.matmul(out, wh, vh, start=(opens and j == 0), stop=False)
                            nc.tensor.matmul(out, wh, vl, start=False, stop=False)
                            ins = nc.tensor.matmul(out, wl, vh, start=False, stop=(closes and j == 1))
                ins.then_inc(tile_done, 1)

            up(0, 0, 0, False)
            up(1, 1, 0, False)
            add(0, 2, 0, opens=first)
            up(2, 3, 0)
            add(1, 4, 0)
            n = (pairs - 2) // 2
            with pe.Fori(1, n) as i:
                up(1, 1, i)
                add(0, 2, i)
                up(2, 3, i)
                add(1, 4, i)
            up(1, 1, n)
            add(0, 2, n)
            add(1, 3, n, closes=last)

        def act_pairs(act, block, l, k, pairs, done, turn, func):
            def high(m, i, guard=True):
                arrived(act, block, l, k + m, i + turn)
                if guard:
                    finished(act, block, l, k + m - 2, i + turn)
                for hf in range(2):
                    n = slice(1024 * hf, 1024 * hf + 1024)
                    nc.scalar.activation(tile_h[:, m % 2, n], slot(k + m)[:, n], ACT.Copy).then_inc(hi_ready, 1)

            def apply(p, m, i, guard=True):
                finished(act, block, l, k + m, i + turn)
                if guard:
                    act.wait_ge(u_w, done + 2 * i + (p - 1))
                nc.scalar.activation(act_sb[p % 2], ps[4 + p % 2][:, :], func).then_inc(u_act, 1)

            high(0, 0, False)
            high(1, 0, False)
            apply(0, 0, 0, False)
            high(2, 0)
            high(3, 0)
            apply(1, 1, 0, False)
            with act.Fori(0, (pairs - 2) // 2) as i:
                high(4, i)
                high(5, i)
                apply(2, 3, i)
                high(6, i)
                high(7, i)
                apply(3, 5, i)

        def dve_pairs(dve, block, l, k, pairs, done, turn, factor):
            def low(m, i):
                for hf in range(2):
                    n = slice(1024 * hf, 1024 * hf + 1024)
                    dve.wait_ge(hi_ready, 4 * done + 8 * i + (2 * m + hf + 1))
                    nc.vector.tensor_tensor(tile_l[:, m % 2, n], slot(k + m)[:, n], tile_h[:, m % 2, n].bitcast(F32),
                                            ALU.subtract).then_inc(lo_ready, 1)

            def weigh(p, m, i, guard=True):
                dve.wait_ge(u_act, done + 2 * i + (p + 1))
                if guard:
                    finished(dve, block, l, k + m, i + turn)
                a = act_sb[p % 2].rearrange("p (b t) -> p b t", b=2)
                f = factor(p, i)
                hi = w_h[:, p % 2, :]
                nc.vector.tensor_tensor(hi.rearrange("p (b t) -> p b t", b=2), a, f, ALU.mult)
                nc.vector.tensor_tensor(a, a, f, ALU.mult).then_inc(u_prod, 1)
                dve.wait_ge(u_prod, done + 2 * i + (p + 1))
                nc.vector.tensor_tensor(w_l[:, p % 2, :], act_sb[p % 2], hi.bitcast(F32), ALU.subtract)\
                    .then_inc(u_w, 1)

            low(0, 0)
            low(1, 0)
            weigh(0, None, 0, False)
            low(2, 0)
            low(3, 0)
            weigh(1, None, 0, False)
            with dve.Fori(0, (pairs - 2) // 2) as i:
                low(4, i)
                low(5, i)
                weigh(2, 2, i)
                low(6, i)
                low(7, i)
                weigh(3, 4, i)

        def act_split_x(act, n):
            nc.scalar.activation(x_h[:, :, :], xT[:, :, :], ACT.Copy).then_inc(xh_ready, 1)

        def dve_split_x(dve, n):
            dve.wait_ge(xh_ready, n + 1)
            nc.vector.tensor_tensor(x_l[:, :, :], xT[:, :, :], x_h[:, :, :].bitcast(F32), ALU.subtract)\
                .then_inc(xl_ready, 1)

        HALF = P // 2
        hot_a = work[:, 0:2, :].rearrange("p s (t i) -> p s t i", t=8)
        hot_b = arena[:, SEQ * P - 2048:].rearrange("p (s t i) -> p s t i", s=2, t=8)
        BY_DVE = 5
        apart = work[:, 2:4, 0:(8 - BY_DVE) * P].rearrange("p s (t i) -> p s t i", i=P)
        GROUPS = SEQ // 8

        def pe_block1(pe, l):
            pe.wait_ge(small_read, l + 1)
            pe.sem_inc(tile_done, 1)
            pe.wait_ge(xt_ready, l * 8 + 4)
            for j in range(12):
                k = A_PROJ + j
                arrived(pe, 1, l, k)
                if j >= 4:
                    pe.wait_ge(proj_ev, l * 12 + (j - 3))
                (up_features if j < 8 else up_tokens)(chunks(k), xT, 4 + j % 4).then_inc(tile_done, 1)
            pe.wait_ge(proj_ev, l * 12 + 12)
            pe_units(pe, l * UNITS_A, diff_units, diff_scores, diff_values)
            pe.wait_ge(pt_ev, l * UNITS_A + UNITS_A)

            def sb_scores(h):
                part = slice(64 * (h % 2), 64 * (h % 2) + 64)
                q, kk = 8 + h // 2, 12 + h // 2
                if h >= 2:
                    pe.wait_ge(z_fail, l * 8 + (h - 1))
                nc.tensor.matmul(ps[4 + h % 2][:, 0:SEQ], qk[part, kk, 0:P], qk[part, q, :], start=True, stop=True)
                nc.tensor.matmul(ps[4 + h % 2][:, SEQ:SEQ + P], qk[part, kk, P:SEQ], qk[part, q, P:SEQ],
                                 start=True, stop=True).then_inc(z_mm, 1)

            sb_scores(0)
            for h in range(8):
                if h + 1 < 8:
                    sb_scores(h + 1)
                pe.wait_ge(z_fail, l * 8 + (h + 1))
                if h:
                    pe.wait_ge(z_exp_in, l * 8 + h)
                f = sb_f[:, h % 2, :]
                nc.tensor.matmul(ps[6][:, 0:SEQ], tri, f[:, 0:SEQ], start=True, stop=False)
                nc.tensor.matmul(ps[6][:, P:SEQ], ones, f[:, SEQ:SEQ + P], start=False, stop=True)
                nc.tensor.matmul(ps[6][:, SEQ:SEQ + P], tri, f[:, SEQ:SEQ + P], start=True,
                                 stop=True).then_inc(z_sum, 1)
                pe.wait_ge(z_w, l * 8 + (h + 1))
                bank = 7 if h // 2 % 2 == 0 else 2
                part = slice(64 * (h % 2), 64 * (h % 2) + 64)
                if h % 2 == 0 and h >= 4:
                    pe.wait_ge(z_out, l * 4 + (h // 2 - 1))
                v = slice(512 + 64 * h, 512 + 64 * h + 64)
                w = sb_w[:, h % 2, :]
                nc.tensor.matmul(ps[bank][part, 0:SEQ], vt[:, 0, v], w[:, 0:SEQ], start=True, stop=False)
                nc.tensor.matmul(ps[bank][part, P:SEQ], vt[:, 1, v], w[:, SEQ:SEQ + P], start=False,
                                 stop=True).then_inc(z_pv, 1)
            for tt in range(TT):
                pe.wait_ge(o_scaled, l * TT + (tt + 1))
                for h in range(4):
                    last = nc.tensor.transpose(ps[4 + tt][:, h * P:(h + 1) * P], O[:, tt, h * P:(h + 1) * P], ident)
                last.then_inc(ot_mm, 1)
            pe.wait_ge(mix_ready, l * TT + TT)
            pe.wait_ge(z_out, l * 4 + 4)
            for j in range(4):
                arrived(pe, 1, l, A_WO + j)
                down(slot(A_WO + j), lambda i, tt: mixT[:, 2 * j + i, tt * P:(tt + 1) * P], j == 0,
                     j == 3).then_inc(tile_done, 1)
            pe_turn_x(pe, l * 2)
            pe.wait_ge(xt_ready, l * 8 + 8)
            pe.wait_ge(keys_ready, l + 1)
            pe.sem_inc(tile_done, 1)

            def key_scores(h):
                pe.wait_ge(wq_ev, l * 8 + (h + 1))
                if h >= 2:
                    pe.wait_ge(key_ev, l * 8 + (h - 1))
                for tt in range(TT):
                    for s in range(2):
                        hp = 2 * h + s
                        last = nc.tensor.matmul(ps[6 + h % 2][:, (2 * tt + s) * P:(2 * tt + s + 1) * P],
                                                q2[:, hp, tt * P:(tt + 1) * P], keys[:, hp * P:(hp + 1) * P],
                                                start=True, stop=True)
                last.then_inc(key_mm, 1)

            for h in range(8):
                arrived(pe, 1, l, A_WQ + h)
                if h >= 2:
                    pe.wait_ge(wq_ev, l * 8 + (h - 1))
                up_features(chunks(A_WQ + h), xT, 4 + h % 2).then_inc(tile_done, 1)
                if h:
                    key_scores(h - 1)
            key_scores(7)
            for tt in range(TT):
                pe.wait_ge(chosen_ready, l * TT + (tt + 1))
                for s in range(3):
                    last = nc.tensor.transpose(ps[tt][:, s * P:(s + 1) * P], chosen[:, tt, s, :], ident)
                last.then_inc(sel_mm, 1)
            pe.wait_ge(key_ev, l * 8 + 8)

            for half in range(2):
                base = l * (2 * GROUPS) + half * GROUPS

                def gate_rows(i, b, guard):
                    pe.wait_ge(hot_ready, base + 2 * i + (b + 1))
                    pe.wait_ge(hotb_ready, base + 2 * i + (b + 1))
                    if guard:
                        pe.wait_ge(gate_ev, base + 2 * i + (b - 1))
                    for t in range(8):
                        last = nc.tensor.matmul(ps[6 + b][:, t * HALF:(t + 1) * HALF], hot_b[:, b, t, :],
                                                hot_a[:, b, t, :], start=True, stop=True)
                    last.then_inc(hot_mm, 1)

                gate_rows(0, 0, False)
                gate_rows(0, 1, False)
                with pe.Fori(1, GROUPS // 2) as i:
                    gate_rows(i, 0, True)
                    gate_rows(i, 1, True)
                pe.wait_ge(gate_ev, base + GROUPS)
                if half == 0:
                    pe.wait_ge(xl_ready, l + 1)
                pe_pairs(pe, 1, l, A_EXP, PAIRS // 2, l * PAIRS + half * PAIRS // 2, half * PAIRS // 4, half == 0,
                         half == 1)
            pe_turn_x(pe, l * 2 + 1)

        def act_block1(act, l):
            act.wait_ge(lam_sum, l + 1)
            nc.scalar.activation(elam, lamp, ACT.Exp).then_inc(lam_exp, 1)
            for j in range(12):
                k = A_PROJ + j
                finished(act, 1, l, k)
                src = ps[4 + j % 4][:, :].rearrange("p (a n) -> p a n", a=2)
                if j < 8:
                    scale = HD ** -0.5 if j in (0, 1, 4, 5) else 1.0
                    nc.scalar.activation(qk[:, 2 * j:2 * j + 2, :], src, ACT.Copy, scale=scale).then_inc(proj_ev, 1)
                else:
                    c = (j - 8) * 256
                    nc.scalar.activation(vt[:, :, c:c + 256], src, ACT.Copy).then_inc(proj_ev, 1)
            act_units(act, l * UNITS_A, diff_units)
            act.wait_ge(pv_mm, l * UNITS_A + UNITS_A)
            for tt in range(TT):
                nc.scalar.activation(O[:, tt, :], ps[tt][:, :], ACT.Copy).then_inc(o_copied, 1)
            for h in range(8):
                u = h % 2
                act.wait_ge(z_mm, l * 8 + (h + 1))
                if h >= 2:
                    act.wait_ge(z_fail, l * 8 + (h - 1))
                nc.scalar.activation(sb_e[:, u, :], ps[4 + u][:, 0:384], ACT.Abs).then_inc(z_abs, 1)
                act.wait_ge(z_abs, l * 16 + (2 * h + 1))
                nc.scalar.activation(sb_e[:, u, :], sb_e[:, u, :], ACT.Exp, scale=-1.0).then_inc(z_abs, 1)
                act.wait_ge(z_abs, l * 16 + (2 * h + 2))
                nc.scalar.activation(sb_l[:, u, :], sb_e[:, u, :], ACT.Ln, bias=1.0).then_inc(z_log, 1)
                act.wait_ge(z_exp_in, l * 8 + (h + 1))
                if h >= 2:
                    act.wait_ge(z_pv, l * 8 + (h - 1))
                nc.scalar.activation(sb_w[:, u, :], sb_z[:, u, :], ACT.Exp).then_inc(z_w, 1)
                if h % 2:
                    act.wait_ge(z_pv, l * 8 + (h + 1))
                    bank = 7 if h // 2 % 2 == 0 else 2
                    nc.scalar.activation(mixT[:, 4 + h // 2, :], ps[bank][:, 0:SEQ], ACT.Copy).then_inc(z_out, 1)
            act.wait_ge(ms_ready, l + 1)
            nc.scalar.activation(rs, ms, ACT.Sqrt, scale=1.0 / P, bias=cs[:, CONST["eps"]][:, 0:1]).then_inc(ms_root, 1)
            for tt in range(TT):
                act.wait_ge(ot_mm, l * TT + (tt + 1))
                nc.scalar.activation(mixT[:, 0:4, tt * P:(tt + 1) * P],
                                     ps[4 + tt][:, :].rearrange("p (h q) -> p h q", h=4), ACT.Copy,
                                     scale=smA[:, A_SUBG - 256:A_SUBG - 255]).then_inc(mix_ready, 1)
            arrived(act, 1, l, A_KEYS)
            nc.scalar.activation(keys, slot(A_KEYS), ACT.Copy).then_inc(keys_ready, 1)
            act_norm(act, l * 2)

            def queries_out(h):
                finished(act, 1, l, A_WQ + h)
                nc.scalar.activation(q2[:, 2 * h:2 * h + 2, :], ps[4 + h % 2][:, :].rearrange("p (a n) -> p a n", a=2),
                                     ACT.Copy).then_inc(wq_ev, 1)

            queries_out(0)
            for h in range(8):
                if h < 7:
                    queries_out(h + 1)
                act.wait_ge(key_mm, l * 8 + (h + 1))
                nc.scalar.activation(sc[:, :, 2 * h:2 * h + 2, :],
                                     ps[6 + h % 2][:, :].rearrange("p (t s n) -> p t s n", t=TT, s=2),
                                     ACT.Copy).then_inc(key_ev, 1)
            for tt in range(TT):
                act.wait_ge(g_diff, l * TT + (tt + 1))
                nc.scalar.activation(gexp[:, tt, :, :], gexp[:, tt, :, :], ACT.Exp).then_inc(g_exp, 1)
            for tt in range(TT):
                act.wait_ge(sel_mm, l * TT + (tt + 1))
                nc.scalar.activation(selT[:, :, tt * P:(tt + 1) * P],
                                     ps[tt][:, 0:3 * P].rearrange("p (s t) -> p s t", s=3), ACT.Copy).then_inc(sel_ev, 1)
            act_split_x(act, l)
            for half in range(2):
                base = l * (2 * GROUPS) + half * GROUPS

                def columns(i, b, guard):
                    act.wait_ge(square_ready, base + 2 * i + (b + 1))
                    if guard:
                        act.wait_ge(hot_mm, base + 2 * i + (b - 1))
                    nc.scalar.activation(hot_b[:, b, BY_DVE:8, :], apart[:, b, :, :], ACT.Relu, scale=-1.0, bias=1.0)\
                        .then_inc(hotb_ready, 1)

                def gate_out(i, b):
                    act.wait_ge(hot_mm, base + 2 * i + (b + 1))
                    nc.scalar.activation(arena[:, bass.ds(i * 1024 + b * 512, 512)], ps[6 + b][:, :],
                                         ACT.Copy).then_inc(gate_ev, 1)

                columns(0, 0, False)
                columns(0, 1, False)
                with act.Fori(0, GROUPS // 2 - 1) as i:
                    for b in range(2):
                        gate_out(i, b)
                        columns(i + 1, b, True)
                for b in range(2):
                    gate_out(GROUPS // 2 - 1, b)
                act_pairs(act, 1, l, A_EXP, PAIRS // 2, l * PAIRS + half * PAIRS // 2, half * PAIRS // 4, ACT.Gelu)
            act_norm(act, l * 2 + 1)

        def dve_block1(dve, l):
            step = Steps(dve, dve_step, 0, DVE_A, l)
            arrived(dve, 1, l, A_SMALL)
            small = slot(A_SMALL)
            lq = small[:, 0:256].rearrange("p (a b n) -> p a b n", a=2, b=2)
            nc.vector.tensor_copy(smA[:, 0:4], small[:, A_SUBG:A_SUBG + 4])
            step.after(nc.vector.tensor_tensor(lam2.rearrange("p (a n) -> p a n", a=2), lq[:, :, 0, :], lq[:, :, 1, :],
                                               ALU.mult))
            dve.sem_inc(small_read, 1)
            nc.vector.tensor_reduce(lamp, lam2.rearrange("p (a n) -> p a n", a=2), AX.X, ALU.add).then_inc(lam_sum, 1)
            step.after(nc.vector.tensor_scalar(smA[:, 0:1], smA[:, 0:1], smA[:, 2:3], None, ALU.mult))
            dve.wait_ge(lam_exp, l + 1)
            step.after(nc.vector.tensor_tensor(neglam, elam[:, 1:2], elam[:, 0:1], ALU.subtract))
            step.after(nc.vector.tensor_tensor(neglam, neglam, smA[:, 1:2], ALU.subtract))
            dve_units(dve, step, l * UNITS_A, diff_units, diff_scale)
            dve.wait_ge(o_copied, l * TT + TT)
            step.after(nc.vector.tensor_tensor(Osq, O, O, ALU.mult))
            nc.vector.tensor_reduce(ms, Osq.rearrange("p t (h n) -> p (t h) n", h=4), AX.X, ALU.add).then_inc(ms_ready, 1)
            strict, negstrict = cs[:, CONST["strict"]], cs[:, CONST["negstrict"]]
            for h in range(8):
                u = h % 2
                z = ps[4 + u][:, 0:384]
                dve.wait_ge(z_log, l * 8 + (h + 1))
                if h >= 2:
                    dve.wait_ge(z_w, l * 8 + (h - 1))
                nc.vector.tensor_tensor(sb_z[:, u, :], z, strict, ALU.add)
                step.after(nc.vector.scalar_tensor_tensor(sb_sp[:, u, :], z, 0.0, sb_l[:, u, :], ALU.max, ALU.add))
                nc.vector.tensor_tensor(sb_f[:, u, :], sb_sp[:, u, :], negstrict, ALU.mult).then_inc(z_fail, 1)
                dve.wait_ge(z_sum, l * 8 + (h + 1))
                nc.vector.tensor_tensor(sb_z[:, u, :], ps[6][:, 0:384], sb_z[:, u, :], ALU.add).then_inc(z_exp_in, 1)
            dve.wait_ge(ms_root, l + 1)
            step.after(nc.vector.reciprocal(rs, rs))
            for tt in range(TT):
                o = O[:, tt, :].rearrange("p (h n) -> p h n", h=4)
                r = rs[:, 4 * tt:4 * tt + 4].unsqueeze(2).to_broadcast([P, 4, P])
                nc.vector.tensor_tensor(o, o, r, ALU.mult).then_inc(o_scaled, 1)
            dve_norm(dve, step, l * 2, 1, l, A_LN1)
            for h in range(8):
                dve.wait_ge(key_ev, l * 8 + (h + 1))
                rows = [(tt, 2 * h + s) for tt in range(TT) for s in range(2)]
                carry_wait()
                for tt, r in rows:
                    last = nc.vector.max(top[:, tt, r, 0:8], sc[:, tt, r, :])
                step.after(last)
                carry_wait()
                for n, (tt, r) in enumerate(rows):
                    nc.vector.max_index(topi[:, tt, r, 0:8], top[:, tt, r, 0:8], sc[:, tt, r, :])
                    last = nc.vector.match_replace(sc2[:, n, :], top[:, tt, r, 0:8], sc[:, tt, r, :], NEG * 1e8)
                step.after(last)
                carry_wait()
                for n, (tt, r) in enumerate(rows):
                    last = nc.vector.max(top[:, tt, r, 8:16], sc2[:, n, :])
                step.after(last)
                carry_wait()
                for n, (tt, r) in enumerate(rows):
                    nc.vector.max_index(topi[:, tt, r, 8:16], top[:, tt, r, 8:16], sc2[:, n, :])
                for tt in range(TT):
                    t2 = top[:, tt, 2 * h:2 * h + 2, :]
                    last = nc.vector.tensor_tensor(cand[:, tt, :].rearrange("p (a b) -> p a b", a=16),
                                                   t2[:, 0, :].unsqueeze(2).to_broadcast([P, 16, 16]),
                                                   t2[:, 1, :].unsqueeze(1).to_broadcast([P, 16, 16]), ALU.add)
                step.after(last)
                carry_wait()
                for tt in range(TT):
                    last = nc.vector.max(best[:, tt, h, 0:8], cand[:, tt, :])
                step.after(last)
                carry_wait()
                for tt in range(TT):
                    nc.vector.max_index(pos[:, tt, h, 0:8], best[:, tt, h, 0:8], cand[:, tt, :])
                    last = nc.vector.match_replace(cand2[:, tt, :], best[:, tt, h, 0:8], cand[:, tt, :], NEG * 1e8)
                step.after(last)
                carry_wait()
                for tt in range(TT):
                    last = nc.vector.max(best[:, tt, h, 8:16], cand2[:, tt, :])
                step.after(last)
                carry_wait()
                for tt in range(TT):
                    last = nc.vector.max_index(pos[:, tt, h, 8:16], best[:, tt, h, 8:16], cand2[:, tt, :])
            for tt in range(TT):
                nc.vector.tensor_copy(topf[:, tt, :, :], topi[:, tt, :, :])
                nc.vector.tensor_tensor(gexp[:, tt, :, :], best[:, tt, :, :],
                                        best[:, tt, :, 0:1].to_broadcast([P, 8, 16]), ALU.subtract).then_inc(g_diff, 1)
            dve.wait_ge(g_diff, l * TT + TT)
            for tt in range(TT):
                nc.vector.tensor_scalar(half_u[:, 0, :, :], pos[:, tt, :, :], 4, None, ALU.logical_shift_right)
                step.after(nc.vector.tensor_scalar(half_u[:, 1, :, :], pos[:, tt, :, :], 15, None, ALU.bitwise_and))
                step.after(nc.vector.tensor_copy(half_f, half_u))
                f2 = topf[:, tt, :, :].rearrange("p (h s) n -> p h s n", s=2)
                for s in range(2):
                    for h in range(8):
                        last = nc.vector.tensor_tensor(hot[:, h, :, :],
                                                       half_f[:, s, h, :].unsqueeze(2).to_broadcast([P, 16, 16]),
                                                       iota[:, 0:16].unsqueeze(1).to_broadcast([P, 16, 16]), ALU.is_equal)
                    step.after(last)
                    for h in range(8):
                        last = nc.vector.tensor_tensor(hot[:, h, :, :], hot[:, h, :, :],
                                                       f2[:, h, s, :].unsqueeze(1).to_broadcast([P, 16, 16]), ALU.mult)
                    step.after(last)
                    step.after(nc.vector.tensor_reduce(chosen[:, tt, s, :].rearrange("p (h n) -> p h n", h=8), hot,
                                                       AX.X, ALU.add))
                dve.wait_ge(g_exp, l * TT + (tt + 1))
                step.after(nc.vector.tensor_reduce(gsum, gexp[:, tt, :, :], AX.X, ALU.add))
                step.after(nc.vector.reciprocal(gsum, gsum))
                nc.vector.tensor_tensor(chosen[:, tt, 2, :].rearrange("p (h n) -> p h n", h=8), gexp[:, tt, :, :],
                                        gsum.unsqueeze(2).to_broadcast([P, 8, 16]), ALU.mult).then_inc(chosen_ready, 1)

            dve_split_x(dve, l)
            dve.wait_ge(sel_ev, l * TT + TT)
            for half in range(2):
                base = l * (2 * GROUPS) + half * GROUPS

                def one_hot(i, b, guard):
                    if guard:
                        dve.wait_ge(hot_mm, base + 2 * i + (b - 1))
                    tok = bass.ds(i * 16 + 8 * b, 8)
                    nc.vector.tensor_tensor(hot_a[:, b, :, :],
                                            iota[:, half * HALF:(half + 1) * HALF].unsqueeze(1).to_broadcast([P, 8, HALF]),
                                            selT[:, 0, tok].unsqueeze(2).to_broadcast([P, 8, HALF]),
                                            ALU.is_equal).then_inc(hot_rows, 1)
                    nc.vector.tensor_tensor(hot_b[:, b, 0:BY_DVE, :], iota.unsqueeze(1).to_broadcast([P, BY_DVE, P]),
                                            selT[:, 1, bass.ds(i * 16 + 8 * b, BY_DVE)].unsqueeze(2)
                                            .to_broadcast([P, BY_DVE, P]), ALU.is_equal)
                    dve.wait_ge(hot_rows, base + 2 * i + (b + 1))
                    nc.vector.tensor_tensor(hot_a[:, b, :, :], hot_a[:, b, :, :],
                                            selT[:, 2, tok].unsqueeze(2).to_broadcast([P, 8, HALF]),
                                            ALU.mult).then_inc(hot_ready, 1)

                if half:
                    dve.wait_ge(u_w, l * PAIRS + PAIRS // 2)
                one_hot(0, 0, False)
                one_hot(0, 1, False)
                with dve.Fori(1, GROUPS // 2) as i:
                    one_hot(i, 0, True)
                    one_hot(i, 1, True)
                dve.wait_ge(gate_ev, base + GROUPS)

                def gate(p, i):
                    return gates[:, :, bass.ds(i * 4 + 2 * p, 2)].rearrange("p t b -> p b t")

                dve_pairs(dve, 1, l, A_EXP, PAIRS // 2, l * PAIRS + half * PAIRS // 2, half * PAIRS // 4, gate)
            dve_norm(dve, step, l * 2 + 1, 1, l, A_LN2)
            step.close()

        def pool_block1(pool, l):
            pool.wait_ge(sel_ev, l * TT + TT)
            for half in range(2):
                base = l * (2 * GROUPS) + half * GROUPS

                def columns(i, b, guard):
                    if guard:
                        pool.wait_ge(hotb_ready, base + 2 * i + (b - 1))
                    tok = bass.ds(i * 16 + (8 * b + BY_DVE), 8 - BY_DVE)
                    d = apart[:, b, :, :]
                    nc.gpsimd.tensor_tensor(d, iota.unsqueeze(1).to_broadcast([P, 8 - BY_DVE, P]),
                                            selT[:, 1, tok].unsqueeze(2).to_broadcast([P, 8 - BY_DVE, P]),
                                            ALU.subtract)\
                        .then_inc(apart_ready, 1)
                    pool.wait_ge(apart_ready, base + 2 * i + (b + 1))
                    nc.gpsimd.tensor_tensor(d, d, d, ALU.mult).then_inc(square_ready, 1)

                columns(0, 0, half == 1)
                columns(0, 1, half == 1)
                with pool.Fori(1, GROUPS // 2) as i:
                    columns(i, 0, True)
                    columns(i, 1, True)

        at[0] = 0
        nq = room(4 * SEQ).rearrange("p (b n) -> p b n", b=4)
        kvc = room(2 * SEQ).rearrange("p (b n) -> p b n", b=2)
        ks = room(2 * SEQ).rearrange("p (b n) -> p b n", b=2)
        kw = room(2 * SEQ).rearrange("p (b n) -> p b n", b=2)
        fq = room(2 * SEQ).rearrange("p (b n) -> p b n", b=2)
        fk = room(2 * SEQ).rearrange("p (b n) -> p b n", b=2)
        vsw = room(TT * 256).rearrange("p (t n) -> p t n", t=TT)
        fv = room(TT * 256).rearrange("p (t n) -> p t n", t=TT)
        cqkv = room(TT * 512).rearrange("p (t n) -> p t n", t=TT)
        misc = room(TT * 64).rearrange("p (t n) -> p t n", t=TT)
        assert at[0] <= shared_top - 3 * 1024
        at[0] = shared_top
        T = room(8 * 256).rearrange("p (h k) -> p h k", h=8)
        smB = room(TILE)
        cT = room(4 * SEQ).rearrange("p (b n) -> p b n", b=4)
        mq = room(TT * 384).rearrange("p (t h n) -> p t h n", t=TT, h=4)
        mk = room(TT * 384).rearrange("p (t h n) -> p t h n", t=TT, h=4)
        mv2 = room(TT * 256).rearrange("p (t h n) -> p t h n", t=TT, h=4)
        mqT = room(4 * SEQ).rearrange("p (h n) -> p h n", h=4)
        mkT = room(4 * SEQ).rearrange("p (h n) -> p h n", h=4)
        lfb = room(TT * 512).rearrange("p (t h n) -> p t h n", t=TT, h=4)
        xb = room(32 * 32).rearrange("p (l g n) -> p l g n", l=32, g=2)
        hid = room(64).rearrange("p (s n) -> p s n", s=2)
        kcT = room(32)
        vc = room(2 * HD)
        cS = room(TT * 8 * 16).rearrange("p (t h n) -> p t h n", t=TT, h=8)
        oT = room(8 * SEQ).rearrange("p (b n) -> p b n", b=8)
        merged = room(8 * SEQ).rearrange("p (b n) -> p b n", b=8)
        late = room(3 * 1024)
        PcT = late[:, 0:TT * 1024].rearrange("p (t h q) -> p t h q", t=TT, h=8)
        sig = late[:, 0:3 * 512].rearrange("p (b n) -> p b n", b=3)
        prod = late[:, 3 * 512:6 * 512].rearrange("p (b n) -> p b n", b=3)
        xq = room(2 * SEQ).rearrange("p (b n) -> p b n", b=2)
        xk = room(2 * SEQ).rearrange("p (b n) -> p b n", b=2)
        xv = room(TT * 256).rearrange("p (t n) -> p t n", t=TT)
        xo = room(2 * SEQ).rearrange("p (b n) -> p b n", b=2)
        sq = merged[:, 0:4, :].rearrange("p (t b) n -> p t (b n)", t=TT)
        rt = room(6 * 64).rearrange("p (s h n) -> p s h n", s=6, h=4)
        rk = room(TT * 32).rearrange("p (t n) -> p t n", t=TT)
        gsig = room(TT * 24).rearrange("p (t h b) -> p t h b", t=TT, b=3)
        rms = room(4).rearrange("p (t s) -> p t s", t=TT)
        rmr = room(4).rearrange("p (t s) -> p t s", t=TT)
        fy, fa, fe, fl, flf = (room(8) for _ in range(5))
        negcum = room(8).rearrange("p (t h) -> p t h", t=TT)
        cmax, csum = (room(16).rearrange("p (t h) -> p t h", t=TT) for _ in range(2))
        bd = room(384)

        b_ev, b_rms, b_root, b_scaled, c_mm, c_ev = (
            sem(n) for n in ("b_ev", "b_rms", "b_root", "b_scaled", "c_mm", "c_ev"))
        q_mm, kv_mm, kv_ev, mla_ready, mt_mm, mt_ev = (
            sem(n) for n in ("q_mm", "kv_mm", "kv_ev", "mla_ready", "mt_mm", "mt_ev"))
        xb_ready, hid_act, kc_mm, kc_ev = sem("xb_ready"), sem("hid_act"), sem("kc_mm"), sem("kc_ev")
        f_y, f_log, f_ready, f_mm, f_cum = (sem(n) for n in ("f_y", "f_log", "f_ready", "f_mm", "f_cum"))
        g_sig, cs_mm, cs_max, cs_exp, cs_p, ct_mm, ct_ev = (
            sem(n) for n in ("g_sig", "cs_mm", "cs_max", "cs_exp", "cs_p", "ct_mm", "ct_ev"))
        ob_ev, sig_mm, sig_ready, br_mm, br_used = (sem(n) for n in ("ob_ev", "sig_mm", "sig_ready", "br_mm", "br_used"))
        x_ev, xo_ev = sem("x_ev"), sem("xo_ev")
        t_mm, t_ev, t_out, t_in, t_flip, t_ready = (
            sem(n) for n in ("t_mm", "t_ev", "t_out", "t_in", "t_flip", "t_ready"))

        causal = cs[:, CONST["causal"]]
        cum = cs[:, CONST["cum"]]
        rope = cs[:, CONST["rope"]].rearrange("p (t s n) -> p t s n", t=TT, s=2)
        cmpok = cs[:, CONST["cmpok"]].rearrange("p (t n) -> p t n", t=TT)
        CN = [7, 15]
        smg = smB[:, B_QN:B_QN + 4]
        w_uq = smB[:, B_UQ:B_UKV].rearrange("p (c n) -> p c n", c=3)
        w_ukv = smB[:, B_UKV:B_W2]
        w_2 = smB[:, B_W2:B_PE].rearrange("p (s n) -> p s n", s=2)

        def unit(kind, pair, qt, **more):
            n = P * (qt + 1)
            off = 0 if qt else P
            u = dict(kind=kind, pair=pair, qt=qt, keys=n, scale=1.0, minus=None, gate=None,
                     table=[causal[:, off:256]] * 2, turned=2)
            u.update(more)
            return u

        mix_units = []
        for pair in range(4):
            for qt in range(TT):
                for kind in (1, 2):
                    off = 0 if qt else P
                    mix_units.append(unit(kind, pair, qt, gate=gsig[:, qt, 2 * pair:2 * pair + 2, kind],
                                          table=[T[:, 2 * pair + m, off:256] for m in range(2)]))
        for pair in range(2):
            for qt in range(TT):
                mix_units.append(unit("mla", pair, qt, scale=96 ** -0.5))
        for pair in range(2):
            for qt in range(TT):
                mix_units.append(unit("fox", pair, qt, minus=[negcum[:, qt, 2 * pair + m:2 * pair + m + 1]
                                                              for m in range(2)]))
        mem_units = [unit("mem", pair, qt, keys=SEQ, table=None) for pair in range(2) for qt in range(TT)]

        def b_scores(w, m, out):
            kind, pair, qt = w["kind"], w["pair"], w["qt"]
            q = slice(qt * P, (qt + 1) * P)
            part = slice(64 * m, 64 * m + 64)
            if kind in (1, 2):
                k = ks if kind == 1 else kw
                return nc.tensor.matmul(out, nq[part, pair, q], k[part, pair // 2, 0:w["keys"]], start=True, stop=True)
            if kind == "mla":
                h = 2 * pair + m
                return nc.tensor.matmul(out, mqT[0:96, h, q], mkT[0:96, h, 0:w["keys"]], start=True, stop=True)
            if kind == "mem":
                return nc.tensor.matmul(out, xq[part, pair, q], xk[part, pair, :], start=True, stop=True)
            h = 2 * pair + m
            nc.tensor.matmul(out, fq[part, pair, q], fk[part, pair, 0:w["keys"]], start=True, stop=False)
            last = nc.tensor.matmul(out, lfb[:, 0, h, :], cum[:, 0:w["keys"]], start=False, stop=(qt == 0))
            if qt:
                last = nc.tensor.matmul(out[:, P:SEQ], lfb[:, 1, h, :], cum[:, 0:P], start=False, stop=True)
            return last

        def b_values(w, m, pt):
            kind, pair, qt = w["kind"], w["pair"], w["qt"]
            part = slice(64 * m, 64 * m + 64)
            col = qt * P
            h = 2 * pair + m
            if kind in (1, 2):
                bank, v = pair, (lambda kt: vsw[:, kt, (kind - 1) * P + (pair // 2) * HD:][:, 0:HD])
            elif kind == "mla":
                bank, col, v = pair, col + SEQ, (lambda kt: mv2[:, kt, h, :])
            elif kind == "fox":
                bank, col, v = 2 + pair, col + SEQ, (lambda kt: fv[:, kt, h * HD:(h + 1) * HD])
            else:
                bank, v = pair, (lambda kt: xv[:, kt, h * HD:(h + 1) * HD])
            out = ps[bank][part, col:col + P]
            n = w["keys"] // P
            for kt in range(n):
                last = nc.tensor.matmul(out, v(kt), pt[:, kt, :], start=(kt == 0 and kind != 2),
                                        stop=(kt == n - 1 and kind != 1), skip_group_check=(kind in (1, 2)))
            if kind == 2:
                g = pair // 2
                last = nc.tensor.matmul(out, vc[0:CN[qt], g * HD:(g + 1) * HD], PcT[0:CN[qt], qt, h, :],
                                        start=False, stop=True, skip_group_check=True)
            return last

        def pe_block2(pe, l):
            turns = 4 + 8 * LAYERS + 12 * l
            pe.wait_ge(small_read, LAYERS + l + 1)
            pe.sem_inc(tile_done, 1)
            pe.wait_ge(xt_ready, turns)
            for j in range(12):
                k = B_PROJ + j
                arrived(pe, 2, l, k)
                if j >= 4:
                    pe.wait_ge(b_ev, l * 12 + (j - 3))
                up = up_features(chunks(k), xT, 4 + j % 4) if j < 7 else \
                    up_tokens(chunks(k), xT, 4 + j % 4, 64 if j == 11 else 256)
                up.then_inc(tile_done, 1)
            pe.wait_ge(b_ev, l * 12 + 12)
            pe.wait_ge(xb_ready, l + 1)
            for j in range(2):
                arrived(pe, 2, l, B_CMP + j)
                w = slot(B_CMP + j).rearrange("p (l n) -> p l n", l=16)
                for s in range(2):
                    part = slice(64 * s, 64 * s + 64)
                    for i in range(16):
                        last = nc.tensor.matmul(ps[4 + s][:, 0:2 * N_CMP], w[part, i, :],
                                                xb[part, 16 * j + i, :, 0:N_CMP],
                                                start=(i == 0 and j == 0), stop=(i == 15 and j == 1))
                last.then_inc(tile_done, 1)
            pe.wait_ge(b_scaled, l + 1)
            for tt in range(TT):
                for c in range(4):
                    last = nc.tensor.transpose(ps[tt][:, c * P:(c + 1) * P], cqkv[:, tt, c * P:(c + 1) * P], ident)
                last.then_inc(c_mm, 1)
            pe.wait_ge(hid_act, l * 2 + 2)
            for half in range(2):
                nc.tensor.matmul(ps[6][64 * half:64 * half + 64, 0:2 * N_CMP], w_2[:, 0, :], hid[:, 0, 0:2 * N_CMP],
                                 start=True, stop=True)
            for g in range(2):
                last = nc.tensor.matmul(ps[7][0:N_CMP, g * HD:(g + 1) * HD], hid[:, 1, g * N_CMP:(g + 1) * N_CMP],
                                        w_2[:, 1, :], start=True, stop=True)
            last.then_inc(kc_mm, 1)
            pe.wait_ge(f_ready, l + 1)
            lf = flf.rearrange("p (t h) -> p t h", t=TT)
            nc.tensor.matmul(ps[3][:, 0:4], cum[:, 0:P], lf[:, 0, :], start=True, stop=True)
            nc.tensor.matmul(ps[3][:, 4:8], cum[:, P:SEQ], lf[:, 0, :], start=True, stop=False)
            nc.tensor.matmul(ps[3][:, 4:8], cum[:, 0:P], lf[:, 1, :], start=False, stop=True).then_inc(f_mm, 1)
            pe.wait_ge(f_cum, l + 1)
            for tt in range(TT):
                pe.wait_ge(c_ev, l * 2 + (tt + 1))
                t = slice(tt * P, (tt + 1) * P)
                for c in range(3):
                    last = nc.tensor.matmul(ps[2 + tt][:, 0:384], cT[:, c, t], w_uq[:, c, :], start=(c == 0),
                                            stop=(c == 2))
                last.then_inc(q_mm, 1)
                nc.tensor.matmul(ps[4 + tt][:, :], cT[:, 3, t], w_ukv, start=True, stop=True).then_inc(kv_mm, 1)
            pe.wait_ge(kc_ev, l * 2 + 2)
            for tt in range(TT):
                for h in range(8):
                    part = slice(64 * (h % 2), 64 * (h % 2) + 64)
                    g = h // 4
                    col = 64 * tt + h // 2 * 16
                    last = nc.tensor.matmul(ps[6 + h % 2][:, col:col + N_CMP], nq[part, h // 2, tt * P:(tt + 1) * P],
                                            kcT[part, g * N_CMP:(g + 1) * N_CMP], start=True, stop=True)
                last.then_inc(cs_mm, 1)
            for tt in range(TT):
                pe.wait_ge(mla_ready, l * 2 + (tt + 1))
                for j, src in enumerate((mq, mk)):
                    for h in range(4):
                        last = nc.tensor.transpose(ps[2 * j + tt][0:96, h * P:(h + 1) * P], src[:, tt, h, :], ident)
                    last.then_inc(mt_mm, 1)
            for tt in range(TT):
                pe.wait_ge(cs_p, l * 2 + (tt + 1))
                for g in range(2):
                    for h in range(4):
                        last = nc.tensor.transpose(ps[4 + 2 * tt + g][0:CN[tt], h * P:(h + 1) * P],
                                                   cS[:, tt, 4 * g + h, 0:CN[tt]], ident)
                    last.then_inc(ct_mm, 1)
            pe.wait_ge(mt_ev, l * 4 + 4)
            pe.wait_ge(ct_ev, l * 4 + 4)
            pe_units(pe, done_b + l * UNITS_B, mix_units, b_scores, b_values)
            pe.wait_ge(ob_ev, l * 4 + 4)
            for i in range(4):
                for b in range(3):
                    k = B_GATE + 4 * i + b
                    arrived(pe, 2, l, k)
                    if i:
                        pe.wait_ge(sig_ready, l * 12 + (3 * (i - 1) + b + 1))
                    up_features(chunks(k), xT, 4 + b).then_inc(tile_done, 1)
                k = B_GATE + 4 * i + 3
                arrived(pe, 2, l, k)
                if i:
                    pe.wait_ge(br_used, l * 4 + i)
                w = chunks(k)
                for b, cc in enumerate(((0, 2, 4, 6), (1, 3), (5, 7))):
                    for fb in range(2):
                        for n, c in enumerate(cc):
                            last = nc.tensor.matmul(ps[b][:, fb * SEQ:(fb + 1) * SEQ], w[:, c, fb * P:(fb + 1) * P],
                                                    oT[:, c, :], start=(n == 0), stop=(n == len(cc) - 1))
                last.then_inc(tile_done, 1)
            pe.wait_ge(br_used, l * 4 + 4)
            for j in range(4):
                arrived(pe, 2, l, B_MIX + j)
                down(slot(B_MIX + j), lambda i, tt: merged[:, 2 * j + i, tt * P:(tt + 1) * P], j == 0,
                     j == 3).then_inc(tile_done, 1)
            norm = 2 * LAYERS + 3 * l
            pe_turn_x(pe, norm)
            pe.wait_ge(xt_ready, turns + 4)
            arrived(pe, 2, l, B_XQ)
            up_features(chunks(B_XQ), xT, 4).then_inc(tile_done, 1)
            arrived(pe, 2, l, B_MEM)
            arrived(pe, 2, l, B_XK)
            up_features(chunks(B_XK), chunks(B_MEM), 5)
            arrived(pe, 2, l, B_XV)
            up_tokens(chunks(B_XV), chunks(B_MEM), 6).then_inc(tile_done, 3)
            pe.wait_ge(x_ev, l * 3 + 3)
            pe_units(pe, done_b + l * UNITS_B + len(mix_units), mem_units, b_scores, b_values)
            pe.wait_ge(xo_ev, l * 2 + 2)
            arrived(pe, 2, l, B_XO)
            down(slot(B_XO), lambda i, tt: xo[:, i, tt * P:(tt + 1) * P], True, True).then_inc(tile_done, 1)
            pe_turn_x(pe, norm + 1)
            pe.wait_ge(xt_ready, turns + 8)
            pe.wait_ge(xl_ready, LAYERS + l + 1)
            pe_pairs(pe, 2, l, B_MLP, MLP_PAIRS, LAYERS * PAIRS + l * MLP_PAIRS, 0, True, True)
            for k in range(B_LN3 + 1, B_TILES):
                arrived(pe, 2, l, k)
            pe_turn_x(pe, norm + 2, B_TILES - B_LN3)

        done_b = LAYERS * UNITS_A

        def act_block2(act, l):
            dests = [nq[:, 0:2, :], nq[:, 2:4, :], kvc, ks, kw, fq, fk, vsw, fv, cqkv[:, :, 0:256], cqkv[:, :, 256:512],
                     misc]
            for j in range(12):
                finished(act, 2, l, B_PROJ + j)
                n = 64 if j == 11 else 256
                src = ps[4 + j % 4][:, :].rearrange("p (a n) -> p a n", a=2)[:, :, 0:n]
                nc.scalar.activation(dests[j], src, ACT.Copy, scale=HD ** -0.5 if j in (0, 1, 5) else 1.0)\
                    .then_inc(b_ev, 1)
            act.wait_ge(b_ev, l * 12 + 12)
            nc.scalar.activation(gsig.rearrange("p t h b -> p t (h b)"), misc[:, :, 32:56], ACT.Sigmoid)\
                .then_inc(g_sig, 1)
            act.wait_ge(b_rms, l + 1)
            nc.scalar.activation(rmr[:, :, 0], rms[:, :, 0], ACT.Sqrt, scale=1.0 / 384, bias=cs[:, CONST["eps"]][:, 1:2])
            nc.scalar.activation(rmr[:, :, 1], rms[:, :, 1], ACT.Sqrt, scale=1.0 / P, bias=cs[:, CONST["eps"]][:, 1:2])\
                .then_inc(b_root, 1)
            act.wait_ge(f_y, l + 1)
            nc.scalar.activation(fa, fy, ACT.Abs).then_inc(f_log, 1)
            act.wait_ge(f_log, l * 3 + 1)
            nc.scalar.activation(fe, fa, ACT.Exp, scale=-1.0).then_inc(f_log, 1)
            act.wait_ge(f_log, l * 3 + 2)
            nc.scalar.activation(fl, fe, ACT.Ln, bias=1.0).then_inc(f_log, 1)
            finished(act, 2, l, B_CMP + 1)
            for s in range(2):
                nc.scalar.activation(hid[:, s, 0:2 * N_CMP], ps[4 + s][:, 0:2 * N_CMP], ACT.Gelu_apprx_tanh)\
                    .then_inc(hid_act, 1)
            act.wait_ge(kc_mm, l + 1)
            nc.scalar.activation(kcT[:, 0:2 * N_CMP], ps[6][:, 0:2 * N_CMP], ACT.Copy).then_inc(kc_ev, 1)
            nc.scalar.activation(vc[0:N_CMP, :], ps[7][0:N_CMP, 0:P], ACT.Copy).then_inc(kc_ev, 1)
            for tt in range(TT):
                act.wait_ge(kv_mm, l * 2 + (tt + 1))
                kv = ps[4 + tt][:, :].rearrange("p (h n) -> p h n", h=4)
                nc.scalar.activation(mk[:, tt, :, 0:HD], kv[:, :, 0:HD], ACT.Copy)
                nc.scalar.activation(mv2[:, tt, :, :], kv[:, :, HD:2 * HD], ACT.Copy).then_inc(kv_ev, 1)
            for tt in range(TT):
                act.wait_ge(cs_max, l * 2 + (tt + 1))
                s = cS[:, tt, :, 0:CN[tt]]
                nc.scalar.activation(s, s, ACT.Exp).then_inc(cs_exp, 1)
            for tt in range(TT):
                for j, dst in enumerate((mqT, mkT)):
                    act.wait_ge(mt_mm, l * 4 + (2 * tt + j + 1))
                    nc.scalar.activation(dst[0:96, :, tt * P:(tt + 1) * P],
                                         ps[2 * j + tt][0:96, :].rearrange("p (h q) -> p h q", h=4), ACT.Copy)\
                        .then_inc(mt_ev, 1)
            for tt in range(TT):
                for g in range(2):
                    act.wait_ge(ct_mm, l * 4 + (2 * tt + g + 1))
                    nc.scalar.activation(PcT[0:CN[tt], tt, 4 * g:4 * g + 4, :],
                                         ps[4 + 2 * tt + g][0:CN[tt], :].rearrange("p (h q) -> p h q", h=4),
                                         ACT.Copy).then_inc(ct_ev, 1)
            act_units(act, done_b + l * UNITS_B, mix_units)
            act.wait_ge(pv_mm, done_b + l * UNITS_B + len(mix_units))
            for b in range(4):
                nc.scalar.activation(oT[:, 2 * b:2 * b + 2, :], ps[b][:, :].rearrange("p (a n) -> p a n", a=2),
                                     ACT.Copy).then_inc(ob_ev, 1)
            for i in range(4):
                for b in range(3):
                    finished(act, 2, l, B_GATE + 4 * i + b)
                    if i:
                        act.wait_ge(br_used, l * 4 + i)
                    nc.scalar.activation(sig[:, b, :], ps[4 + b][:, :], ACT.Sigmoid).then_inc(sig_ready, 1)
            norm = 2 * LAYERS + 3 * l
            act_norm(act, norm)
            finished(act, 2, l, B_XQ)
            nc.scalar.activation(xq, ps[4][:, :].rearrange("p (a n) -> p a n", a=2), ACT.Copy,
                                 scale=HD ** -0.5).then_inc(x_ev, 1)
            finished(act, 2, l, B_XV)
            nc.scalar.activation(xk, ps[5][:, :].rearrange("p (a n) -> p a n", a=2), ACT.Copy).then_inc(x_ev, 1)
            nc.scalar.activation(xv, ps[6][:, :].rearrange("p (a n) -> p a n", a=2), ACT.Copy).then_inc(x_ev, 1)
            act_units(act, done_b + l * UNITS_B + len(mix_units), mem_units)
            act.wait_ge(pv_mm, done_b + (l + 1) * UNITS_B)
            for b in range(2):
                nc.scalar.activation(xo[:, b, :], ps[b][:, 0:SEQ], ACT.Copy).then_inc(xo_ev, 1)
            act_norm(act, norm + 1)
            act.wait_ge(xt_ready, 12 + 8 * LAYERS + 12 * l)
            act_split_x(act, LAYERS + l)
            act_pairs(act, 2, l, B_MLP, MLP_PAIRS, LAYERS * PAIRS + l * MLP_PAIRS, 0, ACT.Relu)
            act_norm(act, norm + 2)

        def dve_block2(dve, l):
            step = Steps(dve, dve_step, LAYERS * DVE_A, DVE_B, l)
            arrived(dve, 2, l, B_SMALL)
            step.after(nc.vector.tensor_copy(smB, slot(B_SMALL)))
            dve.sem_inc(small_read, 1)
            dve.wait_ge(b_ev, l * 12 + 3)
            for g in range(2):
                for part in range(2):
                    src = kvc[:, g, 16 * part:16 * part + 16 * N_CMP].rearrange("p (n l) -> p l n", l=16)
                    pe_ = smB[:, B_PE + 16 * part:B_PE + 16 * part + 16].unsqueeze(2).to_broadcast([P, 16, N_CMP])
                    last = nc.vector.tensor_tensor(xb[:, 16 * part:16 * part + 16, g, 0:N_CMP], src, pe_, ALU.add)
            last.then_inc(xb_ready, 1)
            dve.wait_ge(b_ev, l * 12 + 12)
            step.after(nc.vector.tensor_tensor(sq, cqkv, cqkv, ALU.mult))
            nc.vector.tensor_reduce(rms[:, :, 0], sq[:, :, 0:384], AX.X, ALU.add)
            nc.vector.tensor_reduce(rms[:, :, 1], sq[:, :, 384:512], AX.X, ALU.add).then_inc(b_rms, 1)
            nc.vector.tensor_tensor(fy.rearrange("p (t h) -> p t h", t=TT), misc[:, :, 56:60],
                                    smB[:, B_BF:B_BF + 4].unsqueeze(1).to_broadcast([P, TT, 4]), ALU.add)\
                .then_inc(f_y, 1)
            dve.wait_ge(b_root, l + 1)
            step.after(nc.vector.reciprocal(rmr, rmr))
            for tt in range(TT):
                nc.vector.tensor_scalar(cqkv[:, tt, 0:384], cqkv[:, tt, 0:384], rmr[:, tt, 0:1], None, ALU.mult)
                last = nc.vector.tensor_scalar(cqkv[:, tt, 384:512], cqkv[:, tt, 384:512], rmr[:, tt, 1:2], None,
                                               ALU.mult)
            last.then_inc(b_scaled, 1)
            dve.wait_ge(f_log, l * 3 + 3)
            step.after(nc.vector.scalar_tensor_tensor(flf, fy, 0.0, fl, ALU.min, ALU.subtract))
            for tt in range(TT):
                last = nc.vector.tensor_copy(lfb[:, tt, :, :],
                                             flf[:, 4 * tt:4 * tt + 4].unsqueeze(2).to_broadcast([P, 4, P]))
            last.then_inc(f_ready, 1)
            for tt in range(TT):
                dve.wait_ge(c_mm, l * 2 + (tt + 1))
                nc.vector.tensor_tensor(cT[:, :, tt * P:(tt + 1) * P], ps[tt][:, :].rearrange("p (c q) -> p c q", c=4),
                                        smg.unsqueeze(2).to_broadcast([P, 4, P]), ALU.mult).then_inc(c_ev, 1)
            dve.wait_ge(f_mm, l + 1)
            nc.vector.tensor_copy(negcum.rearrange("p t h -> p (t h)"), ps[3][:, 0:8]).then_inc(f_cum, 1)
            for tt in range(TT):
                q = mq[:, tt, :, :]
                dve.wait_ge(q_mm, l * 2 + (tt + 1))
                raw = ps[2 + tt][:, 0:384].rearrange("p (h n) -> p h n", h=4)
                nc.vector.tensor_copy(q[:, :, 0:HD], raw[:, :, 0:HD])
                cos = rope[:, tt, 0, :].unsqueeze(1).to_broadcast([P, 4, 16])
                sin = rope[:, tt, 1, :].unsqueeze(1).to_broadcast([P, 4, 16])
                x1, x2 = raw[:, :, HD:HD + 16], raw[:, :, HD + 16:HD + 32]
                nc.vector.tensor_tensor(rt[:, 0, :, :], x1, cos, ALU.mult)
                nc.vector.tensor_tensor(rt[:, 1, :, :], x2, sin, ALU.mult)
                nc.vector.tensor_tensor(rt[:, 2, :, :], x1, sin, ALU.mult)
                nc.vector.tensor_tensor(rt[:, 3, :, :], x2, cos, ALU.mult)
                y1, y2 = misc[:, tt, 0:16], misc[:, tt, 16:32]
                c1, s1 = rope[:, tt, 0, :], rope[:, tt, 1, :]
                nc.vector.tensor_tensor(rt[:, 4, 0, :], y1, c1, ALU.mult)
                nc.vector.tensor_tensor(rt[:, 4, 1, :], y2, s1, ALU.mult)
                nc.vector.tensor_tensor(rt[:, 4, 2, :], y1, s1, ALU.mult)
                step.after(nc.vector.tensor_tensor(rt[:, 4, 3, :], y2, c1, ALU.mult))
                nc.vector.tensor_tensor(q[:, :, HD:HD + 16], rt[:, 0, :, :], rt[:, 1, :, :], ALU.subtract)
                nc.vector.tensor_tensor(q[:, :, HD + 16:HD + 32], rt[:, 2, :, :], rt[:, 3, :, :], ALU.add)
                nc.vector.tensor_tensor(rk[:, tt, 0:16], rt[:, 4, 0, :], rt[:, 4, 1, :], ALU.subtract)
                step.after(nc.vector.tensor_tensor(rk[:, tt, 16:32], rt[:, 4, 2, :], rt[:, 4, 3, :], ALU.add))
                dve.wait_ge(kv_ev, l * 2 + (tt + 1))
                nc.vector.tensor_copy(mk[:, tt, :, HD:96], rk[:, tt, :].unsqueeze(1).to_broadcast([P, 4, 32]))\
                    .then_inc(mla_ready, 1)
            for tt in range(TT):
                n = CN[tt]
                first = 31 if tt else 159
                s = cS[:, tt, :, 0:n]
                dve.wait_ge(cs_mm, l * 2 + 2)
                for odd in range(2):
                    raw = ps[6 + odd][:, 64 * tt:64 * tt + 64].rearrange("p (h n) -> p h n", h=4)
                    last = nc.vector.tensor_tensor(s[:, odd:8:2, :], raw[:, :, 0:n],
                                                   T[:, odd:8:2, first:first + 16 * (n - 1) + 1:16], ALU.add)
                step.after(last)
                step.after(nc.vector.tensor_reduce(cmax[:, tt, :], s, AX.X, ALU.max))
                nc.vector.tensor_tensor(s, s, cmax[:, tt, :].unsqueeze(2).to_broadcast([P, 8, n]), ALU.subtract)\
                    .then_inc(cs_max, 1)
            dve.wait_ge(g_sig, l + 1)
            for tt in range(TT):
                n = CN[tt]
                s = cS[:, tt, :, 0:n]
                dve.wait_ge(cs_exp, l * 2 + (tt + 1))
                step.after(nc.vector.tensor_reduce(csum[:, tt, :], s, AX.X, ALU.add))
                step.after(nc.vector.reciprocal(csum[:, tt, :], csum[:, tt, :]))
                step.after(nc.vector.tensor_tensor(csum[:, tt, :], csum[:, tt, :], gsig[:, tt, :, 0], ALU.mult))
                step.after(nc.vector.tensor_tensor(s, s, csum[:, tt, :].unsqueeze(2).to_broadcast([P, 8, n]), ALU.mult))
                nc.vector.tensor_tensor(s, s, cmpok[:, tt, 0:n].unsqueeze(1).to_broadcast([P, 8, n]), ALU.mult)\
                    .then_inc(cs_p, 1)
            dve_units(dve, step, done_b + l * UNITS_B, mix_units, plain_scale)
            for i in range(4):
                finished(dve, 2, l, B_GATE + 4 * i + 3)
                dve.wait_ge(sig_ready, l * 12 + 3 * (i + 1))
                for b in range(3):
                    last = nc.vector.tensor_tensor(prod[:, b, :], ps[b][:, :], sig[:, b, :], ALU.mult)
                step.after(last)
                step.after(nc.vector.tensor_tensor(prod[:, 0, :], prod[:, 0, :], prod[:, 1, :], ALU.add))
                nc.vector.tensor_tensor(merged[:, 2 * i:2 * i + 2, :].rearrange("p a n -> p (a n)"), prod[:, 0, :],
                                        prod[:, 2, :], ALU.add).then_inc(br_used, 1)
            norm = 2 * LAYERS + 3 * l
            dve_norm(dve, step, norm, 2, l, B_LN1)
            dve_units(dve, step, done_b + l * UNITS_B + len(mix_units), mem_units, plain_scale)
            dve_norm(dve, step, norm + 1, 2, l, B_LN2)

            dve_split_x(dve, LAYERS + l)
            dve_pairs(dve, 2, l, B_MLP, MLP_PAIRS, LAYERS * PAIRS + l * MLP_PAIRS, 0,
                      lambda p, i: act_sb[p % 2].rearrange("p (b t) -> p b t", b=2))
            dve_norm(dve, step, norm + 2, 2, l, B_LN3)
            step.close()

        all_norms = 2 * LAYERS + 3 * LAYERS
        block = ctx.enter_context(nc.Block())

        @block.sync
        def _(sp):
            sp.dma_start(x[:, :, :], x_in.rearrange("(t p) n -> p t n", p=P)).then_inc(loaded, 16)
            sp.dma_start(cs[:, :], consts[:, :]).then_inc(loaded, 16)
            sp.dma_start(tab[:, :], table[:, :]).then_inc(loaded, 16)
            for s in range(SLOTS):
                sp.dma_start(slot(s), stream[s, :, :]).then_inc(slot_full[s], 16)
            with sp.Fori(1, ALL_TILES // SLOTS) as g:
                for s in range(SLOTS):
                    sp.wait_ge(tile_done, 4 * g + (s - 3))
                    sp.dma_start(slot(s), stream[bass.ds(4 * g + s, 1), :, :].rearrange("o p n -> p (o n)"))\
                        .then_inc(slot_full[s], 16)
            sp.wait_ge(ln_x, all_norms * TT)
            sp.dma_start(out.rearrange("(t p) n -> p t n", p=P), x[:, :, :]).then_inc(stored, 16)
            sp.wait_ge(stored, 16)

        @block.gpsimd
        def _(pool):
            with pool.Fori(0, LAYERS) as l:
                pool_block1(pool, l)
            pool.wait_ge(t_ev, 1)
            pool.dma_start(scratch[:, :], bd[0:8, :]).then_inc(t_out, 16)
            pool.wait_ge(t_out, 16)
            band = bass.AP(tensor=scratch.tensor, offset=0, ap=[[1, P], [384, 8], [1, 256]])
            pool.dma_start(merged, band).then_inc(t_in, 16)

        @block.scalar
        def _(act):
            act_turn_x(act, 0)
            with act.Fori(0, LAYERS) as l:
                act_block1(act, l)
            act.wait_ge(t_mm, 1)
            nc.scalar.activation(bd[0:8, :], ps[0][0:8, 0:384], ACT.Copy).then_inc(t_ev, 1)
            with act.Fori(0, LAYERS) as l:
                act_block2(act, l)

        @block.vector
        def _(dve):
            dve.wait_ge(loaded, 48)
            with dve.Fori(0, LAYERS) as l:
                dve_block1(dve, l)
            dve.wait_ge(t_flip, 1)
            for b in range(4):
                last = nc.vector.tensor_tensor(T[:, 2 * b:2 * b + 2, :], ps[b][:, :].rearrange("p (h k) -> p h k", h=2),
                                               causal.unsqueeze(1).to_broadcast([P, 2, 256]), ALU.add)
            last.then_inc(t_ready, 1)
            dve.wait_ge(t_ready, 1)
            with dve.Fori(0, LAYERS) as l:
                dve_block2(dve, l)

        @block.tensor
        def _(pe):
            pe.wait_ge(loaded, 48)
            pe_turn_x(pe)
            with pe.Fori(0, LAYERS) as l:
                pe_block1(pe, l)
            nc.tensor.matmul(ps[0][0:8, 0:384], tab[:, :], cs[0:32, CONST["bucket"]], start=True,
                             stop=True).then_inc(t_mm, 1)
            pe.wait_ge(t_in, 16)
            for b in range(4):
                last = nc.tensor.matmul(ps[b][:, :], cs[:, CONST["flip"]],
                                        merged[:, 2 * b:2 * b + 2, :].rearrange("p a n -> p (a n)"), start=True,
                                        stop=True)
            last.then_inc(t_flip, 1)
            with pe.Fori(0, LAYERS) as l:
                pe_block2(pe, l)


def constants():
    c = np.zeros((P, CONST_COLS), np.float32)
    p = np.arange(P)[:, None]
    j = np.arange(256)[None, :]
    c[:, CONST["ident"]] = np.eye(P)
    c[:, CONST["flip"]] = np.eye(P)[::-1]
    c[:, CONST["tri"]] = p >= j[:, :P]
    c[:, CONST["ones"]] = 1.0
    c[:, CONST["iota"]] = j[:, :P]
    dist = P + p - j
    causal = np.where(dist >= 0, 0.0, NEG)
    c[:, CONST["causal"]] = causal
    for h in range(4):
        slope = np.float32(2.0 ** (-8.0 * (h + 1) / 4))
        c[:, CONST["alibi"].start + 256 * h:CONST["alibi"].start + 256 * (h + 1)] = \
            np.where(dist >= 0, -slope * dist.astype(np.float32), NEG)
    strict = p < j
    strict = np.concatenate([strict, strict[:, :P]], 1)
    c[:, CONST["strict"]] = np.where(strict, 0.0, NEG)
    c[:, CONST["negstrict"]] = -1.0 * strict
    c[:, CONST["cum"]] = -1.0 * (p <= j)
    inv = (10000.0 ** (-np.arange(16, dtype=np.float32) / 16)).astype(np.float32)
    rope = np.zeros((P, TT, 2, 16), np.float32)
    ok = np.zeros((P, TT, N_CMP), np.float32)
    for tt in range(TT):
        ang = (tt * P + p).astype(np.float32) * inv[None, :]
        rope[:, tt, 0], rope[:, tt, 1] = np.cos(ang), np.sin(ang)
        ok[:, tt] = tt * P + p >= 16 * np.arange(N_CMP)[None, :] + 31
    c[:, CONST["rope"]] = rope.reshape(P, -1)
    c[:, CONST["cmpok"]] = ok.reshape(P, -1)
    n = np.maximum(255 - np.arange(384), 0)
    f = np.float32
    large = 16 + (np.log(np.maximum(n, 1).astype(f) / f(16)) / f(math.log(8.0)) * f(16)).astype(np.int32)
    bucket = np.where(n < 16, n, np.minimum(large, 31))
    c[:32, CONST["bucket"]] = np.arange(32)[:, None] == bucket[None, :]
    c[:, CONST["eps"]] = [[1e-5, 1e-6, 0.0]]
    return c


def up_tiles(w):
    n = w.shape[1] // 256
    return w.reshape(KC, P, n, 256).transpose(2, 1, 0, 3).reshape(n, P, TILE)


def down_tiles(w):
    n = w.shape[0] // 256
    return w.reshape(n, 2, P, D).transpose(0, 2, 1, 3).reshape(n, P, TILE)


def paired(out, up, dn):
    n = len(up)
    out[0] = up[0]
    out[1:2 * n - 1:2] = up[1:]
    out[2:2 * n - 1:2] = dn[:-1]
    out[2 * n - 1] = dn[-1]


def norm_tile(g, b):
    return np.broadcast_to(np.concatenate([g, b])[None, :], (P, TILE))


def lay_out(v):
    s = np.zeros((ALL_TILES, P, TILE), np.float32)
    for l in range(LAYERS):
        t = s[l * A_TILES:(l + 1) * A_TILES]
        small = t[A_SMALL]
        small[:, 0:256] = np.concatenate([v[n][l] for n in ("lam_q1", "lam_k1", "lam_q2", "lam_k2")])[None, :]
        small[:, A_SUBG] = v["subln_g"][l]
        init = 0.8 - 0.6 * math.exp(-0.3 * l)
        small[:, A_LINI], small[:, A_LOUT] = init, 1.0 - init
        w = v["w_in"][l]
        dq, dk, dv, sq, sk, sv = (w[:, 512 * i:512 * (i + 1)] for i in range(6))
        t[A_PROJ:A_WO] = up_tiles(np.concatenate([dq, dk, sq, sk, dv, sv], 1))
        t[A_WO:A_LN1] = down_tiles(v["w_o"][l])
        t[A_LN1] = norm_tile(v["ln1_g"][l], v["ln1_b"][l])
        t[A_WQ:A_EXP] = up_tiles(v["w_query"][l])
        t[A_KEYS] = v["sub_keys"][l].reshape(16, P, P).transpose(2, 0, 1).reshape(P, TILE)
        u = v["expert_u"][l].reshape(PAIRS, 256, KC, P).transpose(0, 3, 2, 1).reshape(PAIRS, P, TILE)
        dn = down_tiles(v["expert_v"][l])
        h = PAIRS // 2
        paired(t[A_EXP:A_EXP + PAIRS], u[:h], dn[:h])
        paired(t[A_EXP + PAIRS:A_LN2], u[h:], dn[h:])
        t[A_LN2] = norm_tile(v["ln2_g"][l], v["ln2_b"][l])

        t = s[LAYERS * A_TILES + l * B_TILES:][:B_TILES]
        small = t[B_SMALL]
        small[:, B_UQ:B_UKV] = v["mla_w_uq_2"][l].reshape(3, P, 384).transpose(1, 0, 2).reshape(P, 1152)
        small[:, B_UKV:B_W2] = v["mla_w_ukv_2"][l]
        small[:, B_W2:B_PE] = v["cmp_w2_2"][l].transpose(1, 0, 2).reshape(P, 128)
        small[:, B_PE:B_PE + 32] = v["cmp_pe_2"][l].transpose(0, 2, 1).reshape(P, 32)
        small[:, B_QN:B_KVN] = v["mla_q_norm_2"][l].reshape(3, P).T
        small[:, B_KVN] = v["mla_kv_norm_2"][l]
        small[:, B_BF:B_BF + 4] = v["fox_b_f_2"][l][None, :]
        w = v["w_in_2"][l]
        sizes = (512, 128, 128, 128, 128, 128, 128, 24, 384, 128, 32, 256, 256, 256, 4)
        at = np.cumsum((0,) + sizes)
        nq, kc, vc, ks, vs, kw, vw, ng, cq, ckv, kr, fq, fk, fv, ff = (w[:, a:a + n] for a, n in zip(at, sizes))
        g0, g1 = slice(0, 64), slice(64, 128)
        t[B_PROJ:B_CMP] = up_tiles(np.concatenate(
            [nq, kc[:, g0], vc[:, g0], kc[:, g1], vc[:, g1], ks[:, g0], ks[:, g0], ks[:, g1], ks[:, g1],
             kw[:, g0], kw[:, g0], kw[:, g1], kw[:, g1], fq, fk, vs, vw, fv, cq, ckv, kr, ng, ff,
             np.zeros((D, 196), np.float32)], 1))
        w1 = v["cmp_w1_2"][l].reshape(2, 2, 16, HD, P)
        t[B_CMP:B_GATE] = w1.transpose(1, 0, 3, 2, 4).reshape(2, P, TILE)
        gate = up_tiles(v["w_gate_2"][l]).reshape(3, 4, P, TILE)
        a, b, c = v["w_br_nsa_2"][l], v["w_br_mla_2"][l], v["w_br_fox_2"][l]
        rows = [x[P * i:P * (i + 1)] for x, i in ((a, 0), (b, 0), (a, 1), (b, 1), (a, 2), (c, 0), (a, 3), (c, 1))]
        branch = up_tiles(np.concatenate(rows, 0))
        for i in range(4):
            t[B_GATE + 4 * i:B_GATE + 4 * i + 3] = gate[:, i]
            t[B_GATE + 4 * i + 3] = branch[i]
        t[B_MIX:B_LN1] = down_tiles(v["w_mix_out_2"][l])
        for n, k in enumerate((B_LN1, B_LN2, B_LN3)):
            t[k] = norm_tile(v["ln_g_2"][l, n], v["ln_b_2"][l, n])
        t[B_XQ] = up_tiles(v["xa_w_q_2"][l])[0]
        t[B_MEM] = up_tiles(np.ascontiguousarray(v["mem_2"][0].T))[0]
        t[B_XK:B_XO] = up_tiles(v["xa_w_kv_2"][l])
        t[B_XO] = down_tiles(v["xa_w_o_2"][l])[0]
        paired(t[B_MLP:B_LN3], up_tiles(v["mlp_w_up_2"][l]), down_tiles(v["mlp_w_down_2"][l]))
    return s


def kernel(**inputs):
    import concourse.bacc as bacc
    from concourse.bass_utils import run_bass_kernel_spmd

    v = {n: np.asarray(a) for n, a in inputs.items()}
    arrays = {
        "stream": lay_out(v),
        "x_in": np.ascontiguousarray(v["x"][0]),
        "consts": constants(),
        "table": np.ascontiguousarray(v["t5_table_2"]),
    }
    nc = bacc.Bacc("TRN2", target_bir_lowering=False, num_devices=1)
    aps = [nc.dram_tensor(n, a.shape, F32, kind="ExternalInput").ap() for n, a in arrays.items()]
    scratch = nc.dram_tensor("scratch", (8, 384), F32, kind="Internal").ap()
    out = nc.dram_tensor("out", (SEQ, D), F32, kind="ExternalOutput").ap()
    program(nc, *aps, scratch, out)
    r = run_bass_kernel_spmd(nc, [arrays], core_ids=[0])
    return np.asarray(r.results[0]["out"]).reshape(1, SEQ, D)
```
